# Optimizing a Trainium2 kernel written in Bass

```python
import math
import jax, jax.numpy as jnp
from jax import lax
import numpy as np

D_MODEL = 1024
BATCH = 1
SEQ = 512
DEPTH = 1

MEM_LEN = 256
EPS = 1e-6
S5_WIDTH = 512
S5_GROUP = 16
S5_GROUPS = S5_WIDTH // S5_GROUP
S5_STATE = 64
SGU_WIDTH = 1024
SGU_HEADS = 8
SGU_HEAD_DIM = SGU_WIDTH // SGU_HEADS
CHUNK = 128
XATTN_HEADS = 4
XATTN_HEAD_DIM = D_MODEL // XATTN_HEADS
D_FF = ((8 * D_MODEL // 3 + 255) // 256) * 256
OFF_U = S5_WIDTH
OFF_V = OFF_U + SGU_WIDTH
OFF_GA = OFF_V + SGU_WIDTH
OFF_GB = OFF_GA + D_MODEL
IN_COLS = OFF_GB + D_MODEL


def rms_norm(x, g):
    xf = x.astype(jnp.float32)
    y = xf * lax.rsqrt(jnp.mean(xf * xf, axis=-1, keepdims=True) + EPS)
    return (y * g.astype(jnp.float32)).astype(x.dtype)

def layer_norm(x, g, b):
    xf = x.astype(jnp.float32)
    mu = jnp.mean(xf, axis=-1, keepdims=True)
    xc = xf - mu
    y = xc * lax.rsqrt(jnp.mean(xc * xc, axis=-1, keepdims=True) + EPS)
    return (y * g.astype(jnp.float32) + b.astype(jnp.float32)).astype(x.dtype)

def _linear_recurrence(e1, e2):
    a1, b1 = e1
    a2, b2 = e2
    return a1 * a2, a2 * b1 + b2

def s5_scan(u, lam_re, lam_im, log_step, b_re, b_im, c_re, c_im, reverse):
    f32 = jnp.float32
    seq = u.shape[0]
    lam = lax.complex(lam_re.astype(f32), lam_im.astype(f32))
    step = jnp.exp(log_step.astype(f32))[:, None]
    lam_bar = jnp.exp(lam * step)
    b = lax.complex(b_re.astype(f32), b_im.astype(f32))
    b_bar = ((lam_bar - 1.0) / lam)[..., None] * b
    bu = jnp.einsum('gpc,lbgc->lbgp', b_bar, u.astype(jnp.complex64))
    a = jnp.broadcast_to(lam_bar[None, None], (seq, 1) + lam_bar.shape)
    _, states = lax.associative_scan(_linear_recurrence, (a, bu), axis=0, reverse=reverse)
    c = lax.complex(c_re.astype(f32), c_im.astype(f32))
    return jnp.einsum('gcp,lbgp->lbgc', c, states).real

def s5_branch(xa, lam_re, lam_im, log_step, b_re, b_im, c_re, c_im, d, w_glu):
    f32 = jnp.float32
    bsz, seq, _ = xa.shape
    u = xa.astype(f32).reshape(bsz, seq, S5_GROUPS, S5_GROUP).transpose(1, 0, 2, 3)
    y = d.astype(f32).reshape(S5_GROUPS, S5_GROUP) * u
    for direction, reverse in ((0, False), (1, True)):
        y = y + s5_scan(u, lam_re[direction], lam_im[direction], log_step[direction],
                        b_re[direction], b_im[direction], c_re[direction], c_im[direction],
                        reverse)
    y = jax.nn.gelu(y.transpose(1, 0, 2, 3).reshape(bsz, seq, S5_WIDTH))
    y = y * jax.nn.sigmoid(y @ w_glu.astype(f32))
    return y.astype(xa.dtype)

def sgu_branch(zu, zv, ln_g, ln_b, w_s, bias):
    bsz, seq, _ = zu.shape
    zu = jax.nn.gelu(zu)
    zv = layer_norm(jax.nn.gelu(zv), ln_g, ln_b)
    zv = zv.reshape(bsz, seq // CHUNK, CHUNK, SGU_HEADS, SGU_HEAD_DIM)
    sv = jnp.einsum('hts,bnshd->bnthd', w_s, zv) + bias.T[None, None, :, :, None]
    return zu * sv.reshape(bsz, seq, SGU_WIDTH)

def memory_cross_attention(hn, memn, w_q, w_k, w_v, w_o):
    bsz, seq, _ = hn.shape
    q = (hn @ w_q).reshape(bsz, seq, XATTN_HEADS, XATTN_HEAD_DIM)
    k = (memn @ w_k).reshape(bsz, MEM_LEN, XATTN_HEADS, XATTN_HEAD_DIM)
    v = (memn @ w_v).reshape(bsz, MEM_LEN, XATTN_HEADS, XATTN_HEAD_DIM)
    s = jnp.einsum('blhd,bmhd->bhlm', q, k).astype(jnp.float32) * (XATTN_HEAD_DIM ** -0.5)
    p = jax.nn.softmax(s, axis=-1).astype(v.dtype)
    o = jnp.einsum('bhlm,bmhd->blhd', p, v).reshape(bsz, seq, D_MODEL)
    return o @ w_o

def swiglu(hn, w_gate, w_up, w_down):
    return (jax.nn.silu(hn @ w_gate) * (hn @ w_up)) @ w_down

def first_inputs(seed: int = 0) -> dict:
    key = jax.random.key(seed)
    ks = iter(jax.random.split(key, 40))
    f32 = jnp.float32

    def nrm(shape, scale):
        return jax.random.normal(next(ks), shape, f32) * scale

    def gain(shape):
        return 1.0 + nrm(shape, 0.02)

    L, G, P, C, H = DEPTH, S5_GROUPS, S5_STATE, S5_GROUP, SGU_HEADS
    n_idx = jnp.arange(P, dtype=f32)
    lam_re = -0.5 + nrm((L, 2, G, P), 0.01)
    lam_im = math.pi * n_idx + nrm((L, 2, G, P), 0.01)
    log_step = jax.random.uniform(next(ks), (L, 2, G), f32, math.log(1e-3), math.log(1e-1))
    return {
        "x": nrm((BATCH, SEQ, D_MODEL), 1.0),
        "mem": nrm((BATCH, MEM_LEN, D_MODEL), 1.0),
        "mix_norm_g": gain((L, D_MODEL)),
        "w_in": nrm((L, D_MODEL, IN_COLS), D_MODEL ** -0.5),
        "s5_lam_re": lam_re,
        "s5_lam_im": lam_im,
        "s5_log_step": log_step,
        "s5_b_re": nrm((L, 2, G, P, C), (2 * C) ** -0.5),
        "s5_b_im": nrm((L, 2, G, P, C), (2 * C) ** -0.5),
        "s5_c_re": nrm((L, 2, G, C, P), (2 * P) ** -0.5),
        "s5_c_im": nrm((L, 2, G, C, P), (2 * P) ** -0.5),
        "s5_d": nrm((L, S5_WIDTH), 1.0),
        "s5_w_glu": nrm((L, S5_WIDTH, S5_WIDTH), S5_WIDTH ** -0.5),
        "sgu_ln_g": gain((L, SGU_WIDTH)),
        "sgu_ln_b": nrm((L, SGU_WIDTH), 0.02),
        "sgu_w": nrm((L, H, CHUNK, CHUNK), 0.5 * CHUNK ** -0.5),
        "sgu_bias": 1.0 + nrm((L, H, CHUNK), 0.02),
        "w_proj_a": nrm((L, S5_WIDTH, D_MODEL), S5_WIDTH ** -0.5),
        "w_proj_b": nrm((L, SGU_WIDTH, D_MODEL), SGU_WIDTH ** -0.5),
        "w_out": nrm((L, D_MODEL, D_MODEL), D_MODEL ** -0.5),
        "xattn_norm_g": gain((L, D_MODEL)),
        "mem_norm_g": gain((D_MODEL,)),
        "w_q": nrm((L, D_MODEL, D_MODEL), D_MODEL ** -0.5),
        "w_k": nrm((L, D_MODEL, D_MODEL), D_MODEL ** -0.5),
        "w_v": nrm((L, D_MODEL, D_MODEL), D_MODEL ** -0.5),
        "w_xo": nrm((L, D_MODEL, D_MODEL), D_MODEL ** -0.5),
        "ffn_norm_g": gain((L, D_MODEL)),
        "w_gate": nrm((L, D_MODEL, D_FF), D_MODEL ** -0.5),
        "w_up": nrm((L, D_MODEL, D_FF), D_MODEL ** -0.5),
        "w_down": nrm((L, D_FF, D_MODEL), D_FF ** -0.5),
        "final_norm_g": gain((D_MODEL,)),
    }

def first_block(x, mem, mix_norm_g, w_in, s5_lam_re, s5_lam_im, s5_log_step, s5_b_re, s5_b_im,
              s5_c_re, s5_c_im, s5_d, s5_w_glu, sgu_ln_g, sgu_ln_b, sgu_w, sgu_bias,
              w_proj_a, w_proj_b, w_out, xattn_norm_g, mem_norm_g, w_q, w_k, w_v, w_xo,
              ffn_norm_g, w_gate, w_up, w_down, final_norm_g):
    memn = rms_norm(mem, mem_norm_g)
    h = x
    for i in range(DEPTH):
        n = rms_norm(h, mix_norm_g[i])
        proj = n @ w_in[i]
        xa = proj[..., :OFF_U]
        zu = proj[..., OFF_U:OFF_V]
        zv = proj[..., OFF_V:OFF_GA]
        gate_a = jax.nn.sigmoid(proj[..., OFF_GA:OFF_GB])
        gate_b = jax.nn.sigmoid(proj[..., OFF_GB:])
        ya = s5_branch(xa, s5_lam_re[i], s5_lam_im[i], s5_log_step[i], s5_b_re[i], s5_b_im[i],
                       s5_c_re[i], s5_c_im[i], s5_d[i], s5_w_glu[i])
        yb = sgu_branch(zu, zv, sgu_ln_g[i], sgu_ln_b[i], sgu_w[i], sgu_bias[i])
        merged = gate_a * (ya @ w_proj_a[i]) + gate_b * (yb @ w_proj_b[i])
        h = h + merged @ w_out[i]
        h = h + memory_cross_attention(rms_norm(h, xattn_norm_g[i]), memn,
                                       w_q[i], w_k[i], w_v[i], w_xo[i])
        h = h + swiglu(rms_norm(h, ffn_norm_g[i]), w_gate[i], w_up[i], w_down[i])
    return rms_norm(h, final_norm_g)


DEPTH_2 = 2

HEAD_DIM = 64
BLOCK = 128
ROPE_THETA = 10000.0
FOX_HEADS = 8
DSA_HEADS = 8
IDX_HEADS = 4
IDX_DIM = 64
DSA_TOPK_MAX = 256
RET_HEADS = 8
SWA_Q_HEADS = 8
SWA_KV_HEADS = 2
SWA_WINDOW = 128
N_BRANCH = 4
BRANCH_WIDTH = 8 * HEAD_DIM
D_FF_2 = 2816
CONV_WIDTH = 3

COL_SIZES = (
    FOX_HEADS * HEAD_DIM, FOX_HEADS * HEAD_DIM, FOX_HEADS * HEAD_DIM, FOX_HEADS,
    DSA_HEADS * HEAD_DIM, HEAD_DIM, HEAD_DIM, IDX_HEADS * IDX_DIM, IDX_DIM, IDX_HEADS,
    RET_HEADS * HEAD_DIM, RET_HEADS * HEAD_DIM, RET_HEADS * HEAD_DIM, RET_HEADS * HEAD_DIM,
    SWA_Q_HEADS * HEAD_DIM, SWA_KV_HEADS * HEAD_DIM, SWA_KV_HEADS * HEAD_DIM,
    N_BRANCH * D_MODEL,
)
N_IN = sum(COL_SIZES)


def rmsnorm(x, g):
    x32 = x.astype(jnp.float32)
    y = x32 * lax.rsqrt(jnp.mean(x32 * x32, axis=-1, keepdims=True) + EPS)
    return (y * g.astype(jnp.float32)).astype(x.dtype)

def rope(x, pos):
    d = x.shape[-1]
    half = d // 2
    inv = 1.0 / (ROPE_THETA ** (jnp.arange(half, dtype=jnp.float32) * 2.0 / d))
    ang = pos[:, None] * inv[None, :]
    cos = jnp.cos(ang)[None, :, None, :]
    sin = jnp.sin(ang)[None, :, None, :]
    x32 = x.astype(jnp.float32)
    x1, x2 = x32[..., :half], x32[..., half:]
    return jnp.concatenate([x1 * cos - x2 * sin, x2 * cos + x1 * sin], axis=-1).astype(x.dtype)

def to_blocks(t, nb):
    return t.reshape(t.shape[0], nb, BLOCK, *t.shape[2:]).swapaxes(0, 1)

def from_blocks(t):
    t = t.swapaxes(0, 1)
    return t.reshape(t.shape[0], t.shape[1] * t.shape[2], -1)

def forgetting_attention(q, k, v, f_logit, f_bias):
    B, S, H, d = q.shape
    nb = S // BLOCK
    neg = jnp.finfo(jnp.float32).min
    logf = jax.nn.log_sigmoid((f_logit + f_bias).astype(jnp.float32))
    F = jnp.cumsum(logf, axis=1).transpose(0, 2, 1)
    Fq_blocks = F.reshape(B, H, nb, BLOCK).transpose(2, 0, 1, 3)
    key_pos = jnp.arange(S, dtype=jnp.int32)
    scale = d ** -0.5

    def blk(inp):
        qb, Fq, off = inp
        t = off + jnp.arange(BLOCK, dtype=jnp.int32)
        logits = (jnp.einsum('bqhd,bshd->bhqs', qb, k).astype(jnp.float32) * scale
                  + Fq[..., None] - F[:, :, None, :])
        causal = key_pos[None, :] <= t[:, None]
        p = jax.nn.softmax(jnp.where(causal[None, None], logits, neg), axis=-1)
        return jnp.einsum('bhqs,bshd->bqhd', p.astype(v.dtype), v)

    offs = jnp.arange(nb, dtype=jnp.int32) * BLOCK
    out = lax.map(blk, (to_blocks(q, nb), Fq_blocks, offs))
    return from_blocks(out)

def dsa_attention(q, k, v, qi, ki, wi):
    B, S, H, d = q.shape
    nb = S // BLOCK
    topk = min(DSA_TOPK_MAX, S // 4)
    neg = jnp.finfo(jnp.float32).min
    key_pos = jnp.arange(S, dtype=jnp.int32)
    bidx = jnp.arange(B, dtype=jnp.int32)[:, None, None]
    ki32 = ki.astype(jnp.float32)
    w_scale = (IDX_HEADS ** -0.5) * (IDX_DIM ** -0.5)
    scale = d ** -0.5

    def blk(inp):
        qb, qib, wb, off = inp
        t = off + jnp.arange(BLOCK, dtype=jnp.int32)
        dots = jnp.einsum('bqhd,bsd->bqhs', qib.astype(jnp.float32), ki32)
        score = jnp.einsum('bqhs,bqh->bqs', jax.nn.relu(dots), wb.astype(jnp.float32) * w_scale)
        causal = key_pos[None, :] <= t[:, None]
        score = jnp.where(causal[None], score, neg)
        _, sel = lax.top_k(score, topk)
        kg = k[bidx, sel]
        vg = v[bidx, sel]
        logits = jnp.einsum('bqhd,bqkd->bhqk', qb, kg).astype(jnp.float32) * scale
        valid = (sel <= t[None, :, None])[:, None]
        p = jax.nn.softmax(jnp.where(valid, logits, neg), axis=-1)
        return jnp.einsum('bhqk,bqkd->bqhd', p.astype(vg.dtype), vg)

    offs = jnp.arange(nb, dtype=jnp.int32) * BLOCK
    out = lax.map(blk, (to_blocks(q, nb), to_blocks(qi, nb), to_blocks(wi, nb), offs))
    return from_blocks(out)

def retention(q, k, v):
    B, S, H, d = q.shape
    dv = v.shape[-1]
    C = BLOCK
    nc = S // C
    log_g = jnp.log(1.0 - 2.0 ** (-5.0 - jnp.arange(H, dtype=jnp.float32)))
    n = jnp.arange(C, dtype=jnp.float32)
    diff = n[:, None] - n[None, :]
    Dm = jnp.where(diff[None] >= 0, jnp.exp(diff[None] * log_g[:, None, None]), 0.0)
    xi = jnp.exp((n + 1.0)[None, :] * log_g[:, None])
    zeta = jnp.exp((C - 1.0 - n)[None, :] * log_g[:, None])
    gC = jnp.exp(C * log_g)

    def chunks(t):
        return t.reshape(B, nc, C, H, t.shape[-1]).transpose(1, 0, 3, 2, 4)

    def step(R, inp):
        qc, kc, vc = inp
        inner = jnp.einsum('bhnm,bhme->bhne', jnp.einsum('bhnd,bhmd->bhnm', qc, kc) * Dm[None], vc)
        cross = jnp.einsum('bhnd,bhde->bhne', qc, R) * xi[None, :, :, None]
        R = R * gC[None, :, None, None] + jnp.einsum('bhmd,bhme->bhde', kc * zeta[None, :, :, None], vc)
        return R, inner + cross

    R0 = jnp.zeros((B, H, d, dv), jnp.float32)
    _, ys = lax.scan(step, R0, (chunks(q), chunks(k), chunks(v)))
    return ys.transpose(1, 0, 3, 2, 4).reshape(B, S, H, dv)

def head_groupnorm(r, g):
    mu = jnp.mean(r, axis=-1, keepdims=True)
    var = jnp.mean(jnp.square(r - mu), axis=-1, keepdims=True)
    y = (r - mu) * lax.rsqrt(var + EPS)
    return y.reshape(r.shape[0], r.shape[1], -1) * g.astype(jnp.float32)

def sliding_window_gqa(q, k, v, sinks):
    B, S, HQ, d = q.shape
    HKV = k.shape[2]
    G = HQ // HKV
    W = SWA_WINDOW
    nb = S // W
    neg = jnp.finfo(jnp.float32).min
    qb = q.reshape(B, nb, W, HKV, G, d)
    kb = k.reshape(B, nb, W, HKV, d)
    vb = v.reshape(B, nb, W, HKV, d)
    shift = lambda t: jnp.concatenate([jnp.zeros_like(t[:, :1]), t[:, :-1]], axis=1)
    kband = jnp.concatenate([shift(kb), kb], axis=2)
    vband = jnp.concatenate([shift(vb), vb], axis=2)
    logits = jnp.einsum('bnqgrd,bnkgd->bngrqk', qb, kband).astype(jnp.float32) * (d ** -0.5)
    i = jnp.arange(W)[:, None]
    j = jnp.arange(2 * W)[None, :]
    in_band = (j > i) & (j <= i + W)
    kpos = jnp.arange(nb)[:, None, None] * W - W + j[None]
    mask = in_band[None] & (kpos >= 0)
    logits = jnp.where(mask[None, :, None, None], logits, neg)
    sink = sinks.astype(jnp.float32).reshape(HKV, G)[None, None, :, :, None, None]
    m = jnp.maximum(jnp.max(logits, axis=-1, keepdims=True), sink)
    p = jnp.exp(logits - m)
    denom = jnp.sum(p, axis=-1, keepdims=True) + jnp.exp(sink - m)
    out = jnp.einsum('bngrqk,bnkgd->bnqgrd', (p / denom).astype(vband.dtype), vband)
    return out.reshape(B, S, HQ * d)

def causal_dwconv(u, w, b):
    C = u.shape[-1]
    out = lax.conv_general_dilated(u, w.astype(u.dtype)[:, None, :], window_strides=(1,),
                                   padding=[(CONV_WIDTH - 1, 0)],
                                   dimension_numbers=('NWC', 'WIO', 'NWC'),
                                   feature_group_count=C)
    return out + b.astype(u.dtype)

def second_inputs(seed: int = 0) -> dict:
    key = jax.random.key(seed)
    ks = jax.random.split(key, 14)
    nrm = lambda k, shape: jax.random.normal(k, shape, jnp.float32)
    return {
        "x": nrm(ks[0], (BATCH, SEQ, D_MODEL)),
        "attn_norm": 1.0 + 0.02 * nrm(ks[1], (DEPTH_2, D_MODEL)),
        "w_in": nrm(ks[2], (DEPTH_2, D_MODEL, N_IN)) * D_MODEL ** -0.5,
        "forget_bias": 3.0 + 0.1 * nrm(ks[3], (DEPTH_2, FOX_HEADS)),
        "ret_norm": 1.0 + 0.02 * nrm(ks[4], (DEPTH_2, RET_HEADS * HEAD_DIM)),
        "attn_sinks": 0.1 * nrm(ks[5], (DEPTH_2, SWA_Q_HEADS)),
        "w_branch": nrm(ks[6], (DEPTH_2, N_BRANCH, BRANCH_WIDTH, D_MODEL)) * BRANCH_WIDTH ** -0.5,
        "w_out": nrm(ks[7], (DEPTH_2, D_MODEL, D_MODEL)) * D_MODEL ** -0.5,
        "ffn_norm": 1.0 + 0.02 * nrm(ks[8], (DEPTH_2, D_MODEL)),
        "w_up": nrm(ks[9], (DEPTH_2, D_MODEL, 2 * D_FF_2)) * D_MODEL ** -0.5,
        "conv_w": nrm(ks[10], (DEPTH_2, CONV_WIDTH, 2 * D_FF_2)) * CONV_WIDTH ** -0.5,
        "conv_b": 0.01 * nrm(ks[11], (DEPTH_2, 2 * D_FF_2)),
        "w_down": nrm(ks[12], (DEPTH_2, D_FF_2, D_MODEL)) * D_FF_2 ** -0.5,
        "final_norm": 1.0 + 0.02 * nrm(ks[13], (D_MODEL,)),
    }

def second_block(x, attn_norm, w_in, forget_bias, ret_norm, attn_sinks, w_branch, w_out,
              ffn_norm, w_up, conv_w, conv_b, w_down, final_norm):
    B, S, D = x.shape
    pos = jnp.arange(S, dtype=jnp.float32)
    split_at = np.cumsum(COL_SIZES)[:-1].tolist()
    heads = lambda t, n: t.reshape(B, S, n, -1)
    for l in range(DEPTH_2):
        h = rmsnorm(x, attn_norm[l])
        z = h @ w_in[l]
        (qA, kA, vA, fA, qB, kB, vB, qI, kI, wI,
         qC, kC, vC, gC, qD, kD, vD, gates) = jnp.split(z, split_at, axis=-1)

        yA = forgetting_attention(heads(qA, FOX_HEADS), heads(kA, FOX_HEADS), heads(vA, FOX_HEADS),
                                  fA, forget_bias[l])
        yB = dsa_attention(rope(heads(qB, DSA_HEADS), pos), rope(kB[:, :, None], pos)[:, :, 0], vB,
                           rope(heads(qI, IDX_HEADS), pos), rope(kI[:, :, None], pos)[:, :, 0], wI)
        r = retention(rope(heads(qC, RET_HEADS), pos).astype(jnp.float32),
                      (rope(heads(kC, RET_HEADS), pos) * HEAD_DIM ** -0.5).astype(jnp.float32),
                      heads(vC, RET_HEADS).astype(jnp.float32))
        yC = (head_groupnorm(r, ret_norm[l]) * jax.nn.silu(gC.astype(jnp.float32))).astype(x.dtype)
        yD = sliding_window_gqa(rope(heads(qD, SWA_Q_HEADS), pos), rope(heads(kD, SWA_KV_HEADS), pos),
                                heads(vD, SWA_KV_HEADS), attn_sinks[l])

        ys = jnp.stack([yA, yB, yC, yD], axis=2)
        branch = jnp.einsum('bsnc,ncd->bsnd', ys, w_branch[l])
        g = jax.nn.sigmoid(gates.reshape(B, S, N_BRANCH, D))
        merged = jnp.sum(g * branch, axis=2)
        x = x + merged @ w_out[l]

        h = rmsnorm(x, ffn_norm[l])
        u = causal_dwconv(h @ w_up[l], conv_w[l], conv_b[l])
        a, b = jnp.split(u, 2, axis=-1)
        x = x + (jax.nn.silu(a) * b) @ w_down[l]
    return rmsnorm(x, final_norm)


def setup_inputs(seed=0):
    out = dict(first_inputs(seed))
    for name, value in second_inputs(seed + 1).items():
        if name != "x":
            out[name + "_2"] = value
    return out


def reference(
    x, mem, mix_norm_g, w_in, s5_lam_re, s5_lam_im, s5_log_step, s5_b_re, s5_b_im, s5_c_re,
    s5_c_im, s5_d, s5_w_glu, sgu_ln_g, sgu_ln_b, sgu_w, sgu_bias, w_proj_a, w_proj_b, w_out,
    xattn_norm_g, mem_norm_g, w_q, w_k, w_v, w_xo, ffn_norm_g, w_gate, w_up, w_down,
    final_norm_g, attn_norm_2, w_in_2, forget_bias_2, ret_norm_2, attn_sinks_2, w_branch_2,
    w_out_2, ffn_norm_2, w_up_2, conv_w_2, conv_b_2, w_down_2, final_norm_2,
):
    x = first_block(
        x, mem, mix_norm_g, w_in, s5_lam_re, s5_lam_im, s5_log_step, s5_b_re, s5_b_im, s5_c_re,
        s5_c_im, s5_d, s5_w_glu, sgu_ln_g, sgu_ln_b, sgu_w, sgu_bias, w_proj_a, w_proj_b, w_out,
        xattn_norm_g, mem_norm_g, w_q, w_k, w_v, w_xo, ffn_norm_g, w_gate, w_up, w_down,
        final_norm_g,
    )
    return second_block(
        x, attn_norm_2, w_in_2, forget_bias_2, ret_norm_2, attn_sinks_2, w_branch_2, w_out_2,
        ffn_norm_2, w_up_2, conv_w_2, conv_b_2, w_down_2, final_norm_2,
    )


_drawn_inputs = setup_inputs


def setup_inputs(seed=0):
    import zlib

    import numpy as np

    out = dict(_drawn_inputs(seed))
    spreads = {}
    factors = {'s5_lam_re': 64.0,
     'sgu_ln_g': 6.073,
     'sgu_ln_b': 6.312,
     'sgu_bias': 3.577,
     'xattn_norm_g': 8.0,
     'mem_norm_g': 6.455,
     'forget_bias_2': 31.544,
     'ret_norm_2': 5.306,
     'attn_sinks_2': 59.47,
     'conv_b_2': 4.88,
     'final_norm_2': 7.737,
     'ffn_norm_g': 6.608,
     'ffn_norm_2': 3.678}
    for name, (base, spread) in spreads.items():
        noise = np.random.default_rng([zlib.crc32(name.encode()), seed]).standard_normal(out[name].shape)
        drawn = base * np.exp(spread * noise) if base else spread * noise
        out[name] = __import__('jax').numpy.asarray(drawn.astype(out[name].dtype))
    for name, factor in factors.items():
        out[name] = (out[name] * factor).astype(out[name].dtype)
    return out
```

```python
from contextlib import ExitStack

import numpy as np
import concourse.bass as bass
from concourse import mybir

ALU = mybir.AluOpType
ACT = mybir.ActivationFunctionType
F32 = mybir.dt.float32
AXX = mybir.AxisListType.X

P = 128
T = 512
NB = T // P
D = 1024
KD = D // P
M = 256
EPS = 1e-6
FF = 2816
NF = FF // P
NG = NF // 2
H = 8
HD = 64
TOPK = 128
LAYERS = 2
NEG = -1e30
GONE = -3e38
GROUPS, STATE, CHAN = 32, 64, 16
QUADS = 8
TWO_PI = 6.283185
INV_2PI = float(np.float32(1.0 / (2.0 * np.pi)))
C1 = 6.28125
C2 = float(2.0 * np.pi - 6.28125)
ROUND = 12582912.0

FOX_Q, FOX_K, FOX_V, FOX_F = 0, 512, 1024, 1536
DSA_Q, DSA_K, DSA_V, IDX_Q, IDX_K, IDX_W = 1544, 2056, 2120, 2184, 2440, 2504
RET_Q, RET_K, RET_V, RET_G = 2508, 3020, 3532, 4044
SWA_Q, SWA_K, SWA_V = 4556, 5068, 5196
GATES = 5324
MF, MW, MVB, MVD, MIX2 = 0, 8, 12, 76, 204

SLOTS = 8
UNIT = 2 * 512

FIRST = [[("xa", 4, 1)], [("glu", 2, 1)], [("zu0", 4, 1), ("zu1", 4, 1), ("zv0", 4, 1), ("zv1", 4, 1)],
         ("loop", 2, [("ga", 4, 1), ("pa", 2, 1), ("gb", 4, 1), ("pb", 4, 1), (None, 2, 0)]),
         [("wo0", 4, 1), ("wo1", 4, 1), ("wk0", 4, 1), ("wk1", 4, 1), ("wv0", 4, 1), ("wv1", 4, 1),
          ("wq0", 4, 1), ("wq1", 4, 1), ("xo0", 4, 1), ("xo1", 4, 1)],
         ("loop", 5, [("upa", 4, 2), ("upb", 4, 2)]), [("upc", 4, 2), ("dn0", 11, 1), ("dn1", 11, 1)]]
LAYER = [[("mix1", 4, 4), ("mix2", 4, 4), ("qB", 4, 1), ("qA", 4, 1), ("kA", 4, 1), ("vA", 4, 1),
          ("qC", 4, 1), ("kC", 4, 1), ("vC", 4, 1), ("gC", 4, 1), ("qD", 4, 1)],
         ("loop", 2, [(f"{s}{n}", u, 1) for n in range(4) for s, u in (("gt", 4), ("br", 2))]),
         [("wo0", 4, 1), ("wo1", 4, 1)],
         ("loop", 5, [("upa", 4, 2), ("upb", 4, 2)]), [("upc", 4, 2), ("dn0", 11, 1), ("dn1", 11, 1)]]


def pad_units(parts):
    n = sum((p[1] if p[0] == "loop" else 1) * sum(u for _, u, _ in (p[2] if p[0] == "loop" else p))
            for p in parts)
    return parts + [[(None, -n % SLOTS, 0)]]


PRIMED = 1


class Ring:

    def __init__(self):
        self.slot, self.used, self.landed, self.room, self.units = {}, {}, {}, {}, {}
        at = used = 0
        pieces, owner = [0] * SLOTS, [0] * SLOTS
        stages = [("a", 0, pad_units(FIRST))] + [("b", l, pad_units(LAYER)) for l in range(LAYERS)]
        for stage, l, parts in stages:
            for part in parts:
                reps, body = (part[1], part[2]) if part[0] == "loop" else (1, part)
                for i in range(reps):
                    for name, units, dmas in body:
                        for u in range(units):
                            s = at % SLOTS
                            at += 1
                            if name is None:
                                continue
                            key = (stage + name, u)
                            pieces[s] += 16 * dmas
                            assert self.slot.setdefault(key, s) == s
                            self.units[stage + name] = units
                            self.used[key + (l, i)] = used
                            self.landed[key + (l, i)] = pieces[s]
                            room = owner[s] - used
                            self.room[key] = max(self.room.get(key, room), room)
                            used += 1
                            owner[s] = used

    def at(self, table, name, u, l, i):
        v = table[(name, u, 0, 0)]
        for reg, other in ((l, (1, 0)), (i, (0, 1))):
            if (name, u) + other in table:
                v = v + reg * (table[(name, u) + other] - table[(name, u, 0, 0)])
        return v


JOBS_FIRST = ["vecs", "x0", "x1", "memT", "ss_mem", "ss_mix", "xa", "s5col", "s5B", "s5C", "glu", "wsT",
              "zu0", "zu1", "zv0", "zv1", "sv0", "sv1", (2, ["ga", "pa", "gb", "pb"]),
              "wo0", "wo1", "wk0", "wk1", "wv0", "wv1", "ss_xa", "wq0", "wq1",
              "xs0", "xs1", "xt0", "xs2", "xv0", "xt1", "xs3", "xv1", "xt2", "xv2", "xt3", "xv3",
              "xo0", "xo1", "ss_ff", (5, ["upa", "upb"]), "upc", "dn0", "dn1", "ss_fin"]
JOBS_LAYER = ["vecs", "ss_at", "mix1", "mix2", "ix1", "ix2", "ix3", "qB", "qA", "kA", "lf", "vA",
              "ft", "fb0", "fb1", "tA", "tB", "qC", "kC", "vC", "gC", "tC", "qD", "tD",
              (2, [f"{s}{n}" for n in range(4) for s in ("gt", "br")]), "wo0", "wo1", "ss_ff",
              (5, ["upa", "upb"]), "upc", "dn0", "dn1"]
JOBS_LAST = ["ss_fin", "out0", "out1"]


class Jobs:

    def __init__(self):
        self.half, self.before = {}, {}
        seq, count = 0, [0, 0]
        for stage, l, jobs in [("a", 0, JOBS_FIRST)] + [("b", l, JOBS_LAYER) for l in range(LAYERS)] + [
                ("c", 0, JOBS_LAST)]:
            for job in jobs:
                reps, body = job if isinstance(job, tuple) else (1, [job])
                for i in range(reps):
                    for name in body:
                        h = seq % 2
                        assert self.half.setdefault(stage + name, h) == h, (stage, name)
                        self.before[(stage + name, l, i)] = count[h]
                        count[h] += 1
                        seq += 1

    def nth(self, name, l=0, i=0):
        v = self.before[(name, 0, 0)]
        for reg, other in ((l, (1, 0)), (i, (0, 1))):
            if (name,) + other in self.before:
                v = v + reg * (self.before[(name,) + other] - self.before[(name, 0, 0)])
        return v


NORMS = {"ass_mem": 0, "ass_mix": 1, "ass_xa": 2, "ass_ff": 3, "ass_fin": 4, "bss_at": 5, "bss_ff": 6, "css_fin": 9}


def nth_norm(name, l=0):
    return NORMS[name] + (l * 2 if name[0] == "b" else 0) + 1


class Chain:

    def __init__(self, eng, sem, base=0):
        self.eng, self.sem, self.base, self.n = eng, sem, base, 0

    def __call__(self, ins):
        self.n += 1
        ins.then_inc(self.sem, 1)
        self.eng.wait_ge(self.sem, self.base + self.n)


CONSTS = (("ident", P), ("ones", P), ("cmask", T), ("band", 2 * P), ("cos", T), ("sin", T),
          ("dist", T), ("logdecay", H))
N_CONSTS = sum(n for _, n in CONSTS)


def constants():
    f32, row, col = np.float32, np.arange(P)[:, None], np.arange(T)[None, :]
    inv = (1.0 / np.power(f32(10000.0), np.arange(HD // 2, dtype=f32) * f32(2.0) / f32(HD))).astype(f32)
    angle = (np.arange(T, dtype=f32)[None, :] * inv[np.arange(P) % 32][:, None]).astype(f32).astype(np.float64)
    sign = np.where(np.arange(P) % HD < 32, -1.0, 1.0)[:, None]
    j = np.arange(2 * P)[None, :]
    tables = {
        "ident": np.eye(P), "ones": np.ones((P, P)), "iota": np.broadcast_to(col, (P, T)),
        "cmask": np.where(col - (T - P) > row, NEG, 0.0),
        "band": np.where((j > row) & (j <= row + P), 0.0, NEG),
        "cos": np.cos(angle), "sin": np.sin(angle) * sign,
        "dist": np.where(col >= row, col - row, -NEG),
        "logdecay": np.broadcast_to(np.log(1.0 - 2.0 ** (-5.0 - np.arange(H)))[None, :], (P, H)),
    }
    return np.ascontiguousarray(np.concatenate([np.asarray(tables[n], f32) for n in [n for n, _ in CONSTS] + ["iota"]], axis=1))


V_MIX, V_MEM, V_XA, V_FF, V_FIN, V_FIN2, V_D, V_ROWS = 0, 8, 16, 24, 32, 40, 48, 52
W_AT, W_FF, W_RET, W_CB, W_C2, W_C0, W_C1 = 0, 8, 16, 20, 64, 108, 152
W_ROWS1, W_ROWS2 = 108, 88


def two_blocks(nc, I, out):
    ring, jobs = Ring(), Jobs()
    ds = bass.ds
    with ExitStack() as ctx:
        def sb(name, *shape):
            return ctx.enter_context(nc.sbuf_tensor(name, [P, *shape], F32))

        class Signals(dict):
            def __missing__(self, name):
                self[name] = ctx.enter_context(nc.semaphore(name))
                return self[name]

        S = Signals()
        landed = [S[f"weights_landed{s}"] for s in range(SLOTS)]
        weights_used = S["weights_used"]
        drained = [S["half0_drained"], S["half1_drained"]]

        ps = [ctx.enter_context(nc.psum_tensor(f"half{h}", [P, 4 * T], F32)) for h in range(2)]
        hT = sb("hT", KD, T)
        nT = sb("nT", KD, T)
        slot = sb("slot", SLOTS, 2, 512)
        consts = sb("consts", N_CONSTS)
        C, at = {}, 0
        for name, n in CONSTS:
            C[name] = consts[:, at:at + n]
            at += n
        ident, ones = C["ident"], C["ones"]
        vrow = sb("vrow", 2, P)
        vec = sb("vec", W_ROWS1 + W_ROWS2)
        vec0 = sb("vec0", V_ROWS)
        rms = sb("rms", T)
        qz = sb("qz", 2, T)
        small = sb("small", 160)
        eps, half_pi = small[:, 0:1], small[:, 1:2]
        stat = small[:, 2:154]
        arena = sb("arena", 31744)

        def A(at, *shape):
            n = int(np.prod(shape))
            v = arena[:, at:at + n]
            if len(shape) == 2:
                v = v.rearrange("p (a b) -> p a b", b=shape[1])
            elif len(shape) == 3:
                v = v.rearrange("p (a b c) -> p a b c", b=shape[1], c=shape[2])
            return v

        def banks(h, n=4, w=T):
            return ps[h][:, 0:n * T].rearrange("p (a b) -> p a b", b=T)[:, :, 0:w]

        x_in, mem_in, mT = A(0, NB, D), A(4096, 2, D), A(6144, KD, M)
        uT, yT = A(8192, NB, T), A(10240, NB, T)
        s5w = A(12288, QUADS, 5, P)
        cnat = [A(0, QUADS, P), A(1024, QUADS, P)]
        zb = [A(2048, 32, 32), A(3072, 32, 32)]
        ust, stg = A(4096, T), A(4608, 2, 5 * P)
        trig = A(17408, 4, 2, T)
        turn, whole = A(21504, 2, T), A(22528, 2, T)
        prod, zt, st = A(23552, 2, 4, T), A(27648, 2, 2, T), A(29696, 2, 2, T)
        row = A(17408, 24, P)
        bnat, bprod = [A(23552, 32, CHAN), A(24064, 32, CHAN)], [A(24576, 32, CHAN), A(25088, 32, CHAN),
                                                                 A(25600, 32, CHAN), A(26112, 32, CHAN)]
        s5col = sb("s5col", 4, 32)
        zv, zu = A(12288, NB, D), A(16384, KD, T)
        wsn, wsT, sgub = A(20480, H, P), A(21504, H, P), A(22528, H, P)
        lng, lnb, svt = A(23552, D), A(24576, D), A(25600, 4, T)
        gate_a, merged_a, tmp_a = A(0, 2, 4, T), A(20480, KD, T), A(29696, 4, T)
        xq, xk, xv = A(12288, KD, T), A(8192, KD, M), A(10240, 2, D)
        xp, xpT, xo = A(16384, 2, NB, M), A(18432, 2, 2, T), A(20480, KD, T)
        ff, sg_a = A(0, NF, T), A(11264, 2, 2, T)

        Q, K, V = A(0, NB, T), A(2048, NB, T), A(4096, NB, T)
        qB, gC, qD = A(6144, NB, T), A(8192, NB, T), A(10240, NB, T)
        mix1, mix2 = A(12288, NB, T), A(14336, NB, MIX2)
        part = A(15360, NB, T)
        selb = A(17408, 1280)
        logit = A(18688, 2, 1280)
        probT = A(21248, 1280)
        fb = A(22528, H, T)
        otm, yA = A(26624, NB, T), A(28672, NB, T)
        kBB, kII, kDD = A(30720, T), A(31232, T), A(2048, 2, T)
        fx, fe, fF, onehot = A(18688, T), A(19200, T), A(19712, T), A(20224, H, P)
        relu, score = A(28672, NB, T), [None, A(21248, 256), A(21504, 384), A(21888, 512)]
        decay = A(22528, 2, T)
        gsq = A(15360, NB, T)
        gate_b, merged_b, tmp_b = A(15360, 2, 4, T), A(22528, KD, T), A(26624, 4, T)
        conv, sg_b = A(12288, 2, 4, T), A(16384, 2, 2, T)
        o_out = A(0, NB, D)
        ftm = sb("ftm", NB, H)
        sink = sb("sink", H)
        fbias = sb("fbias", 1)

        causal = [(0, 0, 128, 896, 0), (1, 0, 256, 1024, 128), (2, 0, 384, 512, 384), (3, 0, 512, 0, 768)]
        window = [(0, 0, 128, 896, 0), (1, 0, 256, 1024, 128), (2, 128, 256, 512, 384), (3, 256, 256, 0, 640)]
        forward = [(0, 512, 0, 0), (1, 384, 512, 512), (2, 256, 1024, 896), (3, 128, 896, 1152)]

        def turned_blocks(blocks):
            return [(j, b, k0, at) for j in range(NB) for b, k0, n, _, at in blocks if k0 <= j * P < k0 + n]

        def nth_head(br, l):
            return l * (4 * H) + ("fox", "dsa", "ret", "swa").index(br) * H

        def nth_soft(br, l):
            return l * (3 * H) + ("fox", "dsa", "swa").index(br) * H

        def done(eng, name, l=0, i=0):
            eng.wait_ge(weights_used, ring.at(ring.used, name, ring.units[name] - 1, l, i) + 1)

        def plain(eng):
            eng.nop(nofuse=True)

        def read_out(eng, name, l=0, i=0):
            eng.wait_ge(drained[jobs.half[name]], jobs.nth(name, l, i) + 1)

        def lin2(w, r0, c0):
            return lambda u: [(slice(0, 512), w[ds(r0 + u * 256, 256), ds(c0, 512)])]

        block = ctx.enter_context(nc.Block())

        @block.sync
        def _(sp):
            sp.dma_start(x_in, I["x"].rearrange("(b p) d -> p b d", p=P)).then_inc(S["x_loaded"], 16)

            def load(name, pieces, l=0, i=0):
                for u in range(ring.units[name]):
                    s = ring.slot[(name, u)]
                    free = ring.at(ring.used, name, u, l, i) + ring.room[(name, u)]
                    if not isinstance(free, int) or free > 0:
                        sp.wait_ge(weights_used, free)
                        plain(sp)
                    for cols, src in pieces(u):
                        n = src.shape[-1]
                        sp.dma_start(slot[:, s, :, cols], src.rearrange("(k p) n -> p k n", p=P))\
                          .then_inc(landed[s], 16)

            w = I["w_in"]
            load("axa", lin2(w, 0, 0))
            load("aglu", lin2(I["s5_w_glu"], 0, 0))
            for g in range(2):
                load(f"azu{g}", lin2(w, 0, 512 + 512 * g))
            for g in range(2):
                load(f"azv{g}", lin2(w, 0, 1536 + 512 * g))
            with sp.Fori(0, 2) as c:
                load("aga", lin2(w, 0, c * 512 + 2560), 0, c)
                load("apa", lin2(I["w_proj_a"], 0, c * 512), 0, c)
                load("agb", lin2(w, 0, c * 512 + 3584), 0, c)
                load("apb", lin2(I["w_proj_b"], 0, c * 512), 0, c)
            for name, key in (("wo", "w_out"), ("wk", "w_k"), ("wv", "w_v"), ("wq", "w_q"), ("xo", "w_xo")):
                for g in range(2):
                    load(f"a{name}{g}", lin2(I[key], 0, 512 * g))

            def up(first, second, r0, g):
                return lambda u: [(slice(0, 256), first[ds(r0 + u * 256, 256), ds(g * 256, 256)]),
                                  (slice(256, 512), second(u, g))]

            def up_a(g):
                return up(I["w_gate"], lambda u, g: I["w_up"][ds(u * 256, 256), ds(g * 256, 256)], 0, g)

            with sp.Fori(0, 5) as i:
                load("aupa", up_a(i * 2), 0, i)
                load("aupb", up_a(i * 2 + 1), 0, i)
            load("aupc", up_a(NG - 1))
            for g in range(2):
                load(f"adn{g}", lin2(I["w_down"], 0, 512 * g))

            w = I["w_in_2"]
            with sp.Fori(0, LAYERS) as l:
                r = l * D

                def cols(*pieces):
                    def unit(u):
                        at, got = 0, []
                        for c0, n in pieces:
                            got.append((slice(at, at + n), w[ds(r + u * 256, 256), c0:c0 + n]))
                            at += n
                        return got
                    return unit

                load("bmix1", cols((IDX_Q, 256), (DSA_K, 64), (IDX_K, 64), (SWA_K, 128)), l)
                load("bmix2", cols((FOX_F, 8), (IDX_W, 4), (DSA_V, 64), (SWA_V, 128)), l)
                for name, c0 in (("qB", DSA_Q), ("qA", FOX_Q), ("kA", FOX_K), ("vA", FOX_V), ("qC", RET_Q),
                                 ("kC", RET_K), ("vC", RET_V), ("gC", RET_G), ("qD", SWA_Q)):
                    load("b" + name, lin2(w, r, c0), l)
                with sp.Fori(0, 2) as c:
                    for n in range(4):
                        load(f"bgt{n}", lin2(w, r, c * 512 + GATES + n * D), l, c)
                        load(f"bbr{n}", lin2(I["w_branch_2"], l * 2048 + n * 512, c * 512), l, c)
                for g in range(2):
                    load(f"bwo{g}", lin2(I["w_out_2"], r, 512 * g), l)

                def up_b(g):
                    w2 = I["w_up_2"]
                    return up(w2, lambda u, g: w2[ds(r + u * 256, 256), ds(g * 256 + FF, 256)], r, g)

                with sp.Fori(0, 5) as i:
                    load("bupa", up_b(i * 2), l, i)
                    load("bupb", up_b(i * 2 + 1), l, i)
                load("bupc", up_b(NG - 1), l)
                for g in range(2):
                    load(f"bdn{g}", lin2(I["w_down_2"], l * FF, 512 * g), l)

            rows = out.rearrange("(b p) d -> p b d", p=P)
            for g in range(2):
                read_out(sp, f"cout{g}")
                sp.dma_start(rows[:, :, 512 * g:512 * g + 512], o_out[:, :, 512 * g:512 * g + 512])\
                  .then_inc(S["stored"], 16)
            sp.wait_ge(S["stored"], 32)

        @block.tensor
        def _(pe):
            def fill(name, l=0, i=0):
                h, n = jobs.half[name], jobs.nth(name, l, i)
                if not isinstance(n, int) or n > 0:
                    pe.wait_ge(drained[h], n)
                return ps[h]

            def linear(name, act, l=0, i=0, n=T, tokens=None, cols=512):
                o = fill(name, l, i)
                units = ring.units[name]
                for u in range(units):
                    s = ring.slot[(name, u)]
                    pe.wait_ge(landed[s], ring.at(ring.landed, name, u, l, i))
                    for j in range(tokens or 4):
                        for kk in range(2):
                            k = 2 * u + kk
                            if tokens:
                                dst, lhsT, rhs = o[:, j * T:j * T + cols], act(k)[:, j * P:j * P + P], slot[:, s, kk, 0:cols]
                            else:
                                dst, lhsT, rhs = o[:, j * T:j * T + n], slot[:, s, kk, j * P:j * P + P], act(k)
                            mm = pe.matmul(dst, lhsT, rhs, start=(k == 0), stop=(k == 2 * units - 1))
                    mm.then_inc(weights_used, 1)

            def chunk(buf):
                return lambda k: buf[:, k, :]

            def square_sum(name, src, l=0, n=T):
                o = fill(name, l)
                pe.wait_ge(S["squared"], nth_norm(name, l))
                for k in range(KD):
                    mm = pe.matmul(o[:, 0:n], ones, src[:, k, :], start=(k == 0), stop=(k == KD - 1))
                mm.then_inc(S["summed"], 1)

            pe.sem_inc(S["s5_out"], PRIMED)
            pe.wait_ge(S["consts_loaded"], 16)
            pe.wait_ge(S["vecs_loaded"], 16 * 7)
            o = fill("avecs")
            pe.transpose(o[:, 0:V_ROWS], vrow[0:V_ROWS, 0, :], ident[0:V_ROWS, 0:V_ROWS]).then_inc(S["vecs_turned"], 1)
            pe.wait_ge(S["x_loaded"], 16)
            for g in range(2):
                o = fill(f"ax{g}")
                for c in range(4):
                    for b in range(NB):
                        mm = pe.transpose(o[:, c * T + b * P:c * T + b * P + P],
                                          x_in[:, b, (4 * g + c) * P:(4 * g + c + 1) * P], ident)
                mm.then_inc(S["x_turned"], 1)
            pe.wait_ge(S["mem_loaded"], 16)
            o = fill("amemT")
            for c in range(KD):
                for b in range(2):
                    mm = pe.transpose(o[:, c * M + b * P:c * M + b * P + P], mem_in[:, b, c * P:c * P + P], ident)
            mm.then_inc(S["mem_turned"], 1)
            square_sum("ass_mem", A(8192, KD, M), n=M)
            square_sum("ass_mix", nT)
            pe.wait_ge(S["normed"], nth_norm("ass_mix"))
            linear("axa", chunk(nT))

            o = fill("as5col")
            pe.wait_ge(S["s5_params"], 1)
            for n in range(4):
                mm = pe.transpose(o[:, 32 * n:32 * n + 32], row[0:32, n, :], ident[0:32, 0:32])
            mm.then_inc(S["s5_turned"], 1)
            o = fill("as5B")
            pe.wait_ge(S["s5_bbar"], 1)
            for q in range(QUADS):
                for n in range(2):
                    mm = pe.transpose(o[:, (2 * q + n) * P:(2 * q + n + 1) * P], zb[n][:, 4 * q:4 * q + 4, :], ident)
            mm.then_inc(S["s5_turned"], 1)
            o = fill("as5C")
            pe.wait_ge(S["s5c_loaded"], 16 * 16)
            for q in range(QUADS):
                for n in range(2):
                    mm = pe.transpose(o[:, (2 * q + n) * P:(2 * q + n + 1) * P], cnat[n][:, q, :], ident)
            mm.then_inc(S["s5_turned"], 1)
            read_out(pe, "as5B")
            read_out(pe, "as5C")
            with pe.Fori(0, 4) as c:
                def drive(t):
                    d, j, p = t // 4, t % 4, t % 2
                    if j == 0:
                        pe.wait_ge(S["s5_staged"], c * 2 + d + 1)
                    if t >= 2:
                        pe.wait_ge(S["s5_rotated"], c * 8 + t - 1)
                    for n in range(2):
                        mm = pe.matmul(ps[0][:, (2 * p + n) * T:(2 * p + n + 1) * T],
                                       stg[32 * j:32 * j + 32, d, n * P:n * P + P], ust[32 * j:32 * j + 32, :],
                                       start=True, stop=True)
                    mm.then_inc(S["s5_driven"], 1)

                drive(0)
                drive(1)
                for t in range(8):
                    d, j, p = t // 4, t % 4, t % 2
                    pe.wait_ge(S["s5_back_dve"], c * 8 + t + 1)
                    pe.wait_ge(S["s5_back_pool"], PRIMED + c * 8 + t + 1)
                    if t == 0:
                        pe.wait_ge(S["s5_y_read"], PRIMED + c)
                    for n, kind in enumerate((2, 3, 4, 4)):
                        mm = pe.matmul(ps[1][32 * j:32 * j + 32, 0:T],
                                       stg[:, d, kind * P + 32 * j:kind * P + 32 * j + 32], prod[:, p, n, :],
                                       start=(d == 0 and n == 0), stop=(d == 1 and n == 3), skip_group_check=True)
                    mm.then_inc(S["s5_out"], 1)
                    if t < 6:
                        drive(t + 2)
            pe.wait_ge(S["s5_gelu"], 1)
            pe.wait_ge(S["s5_y_read"], PRIMED + 4)
            linear("aglu", chunk(yT))

            o = fill("awsT")
            pe.wait_ge(S["sgu_loaded"], 16 * 4)
            for h in range(H):
                mm = pe.transpose(o[:, h * P:h * P + P], wsn[:, h, :], ident)
            mm.then_inc(S["ws_turned"], 1)
            for g in range(2):
                linear(f"azu{g}", chunk(nT))
            for g in range(2):
                linear(f"azv{g}", chunk(nT), tokens=NB)
            pe.wait_ge(S["zv_normed"], 1)
            read_out(pe, "awsT")
            for g in range(2):
                o = fill(f"asv{g}")
                for h in range(4):
                    for b in range(NB):
                        mm = pe.matmul(o[:, h * T + b * P:h * T + b * P + P], zv[:, b, (4 * g + h) * P:(4 * g + h + 1) * P],
                                       wsT[:, 4 * g + h, :], start=True, stop=True)
                mm.then_inc(S["sv_done"], 1)
            with pe.Fori(0, 2) as c:
                linear("aga", chunk(nT), 0, c)
                pe.wait_ge(S["ya_ready"], 1)
                linear("apa", chunk(yT), 0, c)
                linear("agb", chunk(nT), 0, c)
                pe.wait_ge(S["yb_ready"], 2)
                linear("apb", chunk(zu), 0, c)
            pe.wait_ge(S["merged_a"], 2)
            for g in range(2):
                linear(f"awo{g}", chunk(merged_a))

            pe.wait_ge(S["normed"], nth_norm("ass_mem"))
            for g in range(2):
                linear(f"awk{g}", chunk(mT), n=M)
            for g in range(2):
                linear(f"awv{g}", chunk(mT), tokens=2)
            square_sum("ass_xa", nT)
            pe.wait_ge(S["normed"], nth_norm("ass_xa"))
            for g in range(2):
                linear(f"awq{g}", chunk(nT))
            read_out(pe, "awq0")
            read_out(pe, "awq1")

            def x_scores(h):
                o = fill(f"axs{h}")
                for b in range(NB):
                    for c in range(2):
                        mm = pe.matmul(o[:, b * M:b * M + M], xq[:, 2 * h + c, b * P:b * P + P], xk[:, 2 * h + c, :],
                                       start=(c == 0), stop=(c == 1))
                mm.then_inc(S["x_scores"], 1)

            def x_turn(h):
                pe.wait_ge(S["x_probs"], h + 1)
                o = fill(f"axt{h}")
                for m in range(2):
                    for b in range(NB):
                        mm = pe.transpose(o[:, m * T + b * P:m * T + b * P + P], xp[:, h % 2, b, m * P:m * P + P], ident)
                mm.then_inc(S["x_probs_turned"], 1)

            def x_out(h):
                read_out(pe, f"axt{h}")
                o = fill(f"axv{h}")
                for c in range(2):
                    for m in range(2):
                        mm = pe.matmul(o[:, c * T:c * T + T], xv[:, m, (2 * h + c) * P:(2 * h + c + 1) * P],
                                       xpT[:, h % 2, m, :], start=(m == 0), stop=(m == 1))
                mm.then_inc(S["x_out"], 1)

            x_scores(0)
            x_scores(1)
            x_turn(0)
            x_scores(2)
            x_out(0)
            x_turn(1)
            x_scores(3)
            x_out(1)
            for h in (2, 3):
                x_turn(h)
                x_out(h)
            read_out(pe, "axv3")
            for g in range(2):
                linear(f"axo{g}", chunk(xo))
            square_sum("ass_ff", nT)
            pe.wait_ge(S["normed"], nth_norm("ass_ff"))
            with pe.Fori(0, 5) as i:
                linear("aupa", chunk(nT), 0, i)
                linear("aupb", chunk(nT), 0, i)
            linear("aupc", chunk(nT))
            read_out(pe, "aupc")
            read_out(pe, "aupb", 0, 4)
            for g in range(2):
                linear(f"adn{g}", chunk(ff))
            square_sum("ass_fin", nT)

            with pe.Fori(0, LAYERS) as l:
                o = fill("bvecs", l)
                pe.wait_ge(S["layer_vecs_loaded"], l * (16 * 8) + 16 * 8)
                pe.transpose(o[:, 0:W_ROWS1], vrow[0:W_ROWS1, 0, :], ident[0:W_ROWS1, 0:W_ROWS1])
                pe.transpose(o[:, W_ROWS1:W_ROWS1 + W_ROWS2], vrow[0:W_ROWS2, 1, :], ident[0:W_ROWS2, 0:W_ROWS2])\
                  .then_inc(S["layer_vecs_turned"], 1)
                square_sum("bss_at", nT, l)
                pe.wait_ge(S["normed"], nth_norm("bss_at", l))
                linear("bmix1", chunk(nT), l)
                linear("bmix2", chunk(nT), l, tokens=NB, cols=MIX2)
                pe.wait_ge(S["roped"], PRIMED + l * 5 + 1)
                pe.wait_ge(S["kk_copied"], l * 2 + 1)
                for b in range(1, NB):
                    o = fill(f"bix{b}", l)
                    n = (b + 1) * P
                    for h in range(4):
                        r0 = HD * (h % 2)
                        mm = pe.matmul(o[:, h * T:h * T + n], mix1[r0:r0 + HD, h // 2, b * P:b * P + P],
                                       kII[r0:r0 + HD, 0:n], start=True, stop=True)
                    mm.then_inc(S["index_dots"], 1)
                for name in ("bqB", "bqA", "bkA"):
                    linear(name, chunk(nT), l)
                o = fill("blf", l)
                read_out(pe, "bmix2", l)
                for b in range(NB):
                    mm = pe.transpose(o[0:H, b * P:b * P + P], mix2[:, b, MF:MF + H], ident)
                mm.then_inc(S["forget_turned"], 1)
                linear("bvA", chunk(nT), l, tokens=NB)
                o = fill("bft", l)
                pe.wait_ge(S["forget_sum"], l + 1)
                for b in range(NB):
                    if b == 0:
                        plain(pe)
                    mm = pe.transpose(o[:, b * H:b * H + H], fF[0:H, b * P:b * P + P], ident[0:H, 0:H])
                mm.then_inc(S["forget_turned"], 1)
                for g in range(2):
                    o = fill(f"bfb{g}", l)
                    for h in range(4):
                        mm = pe.matmul(o[:, h * T:h * T + T], onehot[0:H, 4 * g + h, :], fF[0:H, :], start=True, stop=True)
                    mm.then_inc(S["forget_spread"], 1)

                def attend(br, blocks, keys, values, after):
                    for name in after:
                        pe.wait_ge(drained[jobs.half[name[0]]], jobs.nth(name[0], l, name[1]))

                    def scores(i, p):
                        h = i * 2 + p
                        pe.wait_ge(S["heads_staged"], nth_head(br, l) + h + 1)
                        pe.wait_ge(S["heads_scores_read"], PRIMED + nth_head(br, l) + h)
                        for b, k0, n, at, _ in blocks:
                            mm = pe.matmul(ps[0][:, at:at + n], qz[:, p, b * P:b * P + P], keys(i, k0, n),
                                           start=True, stop=True)
                        mm.then_inc(S["heads_scores"], 1)

                    turned = turned_blocks(blocks)

                    def head(i, p, last):
                        h = i * 2 + p
                        pe.wait_ge(S["heads_probs"], nth_soft(br, l) + h + 1)
                        pe.wait_ge(S["heads_out_read"], PRIMED + nth_head(br, l) + h)
                        for n, (j, b, k0, at) in enumerate(turned):
                            mm = pe.transpose(ps[1][:, n * P:n * P + P],
                                              logit[:, p, at + j * P - k0:at + j * P - k0 + P], ident)
                        mm.then_inc(S["heads_turned"], 1)
                        if not last:
                            scores(i + 1, p)
                        pe.wait_ge(S["heads_turned_read"], nth_soft(br, l) + h + 1)
                        for b in range(NB):
                            mine = [(n, j) for n, (j, bb, _, _) in enumerate(turned) if bb == b]
                            for n, j in mine:
                                mm = pe.matmul(ps[1][:, 3 * T + b * HD:3 * T + b * HD + HD], probT[:, n * P:n * P + P],
                                               values(j, i, p), start=(n == mine[0][0]), stop=(n == mine[-1][0]))
                        mm.then_inc(S["heads_out"], 1)

                    scores(0, 0)
                    scores(0, 1)
                    with pe.Fori(0, 3) as i:
                        head(i, 0, False)
                        head(i, 1, False)
                    head(3, 0, True)
                    head(3, 1, True)
                    pe.wait_ge(S["heads_out_read"], PRIMED + nth_head(br, l) + H)

                def turn_out(name):
                    o = fill(name, l)
                    for c in range(NB):
                        for b in range(NB):
                            mm = pe.transpose(o[:, c * T + b * P:c * T + b * P + P], otm[:, b, c * P:c * P + P], ident)
                    mm.then_inc(S["y_turned"], 1)

                attend("fox", causal, lambda i, k0, n: K[:, ds(i, 1), k0:k0 + n].rearrange("p a b -> p (a b)"),
                       lambda j, i, p: V[:, j, ds(i * P + p * HD, HD)], (("btA", 0), ("btB", 0)))
                turn_out("btA")
                attend("dsa", causal, lambda i, k0, n: kBB[:, k0:k0 + n],
                       lambda j, i, p: mix2[:, j, MVB:MVB + HD], (("btB", 0), ("bqC", 0)))
                turn_out("btB")
                for name in ("bqC", "bkC"):
                    linear(name, chunk(nT), l)
                linear("bvC", chunk(nT), l, tokens=NB)
                linear("bgC", chunk(nT), l)

                for name in ("btC", "bqD"):
                    pe.wait_ge(drained[jobs.half[name]], jobs.nth(name, l))
                pe.wait_ge(S["roped"], PRIMED + l * 5 + 4)
                read_out(pe, "bvC", l)

                def ret_scores(i, p):
                    h = i * 2 + p
                    pe.wait_ge(S["heads_staged"], nth_head("ret", l) + h + 1)
                    pe.wait_ge(S["heads_scores_read"], PRIMED + nth_head("ret", l) + h)
                    for j, n, at, _ in forward:
                        mm = pe.matmul(ps[0][:, at:at + n], qz[:, p, j * P:j * P + P],
                                       Q[:, ds(i, 1), j * P:T].rearrange("p a b -> p (a b)"), start=True, stop=True)
                    mm.then_inc(S["heads_scores"], 1)

                def ret_out(i, p):
                    h = i * 2 + p
                    pe.wait_ge(S["heads_scores_read"], PRIMED + nth_head("ret", l) + h + 1)
                    pe.wait_ge(S["heads_out_read"], PRIMED + nth_head("ret", l) + h)
                    for b in range(NB):
                        for j in range(b + 1):
                            at = forward[j][3] + (b - j) * P
                            mm = pe.matmul(ps[1][:, 3 * T + b * HD:3 * T + b * HD + HD], logit[:, p, at:at + P],
                                           V[:, j, ds(i * P + p * HD, HD)], start=(j == 0), stop=(j == b))
                    mm.then_inc(S["heads_out"], 1)

                ret_scores(0, 0)
                with pe.Fori(0, 3) as i:
                    ret_scores(i, 1)
                    ret_out(i, 0)
                    ret_scores(i + 1, 0)
                    ret_out(i, 1)
                ret_scores(3, 1)
                ret_out(3, 0)
                ret_out(3, 1)
                pe.wait_ge(S["group_normed"], l + 1)
                turn_out("btC")
                linear("bqD", chunk(nT), l)
                pe.wait_ge(S["kk_copied"], l * 2 + 2)
                attend("swa", window, lambda i, k0, n: kDD[:, ds(i // 2, 1), k0:k0 + n].rearrange("p a b -> p (a b)"),
                       lambda j, i, p: mix2[:, j, ds(i // 2 * HD + MVD, HD)], (("btD", 0), ("bgt0", 0)))
                turn_out("btD")
                with pe.Fori(0, 2) as c:
                    for n, y in enumerate((yA, qB, gC, qD)):
                        linear(f"bgt{n}", chunk(nT), l, c)
                        linear(f"bbr{n}", chunk(y), l, c)
                pe.wait_ge(S["merged_b"], PRIMED + l * 6 + 6)
                for g in range(2):
                    linear(f"bwo{g}", chunk(merged_b), l)
                square_sum("bss_ff", nT, l)
                pe.wait_ge(S["normed"], nth_norm("bss_ff", l))
                plain(pe)
                with pe.Fori(0, 5) as i:
                    linear("bupa", chunk(nT), l, i)
                    linear("bupb", chunk(nT), l, i)
                linear("bupc", chunk(nT), l)
                pe.wait_ge(S["ff_ready"], l * NG + NG)
                for g in range(2):
                    linear(f"bdn{g}", chunk(ff), l)
            square_sum("css_fin", nT)
            pe.wait_ge(S["normed"], nth_norm("css_fin"))
            for g in range(2):
                o = fill(f"cout{g}")
                for b in range(NB):
                    for c in range(4):
                        mm = pe.transpose(o[:, b * T + c * P:b * T + c * P + P], hT[:, 4 * g + c, b * P:b * P + P], ident)
                mm.then_inc(S["out_turned"], 1)

        @block.scalar
        def _(act):
            link = Chain(act, S["act_step"])
            act.dma_start(consts[:, :], I["consts"][:, 0:N_CONSTS]).then_inc(S["consts_loaded"], 16)
            for at, key in ((V_MIX, "mix_norm_g"), (V_MEM, "mem_norm_g"), (V_XA, "xattn_norm_g"), (V_FF, "ffn_norm_g"),
                            (V_FIN, "final_norm_g"), (V_FIN2, "final_norm_2"), (V_D, "s5_d")):
                n = I[key].shape[-1] // P
                act.dma_start(vrow[at:at + n, 0, :], I[key].rearrange("(r p) -> r p", p=P)).then_inc(S["vecs_loaded"], 16)
            act.dma_start(row[0:32, 4, :], I["s5_lam_re"]).then_inc(S["s5_loaded"], 16)
            act.dma_start(row[0:32, 5, :], I["s5_lam_im"]).then_inc(S["s5_loaded"], 16)
            act.dma_start(row[0:32, 6, 0:2], I["s5_log_step"]).then_inc(S["s5_loaded"], 16)
            act.dma_start(mem_in, I["mem"].rearrange("(b p) d -> p b d", p=P)).then_inc(S["mem_loaded"], 16)

            def evac(dst, src, h, func=ACT.Copy, **kw):
                act.activation(dst, src, func, **kw).then_inc(drained[h], 1)

            def square(name, src, dst, l=0):
                act.activation(dst, src, ACT.Square).then_inc(S["squared"], 1)

            def root(name, l=0, n=T):
                act.wait_ge(S["summed"], nth_norm(name, l))
                evac(rms[:, 0:n], ps[jobs.half[name]][:, 0:n], jobs.half[name], ACT.Sqrt, bias=eps, scale=1.0 / D)

            act.wait_ge(S["vecs_turned"], 1)
            evac(vec0[:, :], ps[jobs.half["avecs"]][:, 0:V_ROWS], jobs.half["avecs"])
            for g in range(2):
                act.wait_ge(S["x_turned"], g + 1)
                evac(hT[:, 4 * g:4 * g + 4, :], banks(jobs.half[f"ax{g}"]), jobs.half[f"ax{g}"])
            act.wait_ge(S["mem_turned"], 1)
            h = jobs.half["amemT"]
            evac(mT, ps[h][:, :].rearrange("p (c m) -> p c m", m=M), h)
            read_out(act, "amemT")
            square("ass_mem", mT, A(8192, KD, M))
            read_out(act, "ax0")
            read_out(act, "ax1")
            square("ass_mix", hT[:, :, :], nT[:, :, :])
            act.wait_ge(S["constants_set"], 2)
            root("ass_mem", n=M)
            act.wait_ge(S["normed"], nth_norm("ass_mem"))
            root("ass_mix")

            R = [row[0:32, n, :] for n in range(24)]
            act.wait_ge(S["s5_loaded"], 48)
            act.activation(row[0:32, 7, 0:2], row[0:32, 6, 0:2], ACT.Exp).then_inc(S["s5_step"], 1)
            act.wait_ge(S["s5_exponent"], 1)
            act.activation(R[0], R[10], ACT.Exp).then_inc(S["s5_magnitude"], 1)
            act.wait_ge(S["s5_phase"], 1)
            link(act.activation(R[11], R[1], ACT.Abs))
            act.activation(R[12], R[1], ACT.Sin, scale=TWO_PI).then_inc(S["s5_circle"], 1)
            act.activation(R[13], R[11], ACT.Sin, bias=half_pi[0:32, :], scale=-TWO_PI).then_inc(S["s5_circle"], 1)
            done(act, "axa")
            evac(uT, banks(jobs.half["axa"]), jobs.half["axa"])
            act.wait_ge(S["s5_turned"], 1)
            h = jobs.half["as5col"]
            link(act.activation(s5col[:, :, :], ps[h][:, 0:4 * 32].rearrange("p (a b) -> p a b", b=32), ACT.Copy))
            evac(s5col[:, 1, 16:32], ps[h][:, 32 + 16:64], h, scale=-1.0)
            act.wait_ge(S["s5_turned"], 2)
            h = jobs.half["as5B"]
            evac(s5w[:, :, 0:2, :], ps[h][:, :].rearrange("p (q k s) -> p q k s", q=QUADS, k=2), h)
            act.wait_ge(S["s5_turned"], 3)
            h = jobs.half["as5C"]
            c_re, c_im = (ps[h][:, :].rearrange("p (q k s) -> p q k s", q=QUADS, k=2)[:, :, k, :] for k in range(2))
            act.activation(s5w[:, :, 2, :], c_re, ACT.Copy)
            act.activation(s5w[:, :, 3, :], c_re, ACT.Copy, scale=-1.0)
            evac(s5w[:, :, 4, :], c_im, h, scale=-1.0)
            read_out(act, "axa")
            read_out(act, "as5B")
            read_out(act, "as5C")
            read_out(act, "as5col")
            act.wait_ge(S["s5_bbar"], 1)
            act.wait_ge(S["iota_loaded"], 16)
            with act.Fori(0, 4) as c:
                act.wait_ge(S["s5_out"], PRIMED + c * 8)
                act.activation(ust, uT[:, ds(c, 1), :].rearrange("p a b -> p (a b)"), ACT.Copy)
                for d in range(2):
                    act.activation(stg[:, d, :], s5w[:, ds(c + 4 * d, 1), :, :].rearrange("p q a b -> p (q a b)"), ACT.Copy)\
                        .then_inc(S["s5_staged"], 1)

                def turns(t):
                    act.activation(turn[:, t % 2, :], rms[:, :], ACT.Copy, scale=s5col[:, 1, ds(c * 4 + (t // 4 * 16 + t % 4), 1)])\
                        .then_inc(S["s5_turns"], 1)

                turns(0)
                turns(1)
                for t in range(8):
                    p = t % 2
                    act.wait_ge(S["s5_fraction"], c * 8 + t + 1)
                    act.activation(whole[:, p, :], turn[:, p, :], ACT.Abs).then_inc(S["s5_abs"], 1)
                    if t >= 4:
                        act.wait_ge(S["s5_back_dve"], c * 8 + t - 3)
                        act.wait_ge(S["s5_back_pool"], PRIMED + c * 8 + t - 3)
                    act.activation(trig[:, t % 4, 1, :], turn[:, p, :], ACT.Sin, scale=TWO_PI)
                    act.wait_ge(S["s5_abs"], c * 8 + t + 1)
                    act.activation(trig[:, t % 4, 0, :], whole[:, p, :], ACT.Sin, bias=half_pi, scale=-TWO_PI)\
                        .then_inc(S["s5_trig"], 1)
                    if t < 6:
                        act.wait_ge(S["s5_trig"], c * 8 + t + 1)
                        turns(t + 2)
            act.wait_ge(S["s5_y_read"], PRIMED + 4)
            act.activation(yT, yT, ACT.Gelu_apprx_tanh).then_inc(S["s5_gelu"], 1)
            done(act, "aglu")
            evac(svt, banks(jobs.half["aglu"]), jobs.half["aglu"], ACT.Sigmoid)

            act.wait_ge(S["ws_turned"], 1)
            h = jobs.half["awsT"]
            evac(wsT, ps[h][:, 0:H * P].rearrange("p (a b) -> p a b", b=P), h)
            for g in range(2):
                done(act, f"azu{g}")
                h = jobs.half[f"azu{g}"]
                evac(zu[:, 4 * g:4 * g + 4, :], banks(h), h, ACT.Gelu_apprx_tanh)
            for g in range(2):
                done(act, f"azv{g}")
                h = jobs.half[f"azv{g}"]
                evac(zv[:, :, 512 * g:512 * g + 512], banks(h), h, ACT.Gelu_apprx_tanh)
            act.wait_ge(S["zv_stats"], 1)
            act.activation(stat[:, 56:60], stat[:, 48:56].rearrange("p (a b) -> p a b", b=2)[:, :, 1], ACT.Sqrt, bias=eps)\
                .then_inc(S["zv_std"], 1)
            with act.Fori(0, 2) as c:
                for n, key in enumerate(("ga", "gb")):
                    done(act, "a" + key, 0, c)
                    act.wait_ge(drained[jobs.half["apa"]], jobs.nth("apa", 0, c) + (n - 1))
                    h = jobs.half["a" + key]
                    evac(gate_a[:, n, :, :], banks(h), h, ACT.Sigmoid)

            for g in range(2):
                done(act, f"awk{g}")
                h = jobs.half[f"awk{g}"]
                evac(xk[:, 4 * g:4 * g + 4, :], banks(h, w=M), h)
            for g in range(2):
                done(act, f"awv{g}")
                h = jobs.half[f"awv{g}"]
                evac(xv[:, :, 512 * g:512 * g + 512], banks(h, n=2), h)
            read_out(act, "awo0")
            read_out(act, "awo1")
            square("ass_xa", hT[:, :, :], nT[:, :, :])
            root("ass_xa")
            for g in range(2):
                done(act, f"awq{g}")
                h = jobs.half[f"awq{g}"]
                evac(xq[:, 4 * g:4 * g + 4, :], banks(h), h)

            def x_exp(h):
                act.wait_ge(S["x_max"], h + 1)
                p, half = h % 2, jobs.half[f"axs{h}"]
                for b in range(NB):
                    ins = act.activation(xp[:, p, b, :], ps[half][:, b * M:b * M + M], ACT.Exp, scale=float((D // 4) ** -0.5),
                                         bias=stat[:, 64 + 4 * p + b:65 + 4 * p + b], accum_out=stat[:, 72 + 4 * p + b:73 + 4 * p + b])
                ins.then_inc(drained[half], 1)

            def x_turned(h):
                act.wait_ge(S["x_probs_turned"], h + 1)
                evac(xpT[:, h % 2, :, :], banks(jobs.half[f"axt{h}"], n=2), jobs.half[f"axt{h}"])

            def x_outs(h):
                act.wait_ge(S["x_out"], h + 1)
                evac(xo[:, 2 * h:2 * h + 2, :], banks(jobs.half[f"axv{h}"], n=2), jobs.half[f"axv{h}"])

            x_exp(0)
            x_exp(1)
            x_turned(0)
            x_exp(2)
            x_outs(0)
            x_turned(1)
            x_exp(3)
            x_outs(1)
            for h in (2, 3):
                x_turned(h)
                x_outs(h)
            read_out(act, "axo0")
            read_out(act, "axo1")
            square("ass_ff", hT[:, :, :], nT[:, :, :])
            root("ass_ff")

            def silu_a(name, p, i=0):
                done(act, name, 0, i)
                act.activation(sg_a[:, p, :, :], banks(jobs.half[name], n=2), ACT.Silu).then_inc(S["silu_a"], 1)

            with act.Fori(0, 5) as i:
                silu_a("aupa", 0, i)
                silu_a("aupb", 1, i)
            silu_a("aupc", 0)
            read_out(act, "adn0")
            read_out(act, "adn1")
            square("ass_fin", hT[:, :, :], nT[:, :, :])
            root("ass_fin")
            act.wait_ge(S["normed"], nth_norm("ass_fin"))

            with act.Fori(0, LAYERS) as l:
                act.wait_ge(S["layer_vecs_turned"], l + 1)
                h = jobs.half["bvecs"]
                evac(vec[:, :], ps[h][:, 0:W_ROWS1 + W_ROWS2], h)
                last = "bdn1"
                act.wait_ge(drained[jobs.half[last]], jobs.nth(last, l) - (jobs.nth(last, 1) - jobs.nth(last, 0)) + 1)
                square("bss_at", hT[:, :, :], nT[:, :, :])
                root("bss_at", l)

                def rope_read(name, dst, turn_no):
                    done(act, name, l)
                    act.wait_ge(S["roped"], PRIMED + l * 5 + turn_no)
                    h = jobs.half[name]
                    act.activation(dst, banks(h), ACT.Copy)
                    for r in range(0, P, 32):
                        ins = act.activation(part[r:r + 32, :, :], banks(h)[r ^ 32:(r ^ 32) + 32, :, :], ACT.Copy)
                    ins.then_inc(drained[h], 1)

                rope_read("bmix1", mix1, 0)
                done(act, "bmix2", l)
                h = jobs.half["bmix2"]
                evac(mix2, banks(h, w=MIX2), h)
                act.wait_ge(S["roped"], PRIMED + l * 5 + 1)
                for r in (0, HD):
                    act.activation(kBB[r:r + HD, :], mix1[0:HD, 2, :], ACT.Copy)
                    ins = act.activation(kII[r:r + HD, :], mix1[HD:P, 2, :], ACT.Copy)
                ins.then_inc(S["kk_copied"], 1)
                for b in range(1, NB):
                    act.wait_ge(S["index_dots"], l * 3 + b)
                    act.wait_ge(S["index_scored"], PRIMED + l * 3 + b - 1)
                    h = jobs.half[f"bix{b}"]
                    evac(relu[:, :, 0:(b + 1) * P], banks(h, w=(b + 1) * P), h, ACT.Relu)
                rope_read("bqB", qB, 1)
                for name, dst in (("bqA", Q), ("bkA", K)):
                    done(act, name, l)
                    evac(dst, banks(jobs.half[name]), jobs.half[name])
                act.wait_ge(S["forget_turned"], l * 2 + 1)
                h = jobs.half["blf"]
                evac(fx[0:H, :], ps[h][0:H, 0:T], h, ACT.Identity, bias=fbias[0:H, :])
                read_out(act, "blf", l)
                steps = Chain(act, S["forget_step"], l * 2)
                steps(act.activation(fe[0:H, :], fx[0:H, :], ACT.Abs))
                steps(act.activation(fe[0:H, :], fe[0:H, :], ACT.Exp, scale=-1.0))
                act.activation(fe[0:H, :], fe[0:H, :], ACT.Ln, bias=ones[0:H, 0:1]).then_inc(S["forget_log"], 1)
                done(act, "bvA", l)
                evac(V, banks(jobs.half["bvA"]), jobs.half["bvA"])
                act.wait_ge(S["forget_turned"], l * 2 + 2)
                h = jobs.half["bft"]
                evac(ftm[:, :, :], ps[h][:, 0:NB * H].rearrange("p (b h) -> p b h", h=H), h)
                for g in range(2):
                    act.wait_ge(S["forget_spread"], l * 2 + g + 1)
                    h = jobs.half[f"bfb{g}"]
                    evac(fb[:, 4 * g:4 * g + 4, :], banks(h), h)

                def stage(br, src, i, p, scale=HD ** -0.5):
                    act.activation(qz[HD * p:HD * p + HD, p, :], src[HD * p:HD * p + HD, ds(i, 1), :]
                                   .rearrange("p a b -> p (a b)"), ACT.Copy, scale=scale).then_inc(S["heads_staged"], 1)

                def attend(br, blocks, src, sinks=False):
                    def exps(i, p):
                        h = i * 2 + p
                        act.wait_ge(S["heads_scores_read"], PRIMED + nth_head(br, l) + h + 1)
                        if sinks:
                            act.activation(stat[:, 88 + 4 * p:92 + 4 * p], stat[:, 64 + 4 * p:68 + 4 * p], ACT.Exp,
                                           bias=sink[:, ds(h, 1)])
                        for b, _, n, _, at in blocks:
                            ins = act.activation(logit[:, p, at:at + n], logit[:, p, at:at + n], ACT.Exp,
                                                 bias=stat[:, 64 + 4 * p + b:65 + 4 * p + b],
                                                 accum_out=stat[:, 72 + 4 * p + b:73 + 4 * p + b])
                        ins.then_inc(S["heads_probs"], 1)

                    n = len(turned_blocks(blocks)) * P

                    def head(i, p, last):
                        h = i * 2 + p
                        if not last:
                            act.wait_ge(S["heads_scores"], nth_head(br, l) + h + 1)
                            stage(br, src, i + 1, p)
                        act.wait_ge(S["heads_turned"], nth_soft(br, l) + h + 1)
                        act.activation(probT[:, 0:n], ps[1][:, 0:n], ACT.Copy).then_inc(S["heads_turned_read"], 1)
                        if p == 0:
                            exps(i, 1)
                        elif not last:
                            exps(i + 1, 0)

                    stage(br, src, 0, 0)
                    stage(br, src, 0, 1)
                    exps(0, 0)
                    with act.Fori(0, 3) as i:
                        head(i, 0, False)
                        head(i, 1, False)
                    head(3, 0, True)
                    head(3, 1, True)

                def turn_out(name, k, dst):
                    act.wait_ge(S["y_turned"], l * 4 + k)
                    evac(dst, banks(jobs.half[name]), jobs.half[name])

                read_out(act, "bqA", l)
                attend("fox", causal, Q)
                turn_out("btA", 1, yA)
                act.wait_ge(S["roped"], PRIMED + l * 5 + 2)
                attend("dsa", causal, qB)
                turn_out("btB", 2, qB)
                rope_read("bqC", Q, 2)
                rope_read("bkC", K, 3)
                done(act, "bvC", l)
                evac(V, banks(jobs.half["bvC"]), jobs.half["bvC"])
                done(act, "bgC", l)
                evac(gC, banks(jobs.half["bgC"]), jobs.half["bgC"], ACT.Silu)

                def ret_stage(i, p):
                    h = i * 2 + p
                    stage("ret", K, i, p)
                    act.activation(decay[:, p, :], C["dist"], ACT.Exp, scale=C["logdecay"][:, ds(h, 1)])\
                        .then_inc(S["ret_decay"], 1)

                def ret_head(i, p, last):
                    h = i * 2 + p
                    if not last:
                        act.wait_ge(S["heads_scores"], nth_head("ret", l) + h + 1)
                        act.wait_ge(S["heads_scores_read"], PRIMED + nth_head("ret", l) + h + 1)
                        ret_stage(i + 1, p)
                    act.wait_ge(S["heads_out"], nth_head("ret", l) + h + 1)
                    act.activation(otm[:, :, ds(i * P + p * HD, HD)], ps[1][:, 3 * T:3 * T + NB * HD]
                                   .rearrange("p (b d) -> p b d", d=HD), ACT.Copy).then_inc(S["heads_out_read"], 1)

                act.wait_ge(S["roped"], PRIMED + l * 5 + 4)
                ret_stage(0, 0)
                ret_stage(0, 1)
                with act.Fori(0, 3) as i:
                    ret_head(i, 0, False)
                    ret_head(i, 1, False)
                ret_head(3, 0, True)
                ret_head(3, 1, True)
                act.wait_ge(S["group_centred"], l + 1)
                act.activation(gsq, otm, ACT.Square).then_inc(S["group_squared"], 1)
                act.wait_ge(S["group_var"], l + 1)
                act.activation(stat[:, 0:32], stat[:, 32:64], ACT.Sqrt, bias=eps, scale=1.0 / HD).then_inc(S["group_std"], 1)
                rope_read("bqD", qD, 4)
                for g in range(2):
                    for r in (0, HD):
                        ins = act.activation(kDD[r:r + HD, g, :], mix1[HD * g:HD * g + HD, 3, :], ACT.Copy)
                ins.then_inc(S["kk_copied"], 1)
                act.wait_ge(S["roped"], PRIMED + l * 5 + 5)
                attend("swa", window, qD, sinks=True)
                turn_out("btD", 4, qD)

                with act.Fori(0, 2) as c:
                    for n in range(4):
                        done(act, f"bgt{n}", l, c)
                        act.wait_ge(drained[jobs.half["bbr0"]], jobs.nth("bbr0", l, c) + (n - 1))
                        h = jobs.half[f"bgt{n}"]
                        evac(gate_b[:, n % 2, :, :], banks(h), h, ACT.Sigmoid)
                read_out(act, "bwo0", l)
                read_out(act, "bwo1", l)
                square("bss_ff", hT[:, :, :], nT[:, :, :])
                root("bss_ff", l)

                def conv_group(name, g, p, i=0):
                    done(act, name, l, i)
                    h = jobs.half[name]
                    for j in range(4):
                        ch = g * 2 + (j if j < 2 else NF + j - 2)
                        ins = act.activation(conv[:, p, j, :], ps[h][:, j * T:j * T + T], ACT.Identity,
                                             scale=vec[:, ds(ch + W_C2, 1)], bias=vec[:, ds(ch + W_CB, 1)])
                    ins.then_inc(S["conv_begun"], 1)
                    read_out(act, name, l, i)
                    act.activation(sg_b[:, p, :, :], conv[:, p, 0:2, :], ACT.Silu).then_inc(S["silu_b"], 1)

                with act.Fori(0, 5) as i:
                    conv_group("bupa", i * 2, 0, i)
                    conv_group("bupb", i * 2 + 1, 1, i)
                conv_group("bupc", NG - 1, 0)
            read_out(act, "bdn0", LAYERS - 1)
            read_out(act, "bdn1", LAYERS - 1)
            square("css_fin", hT[:, :, :], nT[:, :, :])
            root("css_fin")
            for g in range(2):
                act.wait_ge(S["out_turned"], g + 1)
                h = jobs.half[f"cout{g}"]
                evac(o_out[:, :, 512 * g:512 * g + 512], banks(h), h)

        @block.vector
        def _(dve):
            link = Chain(dve, S["dve_step"])
            for name in ("heads_scores_read", "heads_out_read", "s5_y_read", "roped", "index_scored", "merged_b"):
                dve.sem_inc(S[name], PRIMED)
            dve.memset(eps, EPS).then_inc(S["constants_set"], 1)
            dve.memset(half_pi, float(np.pi / 2)).then_inc(S["constants_set"], 1)

            def norm(name, src, dst, gains, l=0, n=T):
                read_out(dve, name, l)
                dve.reciprocal(rms[:, 0:n], rms[:, 0:n]).then_inc(S["rstd"], 1)
                dve.wait_ge(S["rstd"], nth_norm(name, l))
                for k in range(KD):
                    ins = dve.scalar_tensor_tensor(out=dst[:, k, :], in0=src[:, k, :], scalar=gains[:, k:k + 1],
                                                   in1=rms[:, 0:n], op0=ALU.mult, op1=ALU.mult)
                ins.then_inc(S["normed"], 1)

            def add_back(name, g, l=0):
                done(dve, name, l)
                h = jobs.half[name]
                dve.tensor_tensor(hT[:, 4 * g:4 * g + 4, :], hT[:, 4 * g:4 * g + 4, :], banks(h), ALU.add)\
                   .then_inc(drained[h], 1)

            def wide(v, n):
                return v.unsqueeze(2).to_broadcast([v.shape[0], v.shape[1], n])

            read_out(dve, "avecs")
            norm("ass_mem", mT, mT, vec0[:, V_MEM:V_MEM + KD], n=M)
            norm("ass_mix", hT, nT, vec0[:, V_MIX:V_MIX + KD])

            R = [row[0:32, n, :] for n in range(24)]
            lre, lim, lr, theta, k, r, sin, cos, nr, li, den, t1, t2 = (R[n] for n in (4, 5, 10, 8, 9, 1, 12, 13, 14, 15, 16, 17, 18))
            step = row[0:32, 7, 0:2].unsqueeze(2).to_broadcast([32, 2, STATE])

            def halves(v):
                return v.rearrange("p (g s) -> p g s", s=STATE)

            dve.wait_ge(S["s5_loaded"], 48)
            dve.wait_ge(S["s5_step"], 1)
            dve.tensor_tensor(halves(lr), halves(lre), step, ALU.mult).then_inc(S["s5_exponent"], 1)
            link(dve.tensor_tensor(halves(theta), halves(lim), step, ALU.mult))
            link(dve.tensor_scalar(k, theta, INV_2PI, ROUND, ALU.mult, ALU.add))
            link(dve.tensor_scalar(k, k, ROUND, None, ALU.subtract))
            link(dve.scalar_tensor_tensor(out=t1, in0=k, scalar=-C1, in1=theta, op0=ALU.mult, op1=ALU.add))
            link(dve.scalar_tensor_tensor(out=t2, in0=k, scalar=-C2, in1=t1, op0=ALU.mult, op1=ALU.add))
            dve.tensor_scalar(r, t2, INV_2PI, None, ALU.mult).then_inc(S["s5_phase"], 1)
            link(dve.tensor_tensor(t1, lre, lre, ALU.mult))
            link(dve.tensor_tensor(t2, lim, lim, ALU.mult))
            link(dve.tensor_tensor(den, t1, t2, ALU.add))
            link(dve.reciprocal(den, den))
            dve.wait_ge(S["s5_magnitude"], 1)
            dve.wait_ge(S["s5_circle"], 2)
            link(dve.tensor_tensor(nr, R[0], cos, ALU.mult))
            link(dve.tensor_scalar(nr, nr, 1.0, None, ALU.subtract))
            link(dve.tensor_tensor(li, R[0], sin, ALU.mult))
            link(dve.tensor_tensor(t1, nr, lre, ALU.mult))
            link(dve.tensor_tensor(t2, li, lim, ALU.mult))
            link(dve.tensor_tensor(t1, t1, t2, ALU.add))
            link(dve.tensor_tensor(R[2], t1, den, ALU.mult))
            link(dve.tensor_tensor(t1, li, lre, ALU.mult))
            link(dve.tensor_tensor(t2, nr, lim, ALU.mult))
            link(dve.tensor_tensor(t1, t1, t2, ALU.subtract))
            dve.tensor_tensor(R[3], t1, den, ALU.mult).then_inc(S["s5_params"], 1)
            read_out(dve, "as5col")
            dve.wait_ge(S["s5b_loaded"], 32)
            f_re, f_im = (wide(s5col[:, n, :], CHAN) for n in (2, 3))
            for n, (b, f) in enumerate(((0, f_re), (1, f_im), (1, f_re), (0, f_im))):
                link(dve.tensor_tensor(bprod[n], bnat[b], f, ALU.mult))
            dve.wait_ge(S["zeros_set"], 5)
            for g in range(2):
                at, ch = slice(STATE * g, STATE * g + STATE), slice(CHAN * g, CHAN * g + CHAN)
                dve.tensor_tensor(zb[0][at, :, ch], bprod[0][at], bprod[1][at], ALU.subtract)
                ins = dve.tensor_tensor(zb[1][at, :, ch], bprod[2][at], bprod[3][at], ALU.add)
            ins.then_inc(S["s5_bbar"], 1)

            read_out(dve, "as5C")
            read_out(dve, "axa")
            with dve.Fori(0, 4) as c:
                def nearest(t):
                    dve.wait_ge(S["s5_turns"], c * 8 + t + 1)
                    dve.tensor_scalar(whole[:, t % 2, :], turn[:, t % 2, :], ROUND, ROUND, ALU.add, ALU.subtract)\
                       .then_inc(S["s5_whole"], 1)

                def rotate(t):
                    p = t % 2
                    dve.wait_ge(S["s5_driven"], c * 8 + t + 1)
                    dve.wait_ge(S["s5_trig"], c * 8 + t + 1)
                    dve.wait_ge(S["s5_out"], PRIMED + c * 8 + (t - 1 if t >= 2 else 0))
                    for n, (b, f) in enumerate(((0, 0), (1, 1), (1, 0), (0, 1))):
                        ins = dve.tensor_tensor(prod[:, p, n, :], ps[0][:, (2 * p + b) * T:(2 * p + b + 1) * T],
                                                trig[:, t % 4, f, :], ALU.mult)
                    ins.then_inc(S["s5_rotated"], 1)

                def scan(t):
                    p, d = t % 2, t // 4
                    dve.wait_ge(S["s5_z"], c * 8 + t + 1)
                    dve.wait_ge(S["s5_back_pool"], PRIMED + c * 8 + (t - 1 if t >= 2 else 0))
                    decay_rate = s5col[:, 0, ds(c * 4 + (d * 16 + t % 4), 1)].to_broadcast([P, T])
                    for n in range(2):
                        o, z = st[:, p, n, :], zt[:, p, n, :]
                        if d:
                            o, z = o[:, ::-1], z[:, ::-1]
                        ins = dve.tensor_tensor_scan(o, decay_rate, z, 0.0, ALU.mult, ALU.add).then_inc(S["s5_scanned"], 1)
                    dve.wait_ge(S["s5_scanned"], c * 16 + 2 * t + 2)
                    for n in range(2):
                        ins = dve.tensor_tensor(prod[:, p, n, :], st[:, p, n, :], trig[:, t % 4, n, :], ALU.mult)
                    ins.then_inc(S["s5_back_dve"], 1)

                nearest(0)
                nearest(1)
                for t in range(8):
                    rotate(t)
                    if t < 6:
                        nearest(t + 2)
                    if t:
                        scan(t - 1)
                scan(7)
                dve.wait_ge(S["s5_out"], PRIMED + c * 8 + 8)
                dve.scalar_tensor_tensor(out=yT[:, ds(c, 1), :].rearrange("p a b -> p (a b)"),
                                         in0=uT[:, ds(c, 1), :].rearrange("p a b -> p (a b)"),
                                         scalar=vec0[:, ds(c + V_D, 1)], in1=ps[1][:, 0:T], op0=ALU.mult, op1=ALU.add)\
                   .then_inc(S["s5_y_read"], 1)
            read_out(dve, "aglu")
            dve.wait_ge(S["s5_gelu"], 1)
            dve.tensor_tensor(yT, yT, svt, ALU.mult).then_inc(S["ya_ready"], 1)

            read_out(dve, "azv0")
            read_out(dve, "azv1")
            for b in range(NB):
                for g in range(2):
                    link(dve.bn_stats(stat[:, (2 * b + g) * 6:(2 * b + g) * 6 + 6], zv[:, b, 512 * g:512 * g + 512]))
            for b in range(NB):
                ins = dve.bn_aggr(stat[:, 48 + 2 * b:50 + 2 * b], stat[:, 12 * b:12 * b + 12])
            ins.then_inc(S["zv_stats"], 1)
            dve.wait_ge(S["zv_std"], 1)
            link(dve.reciprocal(stat[:, 56:60], stat[:, 56:60]))
            for b in range(NB):
                link(dve.tensor_scalar(zv[:, b, :], zv[:, b, :], stat[:, 48 + 2 * b:49 + 2 * b], stat[:, 56 + b:57 + b],
                                       ALU.subtract, ALU.mult))
            dve.wait_ge(S["sgu_loaded"], 64)
            link(dve.tensor_tensor(zv, zv, lng.unsqueeze(1).to_broadcast([P, NB, D]), ALU.mult))
            dve.tensor_tensor(zv, zv, lnb.unsqueeze(1).to_broadcast([P, NB, D]), ALU.add).then_inc(S["zv_normed"], 1)
            read_out(dve, "azu0")
            read_out(dve, "azu1")
            for g in range(2):
                dve.wait_ge(S["sv_done"], g + 1)
                half = jobs.half[f"asv{g}"]
                for h in range(4):
                    ins = dve.tensor_tensor(svt[:, h, :].rearrange("p (b t) -> p b t", t=P),
                                            ps[half][:, h * T:h * T + T].rearrange("p (b t) -> p b t", t=P),
                                            sgub[:, 4 * g + h, :].unsqueeze(1).to_broadcast([P, NB, P]), ALU.add)
                ins.then_inc(drained[half], 1)
                read_out(dve, f"asv{g}")
                dve.tensor_tensor(zu[:, 4 * g:4 * g + 4, :], zu[:, 4 * g:4 * g + 4, :], svt, ALU.mult).then_inc(S["yb_ready"], 1)
                dve.wait_ge(S["yb_ready"], g + 1)

            with dve.Fori(0, 2) as c:
                read_out(dve, "aga", 0, c)
                done(dve, "apa", 0, c)
                h = jobs.half["apa"]
                dve.tensor_tensor(merged_a[:, ds(c * 4, 4), :], banks(h), gate_a[:, 0, :, :], ALU.mult).then_inc(drained[h], 1)
                read_out(dve, "agb", 0, c)
                done(dve, "apb", 0, c)
                h = jobs.half["apb"]
                dve.tensor_tensor(tmp_a, banks(h), gate_a[:, 1, :, :], ALU.mult).then_inc(drained[h], 1)
                read_out(dve, "apb", 0, c)
                dve.tensor_tensor(merged_a[:, ds(c * 4, 4), :], merged_a[:, ds(c * 4, 4), :], tmp_a, ALU.add)\
                   .then_inc(S["merged_a"], 1)
                dve.wait_ge(S["merged_a"], c + 1)
            for g in range(2):
                add_back(f"awo{g}", g)
            norm("ass_xa", hT, nT, vec0[:, V_XA:V_XA + KD])

            def x_max(h):
                half, p = jobs.half[f"axs{h}"], h % 2
                dve.wait_ge(S["x_scores"], h + 1)
                mx = stat[:, 64 + 4 * p:68 + 4 * p]
                link(dve.tensor_reduce(mx, ps[half][:, 0:NB * M].rearrange("p (b m) -> p b m", m=M), AXX, ALU.max))
                dve.tensor_scalar(mx, mx, -float((D // 4) ** -0.5), None, ALU.mult).then_inc(S["x_max"], 1)

            def x_norm(h):
                p = h % 2
                read_out(dve, f"axs{h}")
                link(dve.reciprocal(stat[:, 80 + 4 * p:84 + 4 * p], stat[:, 72 + 4 * p:76 + 4 * p]))
                dve.tensor_tensor(xp[:, p, :, :], xp[:, p, :, :], wide(stat[:, 80 + 4 * p:84 + 4 * p], M), ALU.mult)\
                   .then_inc(S["x_probs"], 1)

            x_max(0)
            x_max(1)
            for h in range(4):
                x_norm(h)
                if h < 2:
                    x_max(h + 2)
            for g in range(2):
                add_back(f"axo{g}", g)
            norm("ass_ff", hT, nT, vec0[:, V_FF:V_FF + KD])

            def gate_up(name, g, p, i=0):
                dve.wait_ge(S["silu_a"], g + 1)
                h = jobs.half[name]
                dve.tensor_tensor(ff[:, ds(g * 2, 2), :], sg_a[:, p, :, :], banks(h)[:, 2:4, :], ALU.mult).then_inc(drained[h], 1)

            with dve.Fori(0, 5) as i:
                gate_up("aupa", i * 2, 0, i)
                gate_up("aupb", i * 2 + 1, 1, i)
            gate_up("aupc", NG - 1, 0)
            for g in range(2):
                add_back(f"adn{g}", g)
            norm("ass_fin", hT, hT, vec0[:, V_FIN:V_FIN + KD])
            dve.wait_ge(S["normed"], nth_norm("ass_fin"))

            with dve.Fori(0, LAYERS) as l:
                read_out(dve, "bvecs", l)
                norm("bss_at", hT, nT, vec[:, W_AT:W_AT + KD], l)

                def rope(name, buf, n):
                    read_out(dve, name, l)
                    turned = Chain(dve, S["rope_step"], l * 10 + n * 2)
                    cos, sin = (C[x].unsqueeze(1).to_broadcast([P, NB, T]) for x in ("cos", "sin"))
                    turned(dve.tensor_tensor(buf, buf, cos, ALU.mult))
                    turned(dve.tensor_tensor(part, part, sin, ALU.mult))
                    dve.tensor_tensor(buf, buf, part, ALU.add).then_inc(S["roped"], 1)
                    dve.wait_ge(S["roped"], PRIMED + l * 5 + n + 1)

                rope("bmix1", mix1, 0)
                read_out(dve, "bmix2", l)
                wi = stat[:, 96:112].rearrange("p (b h) -> p b h", h=4)
                dve.tensor_scalar(wi, mix2[:, :, MW:MW + 4], float(4 ** -0.5 * 64 ** -0.5), None, ALU.mult)\
                   .then_inc(S["index_weights"], 1)
                dve.wait_ge(S["index_weights"], l + 1)
                steps = Chain(dve, S["index_step"], l * 12)
                for b in range(1, NB):
                    n = (b + 1) * P
                    read_out(dve, f"bix{b}", l)
                    steps(dve.tensor_scalar(score[b], relu[:, 0, 0:n], wi[:, b, 0:1], None, ALU.mult))
                    for h in range(1, 4):
                        steps(dve.scalar_tensor_tensor(out=score[b], in0=relu[:, h, 0:n], scalar=wi[:, b, h:h + 1],
                                                       in1=score[b], op0=ALU.mult, op1=ALU.add))
                    dve.tensor_tensor(score[b], score[b], C["cmask"][:, T - n:T], ALU.add).then_inc(S["index_scored"], 1)
                assert steps.n == 12
                dve.wait_ge(S["index_scored"], PRIMED + l * 3 + 3)
                plain(dve)
                with dve.Fori(0, TOPK // 8) as r:
                    taken = Chain(dve, S["topk_step"], l * (6 * TOPK // 8) + r * 6)
                    best = [None] + [stat[:, 112 + 8 * (b - 1):120 + 8 * (b - 1)] for b in range(1, NB)]
                    for b in range(1, NB):
                        plain(dve)
                        taken(dve.max(best[b], score[b]))
                    for b in range(1, NB):
                        plain(dve)
                        taken(dve.match_replace(score[b], best[b], score[b], GONE))
                dve.tensor_copy(selb[:, 0:P], C["cmask"][:, T - P:T])
                for b in range(1, NB):
                    at = causal[b][4]
                    ins = dve.tensor_scalar(selb[:, at:at + (b + 1) * P], score[b], GONE, NEG, ALU.not_equal, ALU.mult)
                ins.then_inc(S["selected"], 1)
                dve.wait_ge(S["selected"], l + 1)
                rope("bqB", qB, 1)

                dve.wait_ge(S["forget_log"], l + 1)
                dve.tensor_copy(onehot[0:H, :, :], ident[0:H, 0:H].unsqueeze(2).to_broadcast([H, H, P]))
                steps = Chain(dve, S["forget_sum_step"], l * 2)
                steps(dve.tensor_scalar(fx[0:H, :], fx[0:H, :], 0.0, None, ALU.min))
                steps(dve.tensor_tensor(fx[0:H, :], fx[0:H, :], fe[0:H, :], ALU.subtract))
                dve.tensor_tensor_scan(fF[0:H, :], ones[0:H, 0:1].to_broadcast([H, T]), fx[0:H, :], 0.0, ALU.mult, ALU.add)\
                   .then_inc(S["forget_sum"], 1)

                def attend(br, blocks, bias, sinks=False):
                    def scores(i, p):
                        h = i * 2 + p
                        mx = stat[:, 64 + 4 * p:68 + 4 * p]
                        dve.wait_ge(S["heads_scores"], nth_head(br, l) + h + 1)
                        biases = {}
                        for b, k0, n, at, to in blocks:
                            biases[b] = bias(b, k0, n, to, h)
                            if br == "fox":
                                ins = dve.scalar_tensor_tensor(out=logit[:, p, to:to + n], in0=biases[b], scalar=ftm[:, b, ds(h, 1)],
                                                               in1=fb[:, ds(h, 1), k0:k0 + n].rearrange("p a b -> p (a b)"),
                                                               op0=ALU.add, op1=ALU.subtract)
                                biases[b] = logit[:, p, to:to + n]
                        if br == "fox":
                            ins.then_inc(S["fox_biased"], 1)
                            dve.wait_ge(S["fox_biased"], l * H + h + 1)
                        plain(dve)
                        for b, k0, n, at, to in blocks:
                            ins = dve.tensor_tensor_reduce(logit[:, p, to:to + n], ps[0][:, at:at + n], biases[b], 1.0, -3e38,
                                                           ALU.add, ALU.max, mx[:, b:b + 1])
                        ins.then_inc(S["heads_max"], 1)
                        dve.wait_ge(S["heads_max"], nth_soft(br, l) + h + 1)
                        if sinks:
                            dve.tensor_scalar(mx, mx, sink[:, ds(h, 1)], None, ALU.max).then_inc(S["sink_max"], 1)
                            dve.wait_ge(S["sink_max"], l * H + h + 1)
                        dve.tensor_scalar(mx, mx, -1.0, None, ALU.mult).then_inc(S["heads_scores_read"], 1)

                    def head(i, p, last):
                        h = i * 2 + p
                        if not last:
                            scores(i + 1, p)
                        dve.wait_ge(S["heads_out"], nth_head(br, l) + h + 1)
                        total = stat[:, 72 + 4 * p:76 + 4 * p]
                        if sinks:
                            dve.tensor_tensor(total, total, stat[:, 88 + 4 * p:92 + 4 * p], ALU.add).then_inc(S["sink_sum"], 1)
                            dve.wait_ge(S["sink_sum"], l * H + h + 1)
                        dve.reciprocal(stat[:, 80 + 4 * p:84 + 4 * p], total).then_inc(S["heads_inverse"], 1)
                        dve.wait_ge(S["heads_inverse"], nth_soft(br, l) + h + 1)
                        dve.tensor_tensor(otm[:, :, ds(i * P + p * HD, HD)],
                                          ps[1][:, 3 * T:3 * T + NB * HD].rearrange("p (b d) -> p b d", d=HD),
                                          wide(stat[:, 80 + 4 * p:84 + 4 * p], HD), ALU.mult).then_inc(S["heads_out_read"], 1)

                    scores(0, 0)
                    scores(0, 1)
                    with dve.Fori(0, 3) as i:
                        head(i, 0, False)
                        head(i, 1, False)
                    head(3, 0, True)
                    head(3, 1, True)

                read_out(dve, "bft", l)
                read_out(dve, "bfb0", l)
                read_out(dve, "bfb1", l)
                attend("fox", causal, lambda b, k0, n, to, h: C["cmask"][:, T - n:T])
                read_out(dve, "btA", l)
                attend("dsa", causal, lambda b, k0, n, to, h: selb[:, to:to + n])
                rope("bqC", Q, 2)
                rope("bkC", K, 3)

                def ret_decayed(i, p):
                    h = i * 2 + p
                    dve.wait_ge(S["ret_decay"], l * H + h + 1)
                    dve.wait_ge(S["heads_scores"], nth_head("ret", l) + h + 1)
                    for j, n, at, to in forward:
                        ins = dve.tensor_tensor(logit[:, p, to:to + n], ps[0][:, at:at + n], decay[:, p, 0:n], ALU.mult)
                    ins.then_inc(S["heads_scores_read"], 1)

                plain(dve)
                with dve.Fori(0, 4) as i:
                    ret_decayed(i, 0)
                    ret_decayed(i, 1)
                dve.wait_ge(S["heads_out_read"], PRIMED + nth_head("ret", l) + H)
                grouped = otm.rearrange("p b (h d) -> p (b h) d", d=HD)
                mean, var = stat[:, 0:32], stat[:, 32:64]
                steps = Chain(dve, S["group_step"], l * 3)
                steps(dve.tensor_reduce(mean, grouped, AXX, ALU.add))
                steps(dve.tensor_scalar(mean, mean, 1.0 / HD, None, ALU.mult))
                dve.tensor_tensor(grouped, grouped, wide(mean, HD), ALU.subtract).then_inc(S["group_centred"], 1)
                dve.wait_ge(S["group_squared"], l + 1)
                dve.tensor_reduce(var, gsq.rearrange("p b (h d) -> p (b h) d", d=HD), AXX, ALU.add).then_inc(S["group_var"], 1)
                dve.wait_ge(S["group_std"], l + 1)
                steps(dve.reciprocal(mean, mean))
                dve.tensor_tensor(grouped, grouped, wide(mean, HD), ALU.mult).then_inc(S["group_normed"], 1)
                read_out(dve, "bgC", l)
                dve.wait_ge(S["y_turned"], l * 4 + 3)
                h = jobs.half["btC"]
                for c in range(NB):
                    ins = dve.scalar_tensor_tensor(out=gC[:, c, :], in0=ps[h][:, c * T:c * T + T], scalar=vec[:, W_RET + c:W_RET + c + 1],
                                                   in1=gC[:, c, :], op0=ALU.mult, op1=ALU.mult)
                ins.then_inc(drained[h], 1)
                rope("bqD", qD, 4)
                attend("swa", window, lambda b, k0, n, to, h: C["band"][:, 2 * P - n:2 * P], sinks=True)

                with dve.Fori(0, 2) as c:
                    for n in range(4):
                        read_out(dve, f"bgt{n}", l, c)
                        done(dve, f"bbr{n}", l, c)
                        h = jobs.half[f"bbr{n}"]
                        sums = merged_b[:, ds(c * 4, 4), :]
                        dve.tensor_tensor(tmp_b if n else sums, banks(h), gate_b[:, n % 2, :, :], ALU.mult).then_inc(drained[h], 1)
                        read_out(dve, f"bbr{n}", l, c)
                        if n:
                            dve.tensor_tensor(sums, sums, tmp_b, ALU.add).then_inc(S["merged_b"], 1)
                            dve.wait_ge(S["merged_b"], PRIMED + l * 6 + c * 3 + n)
                for g in range(2):
                    add_back(f"bwo{g}", g, l)
                norm("bss_ff", hT, nT, vec[:, W_FF:W_FF + KD], l)

                def conv_group(name, g, p, i=0):
                    dve.wait_ge(S["conv_begun"], l * NG + g + 1)
                    h = jobs.half[name]
                    for shift, at in ((1, W_C1), (2, W_C0)):
                        for j in range(4):
                            ch = g * 2 + (j if j < 2 else NF + j - 2)
                            ins = dve.scalar_tensor_tensor(out=conv[:, p, j, shift:T], in0=ps[h][:, j * T:j * T + T - shift],
                                                           scalar=vec[:, ds(ch + at, 1)], in1=conv[:, p, j, shift:T],
                                                           op0=ALU.mult, op1=ALU.add)
                        if shift == 1:
                            ins.then_inc(S["conv_step"], 1)
                            dve.wait_ge(S["conv_step"], l * NG + g + 1)
                    ins.then_inc(drained[h], 1)
                    dve.wait_ge(S["silu_b"], l * NG + g + 1)
                    dve.tensor_tensor(ff[:, ds(g * 2, 2), :], sg_b[:, p, :, :], conv[:, p, 2:4, :], ALU.mult).then_inc(S["ff_ready"], 1)

                with dve.Fori(0, 5) as i:
                    conv_group("bupa", i * 2, 0, i)
                    conv_group("bupb", i * 2 + 1, 1, i)
                conv_group("bupc", NG - 1, 0)
                for g in range(2):
                    add_back(f"bdn{g}", g, l)
            norm("css_fin", hT, hT, vec0[:, V_FIN2:V_FIN2 + KD])

        @block.gpsimd
        def _(pool):
            pool.sem_inc(S["s5_back_pool"], PRIMED)
            pool.memset(qz[:, :, :], 0.0).then_inc(S["zeros_set"], 1)
            pool.dma_start(bnat[0], I["s5_b_re"].rearrange("(t q) c -> q t c", q=P)).then_inc(S["s5b_loaded"], 16)
            pool.dma_start(bnat[1], I["s5_b_im"].rearrange("(t q) c -> q t c", q=P)).then_inc(S["s5b_loaded"], 16)
            pool.wait_ge(S["x_turned"], 2)
            for buf in zb + cnat:
                pool.memset(buf, 0.0).then_inc(S["zeros_set"], 1)
            pool.wait_ge(S["zeros_set"], 5)
            for n, key in enumerate(("s5_c_re", "s5_c_im")):
                rows = I[key].rearrange("(q r) s -> r q s", r=P)
                for j in range(4):
                    for g in range(2):
                        at = 32 * j + CHAN * g
                        pool.dma_start(cnat[n][at:at + CHAN, :, STATE * g:STATE * g + STATE], rows[at:at + CHAN, :, :])\
                            .then_inc(S["s5c_loaded"], 16)
            pool.wait_ge(S["normed"], nth_norm("ass_mix"))
            pool.dma_start(rms[:, :], I["consts"][:, N_CONSTS:N_CONSTS + T]).then_inc(S["iota_loaded"], 16)
            with pool.Fori(0, 4) as c:
                def fraction(t):
                    pool.wait_ge(S["s5_whole"], c * 8 + t + 1)
                    pool.tensor_tensor(turn[:, t % 2, :], turn[:, t % 2, :], whole[:, t % 2, :], ALU.subtract)\
                        .then_inc(S["s5_fraction"], 1)

                def turned(t):
                    p = t % 2
                    pool.wait_ge(S["s5_rotated"], c * 8 + t + 1)
                    pool.tensor_tensor(zt[:, p, 0, :], prod[:, p, 0, :], prod[:, p, 1, :], ALU.add)
                    pool.tensor_tensor(zt[:, p, 1, :], prod[:, p, 2, :], prod[:, p, 3, :], ALU.subtract).then_inc(S["s5_z"], 1)

                def back(t):
                    p = t % 2
                    pool.wait_ge(S["s5_scanned"], c * 16 + 2 * t + 2)
                    for n in range(2):
                        ins = pool.tensor_tensor(prod[:, p, 2 + n, :], st[:, p, n, :], trig[:, t % 4, 1 - n, :], ALU.mult)
                    ins.then_inc(S["s5_back_pool"], 1)

                fraction(0)
                fraction(1)
                for t in range(8):
                    turned(t)
                    if t < 6:
                        fraction(t + 2)
                    if t:
                        back(t - 1)
                back(7)
            pool.wait_ge(S["s5_y_read"], PRIMED + 4)
            pool.dma_start(wsn, I["sgu_w"].rearrange("h t s -> t h s")).then_inc(S["sgu_loaded"], 16)
            pool.dma_start(sgub, I["sgu_bias"].unsqueeze(0).to_broadcast([P, H, P])).then_inc(S["sgu_loaded"], 16)
            pool.dma_start(lng, I["sgu_ln_g"].unsqueeze(0).to_broadcast([P, D])).then_inc(S["sgu_loaded"], 16)
            pool.dma_start(lnb, I["sgu_ln_b"].unsqueeze(0).to_broadcast([P, D])).then_inc(S["sgu_loaded"], 16)
            pool.wait_ge(S["vecs_turned"], 1)
            with pool.Fori(0, LAYERS) as l:
                pool.wait_ge(S["merged_b"], PRIMED + l * 6)
                seen = S["layer_vecs_loaded"]
                for at, n, key in ((W_AT, 8, "attn_norm_2"), (W_FF, 8, "ffn_norm_2"), (W_RET, 4, "ret_norm_2"), (W_CB, 44, "conv_b_2")):
                    pool.dma_start(vrow[at:at + n, 0, :], I[key][ds(l, 1), :].rearrange("o (r p) -> (o r) p", p=P)).then_inc(seen, 16)
                taps = I["conv_w_2"]
                pool.dma_start(vrow[W_C2:W_C2 + 44, 0, :], taps[ds(l * 3 + 2, 1), :].rearrange("o (r p) -> (o r) p", p=P)).then_inc(seen, 16)
                pool.dma_start(vrow[0:88, 1, :], taps[ds(l * 3, 2), :].rearrange("o (r p) -> (o r) p", p=P)).then_inc(seen, 16)
                pool.dma_start(sink[:, :], I["attn_sinks_2"][ds(l, 1), :].to_broadcast([P, H])).then_inc(seen, 16)
                pool.dma_start(fbias[0:H, :], I["forget_bias_2"][ds(l, 1), :].rearrange("o h -> h o")).then_inc(seen, 16)


_SHAPES = {
    "x": (512, 1024), "mem": (256, 1024), "mix_norm_g": (1024,), "w_in": (1024, 4608), "s5_lam_re": (32, 128),
    "s5_lam_im": (32, 128), "s5_log_step": (32, 2), "s5_b_re": (4096, 16), "s5_b_im": (4096, 16),
    "s5_c_re": (1024, 64), "s5_c_im": (1024, 64), "s5_d": (512,), "s5_w_glu": (512, 512), "sgu_ln_g": (1024,),
    "sgu_ln_b": (1024,), "sgu_w": (8, 128, 128), "sgu_bias": (8, 128), "w_proj_a": (512, 1024),
    "w_proj_b": (1024, 1024), "w_out": (1024, 1024), "xattn_norm_g": (1024,), "mem_norm_g": (1024,),
    "w_q": (1024, 1024), "w_k": (1024, 1024), "w_v": (1024, 1024), "w_xo": (1024, 1024), "ffn_norm_g": (1024,),
    "w_gate": (1024, 2816), "w_up": (1024, 2816), "w_down": (2816, 1024), "final_norm_g": (1024,),
    "attn_norm_2": (2, 1024), "w_in_2": (2048, 9420), "forget_bias_2": (2, 8), "ret_norm_2": (2, 512),
    "attn_sinks_2": (2, 8), "w_branch_2": (4096, 1024), "w_out_2": (2048, 1024), "ffn_norm_2": (2, 1024),
    "w_up_2": (2048, 5632), "conv_w_2": (6, 5632), "conv_b_2": (2, 5632), "w_down_2": (5632, 1024),
    "final_norm_2": (1024,),
}


def kernel(**inputs):
    import numpy as _np
    import concourse.bacc as _bacc
    from concourse import mybir as _mybir
    from concourse.bass_utils import run_bass_kernel_spmd as _run

    nc = _bacc.Bacc("TRN2", target_bir_lowering=False, num_devices=1)
    arrays = {name: _np.ascontiguousarray(inputs[name]).reshape(shape) for name, shape in _SHAPES.items()}
    arrays["consts"] = constants()
    handles = {name: nc.dram_tensor(f"in_{name}", a.shape, _mybir.dt.from_np(a.dtype), kind="ExternalInput").ap()
               for name, a in arrays.items()}
    out = nc.dram_tensor("out", (512, 1024), _mybir.dt.float32, kind="ExternalOutput").ap()
    two_blocks(nc, handles, out)
    r = _run(nc, [{f"in_{name}": a for name, a in arrays.items()}], core_ids=[0])
    return r.results[0]["out"].reshape(1, 512, 1024)
```

```python
from contextlib import ExitStack

import numpy as np
import concourse.bass as bass
from concourse import mybir

ALU = mybir.AluOpType
ACT = mybir.ActivationFunctionType
F32 = mybir.dt.float32
F32R = mybir.dt.float32r
AXX = mybir.AxisListType.X

P = 128
T = 512
NB = T // P
D = 1024
KD = D // P
M = 256
EPS = 1e-6
FF = 2816
NF = FF // P
NG = NF // 2
H = 8
HD = 64
TOPK = 128
LAYERS = 2
NEG = -1e30
GONE = -3e38
GROUPS, STATE, CHAN = 32, 64, 16
QUADS = 8
TWO_PI = 6.283185
INV_2PI = float(np.float32(1.0 / (2.0 * np.pi)))
C1 = 6.28125
C2 = float(2.0 * np.pi - 6.28125)
ROUND = 12582912.0

FOX_Q, FOX_K, FOX_V, FOX_F = 0, 512, 1024, 1536
DSA_Q, DSA_K, DSA_V, IDX_Q, IDX_K, IDX_W = 1544, 2056, 2120, 2184, 2440, 2504
RET_Q, RET_K, RET_V, RET_G = 2508, 3020, 3532, 4044
SWA_Q, SWA_K, SWA_V = 4556, 5068, 5196
GATES = 5324
MF, MW, MVB, MVD, MIX2 = 0, 8, 12, 76, 204

SLOTS = 8
ARENA = 27776
SPLITS = 4

FIRST = [[("xa", 8, 1)], [("glu", 4, 1)], [("zu0", 8, 1), ("zu1", 8, 1), ("zv0", 8, 1), ("zv1", 8, 1)],
         ("loop", 2, [("ga", 8, 1), ("pa", 4, 1), ("gb", 8, 1), ("pb", 8, 1), (None, 4, 0)]),
         [("wo0", 8, 1), ("wo1", 8, 1), ("wk0", 8, 1), ("wk1", 8, 1), ("wv0", 8, 1), ("wv1", 8, 1),
          ("wq0", 8, 1), ("wq1", 8, 1), ("xo0", 8, 1), ("xo1", 8, 1)],
         ("loop", 5, [("upa", 8, 2), ("upb", 8, 2)]), [("upc", 8, 2), ("dn0", 22, 1), ("dn1", 22, 1)]]
LAYER = [[("mix1", 8, 4), ("mix2", 8, 4), ("qB", 8, 1), ("qA", 8, 1), ("kA", 8, 1), ("vA", 8, 1),
          ("qC", 8, 1), ("kC", 8, 1), ("vC", 8, 1), ("gC", 8, 1), ("qD", 8, 1)],
         ("loop", 2, [(f"{s}{n}", u, 1) for n in range(4) for s, u in (("gt", 8), ("br", 4))]),
         [("wo0", 8, 1), ("wo1", 8, 1)],
         ("loop", 5, [("upa", 8, 2), ("upb", 8, 2)]), [("upc", 8, 2), ("dn0", 22, 1), ("dn1", 22, 1)]]


def pad_units(parts):
    n = sum((p[1] if p[0] == "loop" else 1) * sum(u for _, u, _ in (p[2] if p[0] == "loop" else p))
            for p in parts)
    return parts + [[(None, -n % SLOTS, 0)]]


PRIMED = 1


class Ring:

    def __init__(self):
        self.slot, self.split, self.before, self.landed, self.units = {}, {}, {}, {}, {}
        self.room, self.split_room = {}, {}
        at = before = 0
        pieces, owner, split_owner = [0] * SLOTS, [0] * SLOTS, [0] * SPLITS
        stages = [("a", 0, pad_units(FIRST))] + [("b", l, pad_units(LAYER)) for l in range(LAYERS)]
        for stage, l, parts in stages:
            for part in parts:
                reps, body = (part[1], part[2]) if part[0] == "loop" else (1, part)
                for i in range(reps):
                    for name, units, dmas in body:
                        for u in range(units):
                            s, p = at % SLOTS, at % SPLITS
                            at += 1
                            if name is None:
                                continue
                            key = (stage + name, u)
                            pieces[s] += 16 * dmas
                            assert self.slot.setdefault(key, s) == s
                            self.split[key] = p
                            self.units[stage + name] = units
                            self.before[key + (l, i)] = before
                            self.landed[key + (l, i)] = pieces[s]
                            self.room[key] = max(self.room.get(key, -SLOTS), owner[s] - before)
                            self.split_room[key] = max(self.split_room.get(key, -SLOTS), split_owner[p] - before)
                            before += 1
                            owner[s] = split_owner[p] = before

    def at(self, table, name, u, l, i):
        v = table[(name, u, 0, 0)]
        for reg, other in ((l, (1, 0)), (i, (0, 1))):
            if (name, u) + other in table:
                v = v + reg * (table[(name, u) + other] - table[(name, u, 0, 0)])
        return v


JOBS_FIRST = ["vecs", "x0", "x1", "memT", "ss_mem", "ss_mix", "xa", "s5col", "s5B", "s5C", "glu",
              "zu0", "zu1", "zv0", "zv1", "wsT", "sv0", "sv1", (2, ["ga", "pa", "gb", "pb"]),
              "wo0", "wo1", "wk0", "wk1", "wv0", "wv1", "ss_xa", "wq0", "wq1",
              "xs0", "xs1", "xt0", "xs2", "xv0", "xt1", "xs3", "xv1", "xt2", "xv2", "xt3", "xv3",
              "xo0", "xo1", "ss_ff", (5, ["upa", "upb"]), "upc", "dn0", "dn1", "ss_fin"]
JOBS_LAYER = ["vecs", "ss_at", "mix1", "mix2", "ix1", "ix2", "ix3", "qB", "qA", "kA", "lf", "vA",
              "ft", "fb0", "fb1", "tA", "tB", "qC", "kC", "vC", "gC", "tC", "qD", "tD",
              (2, [f"{s}{n}" for n in range(4) for s in ("gt", "br")]), "wo0", "wo1", "ss_ff",
              (5, ["upa", "upb"]), "upc", "dn0", "dn1"]
JOBS_LAST = ["ss_fin", "out0", "out1"]


class Jobs:

    def __init__(self):
        self.half, self.before = {}, {}
        seq, count = 0, [0, 0]
        for stage, l, jobs in [("a", 0, JOBS_FIRST)] + [("b", l, JOBS_LAYER) for l in range(LAYERS)] + [
                ("c", 0, JOBS_LAST)]:
            for job in jobs:
                reps, body = job if isinstance(job, tuple) else (1, [job])
                for i in range(reps):
                    for name in body:
                        h = seq % 2
                        assert self.half.setdefault(stage + name, h) == h, (stage, name)
                        self.before[(stage + name, l, i)] = count[h]
                        count[h] += 1
                        seq += 1

    def nth(self, name, l=0, i=0):
        v = self.before[(name, 0, 0)]
        for reg, other in ((l, (1, 0)), (i, (0, 1))):
            if (name,) + other in self.before:
                v = v + reg * (self.before[(name,) + other] - self.before[(name, 0, 0)])
        return v


NORMS = {"ass_mem": 0, "ass_mix": 1, "ass_xa": 2, "ass_ff": 3, "ass_fin": 4, "bss_at": 5, "bss_ff": 6, "css_fin": 9}
WHOLE_NORMS = {"ass_mem": 1, "ass_fin": 2, "css_fin": 3}
SPLIT_NORMS = {"ass_mix": 0, "ass_xa": 1, "ass_ff": 2, "bss_at": 3, "bss_ff": 4}


def nth_norm(name, l=0):
    return NORMS[name] + (l * 2 if name[0] == "b" else 0) + 1


def split_chunks(name, l=0):
    return SPLIT_NORMS[name] * KD + (l * (2 * KD) if name[0] == "b" else 0)


class Chain:

    def __init__(self, eng, sem, base=0):
        self.eng, self.sem, self.base, self.n = eng, sem, base, 0

    def __call__(self, ins):
        self.n += 1
        ins.then_inc(self.sem, 1)
        self.eng.wait_ge(self.sem, self.base + self.n)


CONSTS = (("ident", P), ("ones", P), ("cmask", T), ("band", 2 * P), ("cos", T), ("sin", T),
          ("dist", T), ("logdecay", H))
N_CONSTS = sum(n for _, n in CONSTS)


def constants():
    f32, row, col = np.float32, np.arange(P)[:, None], np.arange(T)[None, :]
    inv = (1.0 / np.power(f32(10000.0), np.arange(HD // 2, dtype=f32) * f32(2.0) / f32(HD))).astype(f32)
    angle = (np.arange(T, dtype=f32)[None, :] * inv[np.arange(P) % 32][:, None]).astype(f32).astype(np.float64)
    sign = np.where(np.arange(P) % HD < 32, -1.0, 1.0)[:, None]
    j = np.arange(2 * P)[None, :]
    tables = {
        "ident": np.eye(P), "ones": np.ones((P, P)), "iota": np.broadcast_to(col, (P, T)),
        "cmask": np.where(col - (T - P) > row, NEG, 0.0),
        "band": np.where((j > row) & (j <= row + P), 0.0, NEG),
        "cos": np.cos(angle), "sin": np.sin(angle) * sign,
        "dist": np.where(col >= row, col - row, -NEG),
        "logdecay": np.broadcast_to(np.log(1.0 - 2.0 ** (-5.0 - np.arange(H)))[None, :], (P, H)),
    }
    return np.ascontiguousarray(np.concatenate([np.asarray(tables[n], f32) for n in [n for n, _ in CONSTS] + ["iota"]], axis=1))


V_MIX, V_MEM, V_XA, V_FF, V_FIN, V_FIN2, V_D, V_ROWS = 0, 8, 16, 24, 32, 40, 48, 52
W_AT, W_FF, W_RET, W_CB, W_C2, W_C0, W_C1 = 0, 8, 16, 20, 64, 108, 152
W_ROWS1, W_ROWS2 = 108, 88


def two_blocks(nc, I, out):
    ring, jobs = Ring(), Jobs()
    ds = bass.ds
    with ExitStack() as ctx:
        def sb(name, *shape):
            return ctx.enter_context(nc.sbuf_tensor(name, [P, *shape], F32))

        class Signals(dict):
            def __missing__(self, name):
                self[name] = ctx.enter_context(nc.semaphore(name))
                return self[name]

        S = Signals()
        landed = [S[f"weights_landed{s}"] for s in range(SLOTS)]
        weights_high, weights_split = S["weights_high"], S["weights_split"]
        weights_used = S["weights_used"]
        drained = [S["half0_drained"], S["half1_drained"]]

        ps = [ctx.enter_context(nc.psum_tensor(f"half{h}", [P, 4 * T], F32)) for h in range(2)]
        hT = sb("hT", KD, T)
        nH = ctx.enter_context(nc.sbuf_tensor("nH", [P, KD, T], F32R))
        nL = ctx.enter_context(nc.sbuf_tensor("nL", [P, KD, T], F32R))
        slot = sb("slot", SLOTS, 512)
        wH = ctx.enter_context(nc.sbuf_tensor("wH", [P, SPLITS, 512], F32R))
        wL = ctx.enter_context(nc.sbuf_tensor("wL", [P, SPLITS, 512], F32R))
        consts = sb("consts", N_CONSTS)
        C, at = {}, 0
        for name, n in CONSTS:
            C[name] = consts[:, at:at + n]
            at += n
        ident, ones = C["ident"], C["ones"]
        vrow = sb("vrow", 2, P)
        vec = sb("vec", W_ROWS1 + W_ROWS2)
        vec0 = sb("vec0", V_ROWS)
        rms = sb("rms", T)
        qz = sb("qz", 2, T)
        small = sb("small", 160)
        eps, half_pi = small[:, 0:1], small[:, 1:2]
        stat = small[:, 2:154]
        with nc.sbuf_tensor("arena", [P, ARENA], F32) as arena:
            pass
        arena_split = ctx.enter_context(nc.sbuf_tensor("arena_split", [P, ARENA], F32R))

        def A(at, *shape, of=arena):
            n = int(np.prod(shape))
            v = of[:, at:at + n]
            if len(shape) == 2:
                v = v.rearrange("p (a b) -> p a b", b=shape[1])
            elif len(shape) == 3:
                v = v.rearrange("p (a b c) -> p a b c", b=shape[1], c=shape[2])
            return v

        def banks(h, n=4, w=T):
            return ps[h][:, 0:n * T].rearrange("p (a b) -> p a b", b=T)[:, :, 0:w]

        def R(at, *shape):
            return A(at, *shape, of=arena_split)

        def plainly(v):
            return v.bitcast(F32)

        x_in, mem_in, mT = A(0, NB, D), A(4096, 2, D), A(6144, KD, M)
        uT = A(8192, NB, T)
        s5w = A(10240, QUADS, 5, P)
        cnat = [A(0, QUADS, P), A(1024, QUADS, P)]
        zb = [A(2048, 32, 32), A(3072, 32, 32)]
        ust, stg = A(4096, T), A(4608, 2, 5 * P)
        trig = A(0, 4, 2, T)
        turn, whole = A(15360, 2, T), A(16384, 2, T)
        prod, zt, st = A(17408, 2, 4, T), A(21504, 2, 2, T), A(23552, 2, 2, T)
        row = A(17408, 24, P)
        bnat = [A(20480, 32, CHAN), A(20992, 32, CHAN)]
        bprod = [A(15360 + 512 * n, 32, CHAN) for n in range(4)]
        s5col = sb("s5col", 4, 32)
        yH, yL = R(0, NB, T), R(2048, NB, T)
        zv, zu = A(10240, NB, D), A(14336, KD, T)
        wsn, wsT, sgub = A(18432, H, P), A(19456, H, P), A(20480, H, P)
        lng, lnb, svt = A(21504, D), A(22528, D), A(23552, 4, T)
        zuH, zuL = R(18432, KD, T), R(10240, KD, T)
        gate_a, merged_a = [A(4096, 4, T), A(25600, 4, T)], A(14336, KD, T)
        merged_aH, merged_aL = [R(23552, 4, T), R(0, 4, T)], R(14336, KD, T)
        mH, mL = R(8192, KD, M), R(6144, KD, M)
        xq, xk, xv = A(10240, KD, T), A(2048, KD, M), A(4096, 2, D)
        xp, xpT, xoH, xoL = A(14336, 2, NB, M), A(16384, 2, 2, T), R(18432, KD, T), R(22528, KD, T)

        sq = A(22528, KD, T)
        ffH, ffL = R(0, NF, T), R(11264, NF, T)
        sg_a, ff_raw = A(22528, 2, 2, T), A(24576, 2, 2, T)

        Q, K, V = A(0, NB, T), A(2048, NB, T), A(4096, NB, T)
        qB, gC, qD = A(6144, NB, T), K, Q
        mix1, mix2 = A(8192, NB, T), A(10240, NB, MIX2)
        kBB, kII, kDD = A(11056, T), A(11568, T), A(4096, 2, T)
        selb = A(12080, 1280)
        logit = A(13360, 2, 1280)
        probT = A(15920, 1280)
        fb, part = A(17200, H, T), A(17200, NB, T)
        otm = A(21296, NB, T)
        yAH, yAL, yBH, yBL = R(23344, NB, T), R(25392, NB, T), R(6144, NB, T), R(11056, NB, T)
        yCH, yCL, yDH, yDL = R(19248, NB, T), R(2048, NB, T), R(0, NB, T), R(4096, NB, T)
        fx, fe, fF, onehot = A(13360, T), A(13872, T), A(14384, T), A(14896, H, P)
        relu, score = A(23344, NB, T), [None, A(15920, 256), A(16176, 384), A(16560, 512)]
        decay, gsq = A(19248, 2, T), A(17200, NB, T)
        gate_b, merged_b = [A(8192, 4, T), A(21296, 4, T)], A(13104, KD, T)
        merged_bH, merged_bL = [R(17200, 4, T), R(0, 4, T)], R(13104, KD, T)
        conv = A(22528, 2, 4, T)
        o_out = A(0, NB, D)
        ftm = sb("ftm", NB, H)
        sink = sb("sink", H)
        fbias = sb("fbias", 1)

        causal = [(0, 0, 128, 896, 0), (1, 0, 256, 1024, 128), (2, 0, 384, 512, 384), (3, 0, 512, 0, 768)]
        window = [(0, 0, 128, 896, 0), (1, 0, 256, 1024, 128), (2, 128, 256, 512, 384), (3, 256, 256, 0, 640)]
        forward = [(0, 512, 0, 0), (1, 384, 512, 512), (2, 256, 1024, 896), (3, 128, 896, 1152)]

        def turned_blocks(blocks):
            return [(j, b, k0, at) for j in range(NB) for b, k0, n, _, at in blocks if k0 <= j * P < k0 + n]

        def nth_head(br, l):
            return l * (4 * H) + ("fox", "dsa", "ret", "swa").index(br) * H

        def nth_soft(br, l):
            return l * (3 * H) + ("fox", "dsa", "swa").index(br) * H

        def done(eng, name, l=0, i=0):
            eng.wait_ge(weights_used, ring.at(ring.before, name, ring.units[name] - 1, l, i) + 1)

        def plain(eng):
            eng.nop(nofuse=True)

        def read_out(eng, name, l=0, i=0):
            eng.wait_ge(drained[jobs.half[name]], jobs.nth(name, l, i) + 1)

        for name, reps, after in (("aga", 2, "awo0"), ("aupa", 5, "aupc"), ("bgt0", 2, "bwo0"), ("bupa", 5, "bupc")):
            for u in range(SPLITS):
                assert ring.slot[(name, u)] == ring.slot[(after, u)] and ring.split_room[(name, u)] == ring.split_room[(after, u)]
                for table in (ring.before, ring.landed):
                    assert ring.at(table, name, u, 0, reps) == ring.at(table, after, u, 0, 0)

        def lin(w, r0, c0):
            return lambda u: [(slice(0, 512), w[ds(r0 + u * P, P), ds(c0, 512)])]

        block = ctx.enter_context(nc.Block())

        @block.sync
        def _(sp):
            sp.dma_start(x_in, I["x"].rearrange("(b p) d -> p b d", p=P)).then_inc(S["x_loaded"], 16)

            def load(name, pieces, l=0, i=0):
                for u in range(ring.units[name]):
                    s = ring.slot[(name, u)]
                    free = ring.at(ring.before, name, u, l, i) + ring.room[(name, u)]
                    if not isinstance(free, int) or free > 0:
                        sp.wait_ge(weights_split, free)
                        plain(sp)
                    for cols, src in pieces(u):
                        sp.dma_start(slot[:, s, cols], src).then_inc(landed[s], 16)

            w = I["w_in"]
            load("axa", lin(w, 0, 0))
            load("aglu", lin(I["s5_w_glu"], 0, 0))
            for g in range(2):
                load(f"azu{g}", lin(w, 0, 512 + 512 * g))
            for g in range(2):
                load(f"azv{g}", lin(w, 0, 1536 + 512 * g))
            with sp.Fori(0, 2) as c:
                load("aga", lin(w, 0, c * 512 + 2560), 0, c)
                load("apa", lin(I["w_proj_a"], 0, c * 512), 0, c)
                load("agb", lin(w, 0, c * 512 + 3584), 0, c)
                load("apb", lin(I["w_proj_b"], 0, c * 512), 0, c)
            for name, key in (("wo", "w_out"), ("wk", "w_k"), ("wv", "w_v"), ("wq", "w_q"), ("xo", "w_xo")):
                for g in range(2):
                    load(f"a{name}{g}", lin(I[key], 0, 512 * g))

            def up(first, second, r0, g):
                return lambda u: [(slice(0, 256), first[ds(r0 + u * P, P), ds(g * 256, 256)]),
                                  (slice(256, 512), second(u, g))]

            def up_a(g):
                return up(I["w_gate"], lambda u, g: I["w_up"][ds(u * P, P), ds(g * 256, 256)], 0, g)

            with sp.Fori(0, 5) as i:
                load("aupa", up_a(i * 2), 0, i)
                load("aupb", up_a(i * 2 + 1), 0, i)
            load("aupc", up_a(NG - 1))
            for g in range(2):
                load(f"adn{g}", lin(I["w_down"], 0, 512 * g))

            w = I["w_in_2"]
            with sp.Fori(0, LAYERS) as l:
                r = l * D
                sp.wait_ge(S["vecs_turned"], 1)
                sp.wait_ge(S["merged_b"], PRIMED + l * 6)
                seen = S["layer_vecs_loaded"]
                for at, n, key in ((W_AT, 8, "attn_norm_2"), (W_FF, 8, "ffn_norm_2"), (W_RET, 4, "ret_norm_2"), (W_CB, 44, "conv_b_2")):
                    sp.dma_start(vrow[at:at + n, 0, :], I[key][ds(l, 1), :].rearrange("o (r p) -> (o r) p", p=P)).then_inc(seen, 16)
                taps = I["conv_w_2"]
                sp.dma_start(vrow[W_C2:W_C2 + 44, 0, :], taps[ds(l * 3 + 2, 1), :].rearrange("o (r p) -> (o r) p", p=P)).then_inc(seen, 16)
                sp.dma_start(vrow[0:88, 1, :], taps[ds(l * 3, 2), :].rearrange("o (r p) -> (o r) p", p=P)).then_inc(seen, 16)
                sp.dma_start(sink[:, :], I["attn_sinks_2"][ds(l, 1), :].to_broadcast([P, H])).then_inc(seen, 16)
                sp.dma_start(fbias[0:H, :], I["forget_bias_2"][ds(l, 1), :].rearrange("o h -> h o")).then_inc(seen, 16)

                def cols(*pieces):
                    def unit(u):
                        at, got = 0, []
                        for c0, n in pieces:
                            got.append((slice(at, at + n), w[ds(r + u * P, P), c0:c0 + n]))
                            at += n
                        return got
                    return unit

                load("bmix1", cols((IDX_Q, 256), (DSA_K, 64), (IDX_K, 64), (SWA_K, 128)), l)
                load("bmix2", cols((FOX_F, 8), (IDX_W, 4), (DSA_V, 64), (SWA_V, 128)), l)
                for name, c0 in (("qB", DSA_Q), ("qA", FOX_Q), ("kA", FOX_K), ("vA", FOX_V), ("qC", RET_Q),
                                 ("kC", RET_K), ("vC", RET_V), ("gC", RET_G), ("qD", SWA_Q)):
                    load("b" + name, lin(w, r, c0), l)
                with sp.Fori(0, 2) as c:
                    for n in range(4):
                        load(f"bgt{n}", lin(w, r, c * 512 + GATES + n * D), l, c)
                        load(f"bbr{n}", lin(I["w_branch_2"], l * 2048 + n * 512, c * 512), l, c)
                for g in range(2):
                    load(f"bwo{g}", lin(I["w_out_2"], r, 512 * g), l)

                def up_b(g):
                    w2 = I["w_up_2"]
                    return up(w2, lambda u, g: w2[ds(r + u * P, P), ds(g * 256 + FF, 256)], r, g)

                with sp.Fori(0, 5) as i:
                    load("bupa", up_b(i * 2), l, i)
                    load("bupb", up_b(i * 2 + 1), l, i)
                load("bupc", up_b(NG - 1), l)
                for g in range(2):
                    load(f"bdn{g}", lin(I["w_down_2"], l * FF, 512 * g), l)

            rows = out.rearrange("(b p) d -> p b d", p=P)
            for g in range(2):
                read_out(sp, f"cout{g}")
                sp.dma_start(rows[:, :, 512 * g:512 * g + 512], o_out[:, :, 512 * g:512 * g + 512])\
                  .then_inc(S["stored"], 16)
            sp.wait_ge(S["stored"], 32)

        @block.tensor
        def _(pe):
            def fill(name, l=0, i=0):
                h, n = jobs.half[name], jobs.nth(name, l, i)
                if not isinstance(n, int) or n > 0:
                    pe.wait_ge(drained[h], n)
                return ps[h]

            def linear(name, act, l=0, i=0, n=T, tokens=None, cols=512, normed=None):
                o = fill(name, l, i)
                last = ring.units[name] - 1
                for k in range(last + 1):
                    p = ring.split[(name, k)]
                    pe.wait_ge(weights_split, ring.at(ring.before, name, k, l, i) + 1)
                    if normed is not None:
                        pe.wait_ge(S["normed_split"], normed + k + 1)
                    high, rest = act(k)
                    for j in range(tokens or 4):
                        block = slice(j * P, j * P + P)
                        if tokens:
                            dst = o[:, j * T:j * T + cols]
                            passes = [(high[:, block], wH[:, p, 0:cols]), (high[:, block], wL[:, p, 0:cols]),
                                      (rest[:, block], wH[:, p, 0:cols])]
                        else:
                            dst = o[:, j * T:j * T + n]
                            passes = [(wH[:, p, block], high), (wH[:, p, block], rest), (wL[:, p, block], high)]
                        for m, (lhsT, rhs) in enumerate(passes):
                            mm = pe.matmul(dst, lhsT, rhs, start=(k == 0 and m == 0), stop=(k == last and m == 2))
                    mm.then_inc(weights_used, 1)

            def split(high, rest):
                return lambda k: (high[:, k, :], rest[:, k, :])

            stream = split(nH, nL)

            def halves(high, rest):
                return lambda k: (high[k // 4][:, k % 4, :], rest[:, k, :])

            def square_sum(name, l=0, n=T):
                o = fill(name, l)
                pe.wait_ge(S["squared"], nth_norm(name, l))
                squares = A(8192, KD, M) if name == "ass_mem" else sq
                for k in range(KD):
                    mm = pe.matmul(o[:, 0:n], ones, squares[:, k, :], start=(k == 0), stop=(k == KD - 1))
                mm.then_inc(S["summed"], 1)

            pe.sem_inc(S["s5_out"], PRIMED)
            pe.wait_ge(S["consts_loaded"], 16)
            pe.wait_ge(S["vecs_loaded"], 16 * 7)
            o = fill("avecs")
            pe.transpose(o[:, 0:V_ROWS], vrow[0:V_ROWS, 0, :], ident[0:V_ROWS, 0:V_ROWS]).then_inc(S["vecs_turned"], 1)
            pe.wait_ge(S["x_loaded"], 16)
            for g in range(2):
                o = fill(f"ax{g}")
                for c in range(4):
                    for b in range(NB):
                        mm = pe.transpose(o[:, c * T + b * P:c * T + b * P + P],
                                          x_in[:, b, (4 * g + c) * P:(4 * g + c + 1) * P], ident)
                mm.then_inc(S["x_turned"], 1)
            pe.wait_ge(S["mem_loaded"], 16)
            o = fill("amemT")
            for c in range(KD):
                for b in range(2):
                    mm = pe.transpose(o[:, c * M + b * P:c * M + b * P + P], mem_in[:, b, c * P:c * P + P], ident)
            mm.then_inc(S["mem_turned"], 1)
            square_sum("ass_mem", n=M)
            square_sum("ass_mix")
            linear("axa", stream, normed=split_chunks("ass_mix"))

            o = fill("as5col")
            pe.wait_ge(S["s5_params"], 1)
            for n in range(4):
                mm = pe.transpose(o[:, 32 * n:32 * n + 32], row[0:32, n, :], ident[0:32, 0:32])
            mm.then_inc(S["s5_turned"], 1)
            o = fill("as5B")
            pe.wait_ge(S["s5_bbar"], 1)
            for q in range(QUADS):
                for n in range(2):
                    mm = pe.transpose(o[:, (2 * q + n) * P:(2 * q + n + 1) * P], zb[n][:, 4 * q:4 * q + 4, :], ident)
            mm.then_inc(S["s5_turned"], 1)
            o = fill("as5C")
            pe.wait_ge(S["s5c_loaded"], 16 * 16)
            for q in range(QUADS):
                for n in range(2):
                    mm = pe.transpose(o[:, (2 * q + n) * P:(2 * q + n + 1) * P], cnat[n][:, q, :], ident)
            mm.then_inc(S["s5_turned"], 1)
            read_out(pe, "as5B")
            read_out(pe, "as5C")
            with pe.Fori(0, 4) as c:
                def drive(t):
                    d, j, p = t // 4, t % 4, t % 2
                    if j == 0:
                        pe.wait_ge(S["s5_staged"], c * 2 + d + 1)
                    if t >= 2:
                        pe.wait_ge(S["s5_rotated"], c * 8 + t - 1)
                    for n in range(2):
                        mm = pe.matmul(ps[0][:, (2 * p + n) * T:(2 * p + n + 1) * T],
                                       stg[32 * j:32 * j + 32, d, n * P:n * P + P], ust[32 * j:32 * j + 32, :],
                                       start=True, stop=True)
                    mm.then_inc(S["s5_driven"], 1)

                drive(0)
                drive(1)
                for t in range(8):
                    d, j, p = t // 4, t % 4, t % 2
                    pe.wait_ge(S["s5_back_dve"], c * 8 + t + 1)
                    pe.wait_ge(S["s5_back_pool"], PRIMED + c * 8 + t + 1)
                    if t == 0:
                        pe.wait_ge(S["s5_y_read"], PRIMED + c)
                    for n, kind in enumerate((2, 3, 4, 4)):
                        mm = pe.matmul(ps[1][32 * j:32 * j + 32, 0:T],
                                       stg[:, d, kind * P + 32 * j:kind * P + 32 * j + 32], prod[:, p, n, :],
                                       start=(d == 0 and n == 0), stop=(d == 1 and n == 3), skip_group_check=True)
                    mm.then_inc(S["s5_out"], 1)
                    if t < 6:
                        drive(t + 2)
            pe.wait_ge(S["s5_y_read"], PRIMED + 4)
            pe.wait_ge(S["ya_split"], 1)
            linear("aglu", split(yH, yL))

            for g in range(2):
                linear(f"azu{g}", stream)
            for g in range(2):
                linear(f"azv{g}", stream, tokens=NB)
            o = fill("awsT")
            pe.wait_ge(S["sgu_loaded"], 16 * 4)
            for h in range(H):
                mm = pe.transpose(o[:, h * P:h * P + P], wsn[:, h, :], ident)
            mm.then_inc(S["ws_turned"], 1)
            pe.wait_ge(S["zv_normed"], 1)
            read_out(pe, "awsT")
            for g in range(2):
                o = fill(f"asv{g}")
                for h in range(4):
                    for b in range(NB):
                        mm = pe.matmul(o[:, h * T + b * P:h * T + b * P + P], zv[:, b, (4 * g + h) * P:(4 * g + h + 1) * P],
                                       wsT[:, 4 * g + h, :], start=True, stop=True)
                mm.then_inc(S["sv_done"], 1)
            with pe.Fori(0, 2) as c:
                linear("aga", stream, 0, c)
                pe.wait_ge(S["ya_split"], 2)
                linear("apa", split(yH, yL), 0, c)
                linear("agb", stream, 0, c)
                pe.wait_ge(S["yb_split"], 2)
                linear("apb", split(zuH, zuL), 0, c)
            pe.wait_ge(S["merged_a_split"], 2)
            for g in range(2):
                linear(f"awo{g}", halves(merged_aH, merged_aL))

            pe.wait_ge(S["mem_split"], 1)
            for g in range(2):
                linear(f"awk{g}", split(mH, mL), n=M)
            for g in range(2):
                linear(f"awv{g}", split(mH, mL), tokens=2)
            square_sum("ass_xa")
            for g in range(2):
                linear(f"awq{g}", stream, normed=split_chunks("ass_xa"))
            read_out(pe, "awq0")
            read_out(pe, "awq1")

            def x_scores(h):
                o = fill(f"axs{h}")
                for b in range(NB):
                    for c in range(2):
                        mm = pe.matmul(o[:, b * M:b * M + M], xq[:, 2 * h + c, b * P:b * P + P], xk[:, 2 * h + c, :],
                                       start=(c == 0), stop=(c == 1))
                mm.then_inc(S["x_scores"], 1)

            def x_turn(h):
                pe.wait_ge(S["x_probs"], h + 1)
                o = fill(f"axt{h}")
                for m in range(2):
                    for b in range(NB):
                        mm = pe.transpose(o[:, m * T + b * P:m * T + b * P + P], xp[:, h % 2, b, m * P:m * P + P], ident)
                mm.then_inc(S["x_probs_turned"], 1)

            def x_out(h):
                read_out(pe, f"axt{h}")
                o = fill(f"axv{h}")
                for c in range(2):
                    for m in range(2):
                        mm = pe.matmul(o[:, c * T:c * T + T], xv[:, m, (2 * h + c) * P:(2 * h + c + 1) * P],
                                       xpT[:, h % 2, m, :], start=(m == 0), stop=(m == 1))
                mm.then_inc(S["x_out"], 1)

            x_scores(0)
            x_scores(1)
            x_turn(0)
            x_scores(2)
            x_out(0)
            x_turn(1)
            x_scores(3)
            x_out(1)
            for h in (2, 3):
                x_turn(h)
                x_out(h)
            read_out(pe, "axv3")
            for g in range(2):
                linear(f"axo{g}", split(xoH, xoL))
            square_sum("ass_ff")
            with pe.Fori(0, 5) as i:
                linear("aupa", stream, 0, i, normed=split_chunks("ass_ff"))
                linear("aupb", stream, 0, i)
            linear("aupc", stream)
            pe.wait_ge(S["ff_split"], NG)
            for g in range(2):
                linear(f"adn{g}", split(ffH, ffL))
            square_sum("ass_fin")

            with pe.Fori(0, LAYERS) as l:
                o = fill("bvecs", l)
                pe.wait_ge(S["layer_vecs_loaded"], l * (16 * 8) + 16 * 8)
                pe.transpose(o[:, 0:W_ROWS1], vrow[0:W_ROWS1, 0, :], ident[0:W_ROWS1, 0:W_ROWS1])
                pe.transpose(o[:, W_ROWS1:W_ROWS1 + W_ROWS2], vrow[0:W_ROWS2, 1, :], ident[0:W_ROWS2, 0:W_ROWS2])\
                  .then_inc(S["layer_vecs_turned"], 1)
                square_sum("bss_at", l)
                linear("bmix1", stream, l, normed=split_chunks("bss_at", l))
                linear("bmix2", stream, l, tokens=NB, cols=MIX2)
                pe.wait_ge(S["roped"], PRIMED + l * 5 + 1)
                pe.wait_ge(S["kk_copied"], l * 2 + 1)
                for b in range(1, NB):
                    o = fill(f"bix{b}", l)
                    n = (b + 1) * P
                    for h in range(4):
                        r0 = HD * (h % 2)
                        mm = pe.matmul(o[:, h * T:h * T + n], mix1[r0:r0 + HD, h // 2, b * P:b * P + P],
                                       kII[r0:r0 + HD, 0:n], start=True, stop=True)
                    mm.then_inc(S["index_dots"], 1)
                for name in ("bqB", "bqA", "bkA"):
                    linear(name, stream, l)
                o = fill("blf", l)
                read_out(pe, "bmix2", l)
                for b in range(NB):
                    mm = pe.transpose(o[0:H, b * P:b * P + P], mix2[:, b, MF:MF + H], ident)
                mm.then_inc(S["forget_turned"], 1)
                linear("bvA", stream, l, tokens=NB)
                o = fill("bft", l)
                pe.wait_ge(S["forget_sum"], l + 1)
                for b in range(NB):
                    if b == 0:
                        plain(pe)
                    mm = pe.transpose(o[:, b * H:b * H + H], fF[0:H, b * P:b * P + P], ident[0:H, 0:H])
                mm.then_inc(S["forget_turned"], 1)
                for g in range(2):
                    o = fill(f"bfb{g}", l)
                    for h in range(4):
                        mm = pe.matmul(o[:, h * T:h * T + T], onehot[0:H, 4 * g + h, :], fF[0:H, :], start=True, stop=True)
                    mm.then_inc(S["forget_spread"], 1)

                def attend(br, blocks, keys, values, after):
                    for name in after:
                        pe.wait_ge(drained[jobs.half[name[0]]], jobs.nth(name[0], l, name[1]))

                    def scores(i, p):
                        h = i * 2 + p
                        pe.wait_ge(S["heads_staged"], nth_head(br, l) + h + 1)
                        pe.wait_ge(S["heads_scores_read"], PRIMED + nth_head(br, l) + h)
                        for b, k0, n, at, _ in blocks:
                            mm = pe.matmul(ps[0][:, at:at + n], qz[:, p, b * P:b * P + P], keys(i, k0, n),
                                           start=True, stop=True)
                        mm.then_inc(S["heads_scores"], 1)

                    turned = turned_blocks(blocks)

                    def head(i, p, last):
                        h = i * 2 + p
                        pe.wait_ge(S["heads_probs"], nth_soft(br, l) + h + 1)
                        pe.wait_ge(S["heads_out_read"], PRIMED + nth_head(br, l) + h)
                        for n, (j, b, k0, at) in enumerate(turned):
                            mm = pe.transpose(ps[1][:, n * P:n * P + P],
                                              logit[:, p, at + j * P - k0:at + j * P - k0 + P], ident)
                        mm.then_inc(S["heads_turned"], 1)
                        if not last:
                            scores(i + 1, p)
                        pe.wait_ge(S["heads_turned_read"], nth_soft(br, l) + h + 1)
                        for b in range(NB):
                            mine = [(n, j) for n, (j, bb, _, _) in enumerate(turned) if bb == b]
                            for n, j in mine:
                                mm = pe.matmul(ps[1][:, 3 * T + b * HD:3 * T + b * HD + HD], probT[:, n * P:n * P + P],
                                               values(j, i, p), start=(n == mine[0][0]), stop=(n == mine[-1][0]))
                        mm.then_inc(S["heads_out"], 1)

                    scores(0, 0)
                    scores(0, 1)
                    with pe.Fori(0, 3) as i:
                        head(i, 0, False)
                        head(i, 1, False)
                    head(3, 0, True)
                    head(3, 1, True)
                    pe.wait_ge(S["heads_out_read"], PRIMED + nth_head(br, l) + H)

                def turn_out(name):
                    o = fill(name, l)
                    for c in range(NB):
                        for b in range(NB):
                            mm = pe.transpose(o[:, c * T + b * P:c * T + b * P + P], otm[:, b, c * P:c * P + P], ident)
                    mm.then_inc(S["y_turned"], 1)

                attend("fox", causal, lambda i, k0, n: K[:, ds(i, 1), k0:k0 + n].rearrange("p a b -> p (a b)"),
                       lambda j, i, p: V[:, j, ds(i * P + p * HD, HD)], (("btA", 0), ("btB", 0)))
                turn_out("btA")
                attend("dsa", causal, lambda i, k0, n: kBB[:, k0:k0 + n],
                       lambda j, i, p: mix2[:, j, MVB:MVB + HD], (("btB", 0), ("bqC", 0)))
                turn_out("btB")
                for name in ("bqC", "bkC"):
                    linear(name, stream, l)
                linear("bvC", stream, l, tokens=NB)

                for name in ("bgC", "btC"):
                    pe.wait_ge(drained[jobs.half[name]], jobs.nth(name, l))
                pe.wait_ge(S["roped"], PRIMED + l * 5 + 4)
                read_out(pe, "bvC", l)

                def ret_scores(i, p):
                    h = i * 2 + p
                    pe.wait_ge(S["heads_staged"], nth_head("ret", l) + h + 1)
                    pe.wait_ge(S["heads_scores_read"], PRIMED + nth_head("ret", l) + h)
                    for j, n, at, _ in forward:
                        mm = pe.matmul(ps[0][:, at:at + n], qz[:, p, j * P:j * P + P],
                                       Q[:, ds(i, 1), j * P:T].rearrange("p a b -> p (a b)"), start=True, stop=True)
                    mm.then_inc(S["heads_scores"], 1)

                def ret_out(i, p):
                    h = i * 2 + p
                    pe.wait_ge(S["heads_scores_read"], PRIMED + nth_head("ret", l) + h + 1)
                    pe.wait_ge(S["heads_out_read"], PRIMED + nth_head("ret", l) + h)
                    for b in range(NB):
                        for j in range(b + 1):
                            at = forward[j][3] + (b - j) * P
                            mm = pe.matmul(ps[1][:, 3 * T + b * HD:3 * T + b * HD + HD], logit[:, p, at:at + P],
                                           V[:, j, ds(i * P + p * HD, HD)], start=(j == 0), stop=(j == b))
                    mm.then_inc(S["heads_out"], 1)

                ret_scores(0, 0)
                with pe.Fori(0, 3) as i:
                    ret_scores(i, 1)
                    ret_out(i, 0)
                    ret_scores(i + 1, 0)
                    ret_out(i, 1)
                ret_scores(3, 1)
                ret_out(3, 0)
                ret_out(3, 1)
                pe.wait_ge(S["heads_out_read"], PRIMED + nth_head("ret", l) + H)
                linear("bgC", stream, l)
                pe.wait_ge(S["group_normed"], l + 1)
                turn_out("btC")
                linear("bqD", stream, l)
                pe.wait_ge(S["kk_copied"], l * 2 + 2)
                attend("swa", window, lambda i, k0, n: kDD[:, ds(i // 2, 1), k0:k0 + n].rearrange("p a b -> p (a b)"),
                       lambda j, i, p: mix2[:, j, ds(i // 2 * HD + MVD, HD)], (("btD", 0), ("bgt0", 0)))
                turn_out("btD")
                with pe.Fori(0, 2) as c:
                    for n, (high, rest) in enumerate(((yAH, yAL), (yBH, yBL), (yCH, yCL), (yDH, yDL))):
                        linear(f"bgt{n}", stream, l, c)
                        if n == 2:
                            pe.wait_ge(S["yc_split"], l + 1)
                        linear(f"bbr{n}", split(high, rest), l, c)
                pe.wait_ge(S["merged_b_split"], l * 2 + 2)
                for g in range(2):
                    linear(f"bwo{g}", halves(merged_bH, merged_bL), l)
                square_sum("bss_ff", l)
                with pe.Fori(0, 5) as i:
                    linear("bupa", stream, l, i, normed=split_chunks("bss_ff", l))
                    linear("bupb", stream, l, i)
                linear("bupc", stream, l)
                pe.wait_ge(S["ff_split"], NG + l * NG + NG)
                for g in range(2):
                    linear(f"bdn{g}", split(ffH, ffL), l)
            square_sum("css_fin")
            pe.wait_ge(S["normed"], WHOLE_NORMS["css_fin"])
            for g in range(2):
                o = fill(f"cout{g}")
                for b in range(NB):
                    for c in range(4):
                        mm = pe.transpose(o[:, b * T + c * P:b * T + c * P + P], hT[:, 4 * g + c, b * P:b * P + P], ident)
                mm.then_inc(S["out_turned"], 1)

        @block.scalar
        def _(act):
            link = Chain(act, S["act_step"])
            act.dma_start(consts[:, :], I["consts"][:, 0:N_CONSTS]).then_inc(S["consts_loaded"], 16)
            for at, key in ((V_MIX, "mix_norm_g"), (V_MEM, "mem_norm_g"), (V_XA, "xattn_norm_g"), (V_FF, "ffn_norm_g"),
                            (V_FIN, "final_norm_g"), (V_FIN2, "final_norm_2"), (V_D, "s5_d")):
                n = I[key].shape[-1] // P
                act.dma_start(vrow[at:at + n, 0, :], I[key].rearrange("(r p) -> r p", p=P)).then_inc(S["vecs_loaded"], 16)
            act.dma_start(row[0:32, 4, :], I["s5_lam_re"]).then_inc(S["s5_loaded"], 16)
            act.dma_start(row[0:32, 5, :], I["s5_lam_im"]).then_inc(S["s5_loaded"], 16)
            act.dma_start(row[0:32, 6, 0:2], I["s5_log_step"]).then_inc(S["s5_loaded"], 16)
            act.dma_start(mem_in, I["mem"].rearrange("(b p) d -> p b d", p=P)).then_inc(S["mem_loaded"], 16)

            def evac(dst, src, h, func=ACT.Copy, **kw):
                act.activation(dst, src, func, **kw).then_inc(drained[h], 1)

            def round_units(name, l, i, units, cols):
                for u in units:
                    s, p = ring.slot[(name, u)], ring.split[(name, u)]
                    act.wait_ge(landed[s], ring.at(ring.landed, name, u, l, i))
                    free = ring.at(ring.before, name, u, l, i) + ring.split_room[(name, u)]
                    if not isinstance(free, int) or free > 0:
                        act.wait_ge(weights_used, free)
                    act.activation(wH[:, p, 0:cols], slot[:, s, 0:cols], ACT.Copy).then_inc(weights_high, 1)

            def ahead(name, l=0, i=0, cols=512):
                round_units(name, l, i, range(SPLITS), cols)

            def others(name, l=0, i=0, cols=512):
                round_units(name, l, i, range(SPLITS, ring.units[name]), cols)

            def square(name):
                if name == "ass_mem":
                    act.activation(A(8192, KD, M), mT, ACT.Square).then_inc(S["squared"], 1)
                else:
                    act.activation(sq, hT[:, :, :], ACT.Square).then_inc(S["squared"], 1)

            def root(name, l=0, n=T):
                act.wait_ge(S["summed"], nth_norm(name, l))
                evac(rms[:, 0:n], ps[jobs.half[name]][:, 0:n], jobs.half[name], ACT.Sqrt, bias=eps, scale=1.0 / D)

            def round_norm(name, l=0):
                for k in range(KD):
                    act.wait_ge(S["normed_chunk"], split_chunks(name, l) + k + 1)
                    act.activation(nH[:, k, :], sq[:, k, :], ACT.Copy).then_inc(S["normed_high"], 1)

            act.wait_ge(S["vecs_turned"], 1)
            evac(vec0[:, :], ps[jobs.half["avecs"]][:, 0:V_ROWS], jobs.half["avecs"])
            for g in range(2):
                act.wait_ge(S["x_turned"], g + 1)
                evac(hT[:, 4 * g:4 * g + 4, :], banks(jobs.half[f"ax{g}"]), jobs.half[f"ax{g}"])
            act.wait_ge(S["mem_turned"], 1)
            h = jobs.half["amemT"]
            evac(mT, ps[h][:, :].rearrange("p (c m) -> p c m", m=M), h)
            read_out(act, "amemT")
            square("ass_mem")
            read_out(act, "ax0")
            read_out(act, "ax1")
            square("ass_mix")
            act.wait_ge(S["constants_set"], 2)
            root("ass_mem", n=M)
            ahead("axa")
            act.wait_ge(S["normed"], WHOLE_NORMS["ass_mem"])
            root("ass_mix")
            round_norm("ass_mix")
            others("axa")

            R = [row[0:32, n, :] for n in range(24)]
            act.wait_ge(S["s5_loaded"], 48)
            act.activation(row[0:32, 7, 0:2], row[0:32, 6, 0:2], ACT.Exp).then_inc(S["s5_step"], 1)
            act.wait_ge(S["s5_exponent"], 1)
            act.activation(R[0], R[10], ACT.Exp).then_inc(S["s5_magnitude"], 1)
            act.wait_ge(S["s5_phase"], 1)
            link(act.activation(R[11], R[1], ACT.Abs))
            act.activation(R[12], R[1], ACT.Sin, scale=TWO_PI).then_inc(S["s5_circle"], 1)
            act.activation(R[13], R[11], ACT.Sin, bias=half_pi[0:32, :], scale=-TWO_PI).then_inc(S["s5_circle"], 1)
            done(act, "axa")
            evac(uT, banks(jobs.half["axa"]), jobs.half["axa"])
            act.wait_ge(S["s5_turned"], 1)
            h = jobs.half["as5col"]
            link(act.activation(s5col[:, :, :], ps[h][:, 0:4 * 32].rearrange("p (a b) -> p a b", b=32), ACT.Copy))
            evac(s5col[:, 1, 16:32], ps[h][:, 32 + 16:64], h, scale=-1.0)
            act.wait_ge(S["s5_turned"], 2)
            h = jobs.half["as5B"]
            evac(s5w[:, :, 0:2, :], ps[h][:, :].rearrange("p (q k s) -> p q k s", q=QUADS, k=2), h)
            act.wait_ge(S["s5_turned"], 3)
            h = jobs.half["as5C"]
            c_re, c_im = (ps[h][:, :].rearrange("p (q k s) -> p q k s", q=QUADS, k=2)[:, :, k, :] for k in range(2))
            act.activation(s5w[:, :, 2, :], c_re, ACT.Copy)
            act.activation(s5w[:, :, 3, :], c_re, ACT.Copy, scale=-1.0)
            evac(s5w[:, :, 4, :], c_im, h, scale=-1.0)
            read_out(act, "axa")
            read_out(act, "as5B")
            read_out(act, "as5C")
            read_out(act, "as5col")
            act.wait_ge(S["s5_bbar"], 1)
            act.wait_ge(S["iota_loaded"], 16)
            ahead("aglu")
            with act.Fori(0, 4) as c:
                act.wait_ge(S["s5_out"], PRIMED + c * 8)
                act.activation(ust, uT[:, ds(c, 1), :].rearrange("p a b -> p (a b)"), ACT.Copy)
                for d in range(2):
                    act.activation(stg[:, d, :], s5w[:, ds(c + 4 * d, 1), :, :].rearrange("p q a b -> p (q a b)"), ACT.Copy)\
                        .then_inc(S["s5_staged"], 1)

                def turns(t):
                    act.activation(turn[:, t % 2, :], rms[:, :], ACT.Copy, scale=s5col[:, 1, ds(c * 4 + (t // 4 * 16 + t % 4), 1)])\
                        .then_inc(S["s5_turns"], 1)

                turns(0)
                turns(1)
                for t in range(8):
                    p = t % 2
                    act.wait_ge(S["s5_fraction"], c * 8 + t + 1)
                    act.activation(whole[:, p, :], turn[:, p, :], ACT.Abs).then_inc(S["s5_abs"], 1)
                    if t >= 4:
                        act.wait_ge(S["s5_back_dve"], c * 8 + t - 3)
                        act.wait_ge(S["s5_back_pool"], PRIMED + c * 8 + t - 3)
                    act.activation(trig[:, t % 4, 1, :], turn[:, p, :], ACT.Sin, scale=TWO_PI)
                    act.wait_ge(S["s5_abs"], c * 8 + t + 1)
                    act.activation(trig[:, t % 4, 0, :], whole[:, p, :], ACT.Sin, bias=half_pi, scale=-TWO_PI)\
                        .then_inc(S["s5_trig"], 1)
                    if t < 6:
                        act.wait_ge(S["s5_trig"], c * 8 + t + 1)
                        turns(t + 2)
            act.wait_ge(S["s5_y_read"], PRIMED + 4)
            act.activation(uT, uT, ACT.Gelu_apprx_tanh).then_inc(S["s5_gelu"], 1)
            act.wait_ge(S["s5_gelu"], 1)
            act.activation(yH, uT, ACT.Copy).then_inc(S["ya_high"], 1)
            ahead("azu0")
            done(act, "aglu")
            evac(svt, banks(jobs.half["aglu"]), jobs.half["aglu"], ACT.Sigmoid)
            others("azu0")
            act.wait_ge(S["ya_ready"], 1)
            act.activation(yH, uT, ACT.Copy).then_inc(S["ya_high"], 1)

            ahead("azu1")
            done(act, "azu0")
            evac(zu[:, 0:4, :], banks(jobs.half["azu0"]), jobs.half["azu0"], ACT.Gelu_apprx_tanh)
            others("azu1")
            ahead("azv0")
            done(act, "azu1")
            evac(zu[:, 4:8, :], banks(jobs.half["azu1"]), jobs.half["azu1"], ACT.Gelu_apprx_tanh)
            others("azv0")
            act.wait_ge(S["ya_split"], 2)
            act.activation(mH, mT, ACT.Copy).then_inc(S["mem_high"], 1)
            ahead("azv1")
            done(act, "azv0")
            evac(zv[:, :, 0:512], banks(jobs.half["azv0"]), jobs.half["azv0"], ACT.Gelu_apprx_tanh)
            others("azv1")
            ahead("aga")
            done(act, "azv1")
            evac(zv[:, :, 512:1024], banks(jobs.half["azv1"]), jobs.half["azv1"], ACT.Gelu_apprx_tanh)
            act.wait_ge(S["ws_turned"], 1)
            h = jobs.half["awsT"]
            evac(wsT, ps[h][:, 0:H * P].rearrange("p (a b) -> p a b", b=P), h)
            act.wait_ge(S["zv_stats"], 1)
            act.activation(stat[:, 56:60], stat[:, 48:56].rearrange("p (a b) -> p a b", b=2)[:, :, 1], ACT.Sqrt, bias=eps)\
               .then_inc(S["zv_std"], 1)
            act.wait_ge(S["yb_ready"], 2)
            for g in range(2):
                act.activation(zuH[:, 4 * g:4 * g + 4, :], zu[:, 4 * g:4 * g + 4, :], ACT.Copy).then_inc(S["yb_high"], 1)
            with act.Fori(0, 2) as c:
                others("aga", 0, c)
                ahead("apa", 0, c)
                for n, (key, then) in enumerate((("ga", "gb"), ("gb", None))):
                    done(act, "a" + key, 0, c)
                    act.wait_ge(drained[jobs.half["apa"]], jobs.nth("apa", 0, c) + (n - 1))
                    h = jobs.half["a" + key]
                    evac(gate_a[n], banks(h), h, ACT.Sigmoid)
                    if n == 0:
                        ahead("agb", 0, c)
                        others("agb", 0, c)
                        ahead("apb", 0, c)
                others("apb", 0, c)
                ahead("aga", 0, c + 1)
            for c in range(2):
                act.wait_ge(S["merged_a"], c + 1)
                act.activation(merged_aH[c], merged_a[:, 4 * c:4 * c + 4, :], ACT.Copy).then_inc(S["merged_a_high"], 1)
            others("awo0")
            ahead("awo1")
            others("awo1")

            ahead("awk0")
            others("awk0")
            read_out(act, "awo0")
            read_out(act, "awo1")
            square("ass_xa")
            ahead("awk1")
            done(act, "awk0")
            evac(xk[:, 0:4, :], banks(jobs.half["awk0"], w=M), jobs.half["awk0"])
            others("awk1")
            ahead("awv0")
            done(act, "awk1")
            evac(xk[:, 4:8, :], banks(jobs.half["awk1"], w=M), jobs.half["awk1"])
            others("awv0")
            ahead("awv1")
            done(act, "awv0")
            evac(xv[:, :, 0:512], banks(jobs.half["awv0"], n=2), jobs.half["awv0"])
            others("awv1")
            ahead("awq0")
            done(act, "awv1")
            evac(xv[:, :, 512:1024], banks(jobs.half["awv1"], n=2), jobs.half["awv1"])
            root("ass_xa")
            round_norm("ass_xa")
            others("awq0")
            ahead("awq1")
            done(act, "awq0")
            evac(xq[:, 0:4, :], banks(jobs.half["awq0"]), jobs.half["awq0"])
            others("awq1")
            ahead("axo0")
            done(act, "awq1")
            evac(xq[:, 4:8, :], banks(jobs.half["awq1"]), jobs.half["awq1"])

            def x_exp(h):
                act.wait_ge(S["x_max"], h + 1)
                p, half = h % 2, jobs.half[f"axs{h}"]
                for b in range(NB):
                    ins = act.activation(xp[:, p, b, :], ps[half][:, b * M:b * M + M], ACT.Exp, scale=float((D // 4) ** -0.5),
                                         bias=stat[:, 64 + 4 * p + b:65 + 4 * p + b], accum_out=stat[:, 72 + 4 * p + b:73 + 4 * p + b])
                ins.then_inc(drained[half], 1)

            def x_turned(h):
                act.wait_ge(S["x_probs_turned"], h + 1)
                evac(xpT[:, h % 2, :, :], banks(jobs.half[f"axt{h}"], n=2), jobs.half[f"axt{h}"])

            def x_outs(h):
                act.wait_ge(S["x_out"], h + 1)
                act.activation(xoH[:, 2 * h:2 * h + 2, :], banks(jobs.half[f"axv{h}"], n=2), ACT.Copy).then_inc(S["xo_high"], 1)

            x_exp(0)
            x_exp(1)
            x_turned(0)
            x_exp(2)
            x_outs(0)
            x_turned(1)
            x_exp(3)
            x_outs(1)
            for h in (2, 3):
                x_turned(h)
                x_outs(h)
            others("axo0")
            ahead("axo1")
            others("axo1")
            ahead("aupa")
            read_out(act, "axo0")
            read_out(act, "axo1")
            square("ass_ff")
            root("ass_ff")
            round_norm("ass_ff")

            def round_ff(raw, g):
                act.activation(ffH[:, ds(g * 2, 2), :], raw, ACT.Copy).then_inc(S["ff_high"], 1)

            def round_ff_a(name, g, p, i=0):
                read_out(act, name, 0, i)
                round_ff(ff_raw[:, p, :, :], g)

            def silu_a(name, p, i=0):
                done(act, name, 0, i)
                act.activation(sg_a[:, p, :, :], banks(jobs.half[name], n=2), ACT.Silu).then_inc(S["silu_a"], 1)

            with act.Fori(0, 5) as i:
                others("aupa", 0, i)
                ahead("aupb", 0, i)
                silu_a("aupa", 0, i)
                others("aupb", 0, i)
                round_ff_a("aupa", i * 2, 0, i)
                ahead("aupa", 0, i + 1)
                silu_a("aupb", 1, i)
                round_ff_a("aupb", i * 2 + 1, 1, i)
            others("aupc")
            ahead("adn0")
            silu_a("aupc", 0)
            round_ff_a("aupc", NG - 1, 0)
            others("adn0")
            ahead("adn1")
            others("adn1")
            read_out(act, "adn0")
            read_out(act, "adn1")
            square("ass_fin")
            root("ass_fin")
            act.wait_ge(S["normed"], WHOLE_NORMS["ass_fin"])

            with act.Fori(0, LAYERS) as l:
                act.wait_ge(S["layer_vecs_turned"], l + 1)
                h = jobs.half["bvecs"]
                evac(vec[:, :], ps[h][:, 0:W_ROWS1 + W_ROWS2], h)
                last = "bdn1"
                act.wait_ge(drained[jobs.half[last]], jobs.nth(last, l) - (jobs.nth(last, 1) - jobs.nth(last, 0)) + 1)
                square("bss_at")
                ahead("bmix1", l)
                root("bss_at", l)
                round_norm("bss_at", l)

                def rope_read(name, dst, turn_no):
                    done(act, name, l)
                    act.wait_ge(S["roped"], PRIMED + l * 5 + turn_no)
                    h = jobs.half[name]
                    act.activation(dst, banks(h), ACT.Copy)
                    for r in range(0, P, 32):
                        ins = act.activation(part[r:r + 32, :, :], banks(h)[r ^ 32:(r ^ 32) + 32, :, :], ACT.Copy)
                    ins.then_inc(drained[h], 1)

                others("bmix1", l)
                ahead("bmix2", l, cols=MIX2)
                rope_read("bmix1", mix1, 0)
                others("bmix2", l, cols=MIX2)
                ahead("bqB", l)
                done(act, "bmix2", l)
                h = jobs.half["bmix2"]
                evac(mix2, banks(h, w=MIX2), h)
                act.wait_ge(S["roped"], PRIMED + l * 5 + 1)
                for r in (0, HD):
                    act.activation(kBB[r:r + HD, :], mix1[0:HD, 2, :], ACT.Copy)
                    ins = act.activation(kII[r:r + HD, :], mix1[HD:P, 2, :], ACT.Copy)
                ins.then_inc(S["kk_copied"], 1)
                for b in range(1, NB):
                    act.wait_ge(S["index_dots"], l * 3 + b)
                    act.wait_ge(S["index_scored"], PRIMED + l * 3 + b - 1)
                    h = jobs.half[f"bix{b}"]
                    evac(relu[:, :, 0:(b + 1) * P], banks(h, w=(b + 1) * P), h, ACT.Relu)
                others("bqB", l)
                ahead("bqA", l)
                rope_read("bqB", qB, 1)
                others("bqA", l)
                ahead("bkA", l)
                done(act, "bqA", l)
                evac(Q, banks(jobs.half["bqA"]), jobs.half["bqA"])
                others("bkA", l)
                ahead("bvA", l)
                done(act, "bkA", l)
                evac(K, banks(jobs.half["bkA"]), jobs.half["bkA"])
                act.wait_ge(S["forget_turned"], l * 2 + 1)
                h = jobs.half["blf"]
                evac(fx[0:H, :], ps[h][0:H, 0:T], h, ACT.Identity, bias=fbias[0:H, :])
                read_out(act, "blf", l)
                steps = Chain(act, S["forget_step"], l * 2)
                steps(act.activation(fe[0:H, :], fx[0:H, :], ACT.Abs))
                steps(act.activation(fe[0:H, :], fe[0:H, :], ACT.Exp, scale=-1.0))
                act.activation(fe[0:H, :], fe[0:H, :], ACT.Ln, bias=ones[0:H, 0:1]).then_inc(S["forget_log"], 1)
                others("bvA", l)
                ahead("bqC", l)
                done(act, "bvA", l)
                evac(V, banks(jobs.half["bvA"]), jobs.half["bvA"])
                act.wait_ge(S["forget_turned"], l * 2 + 2)
                h = jobs.half["bft"]
                evac(ftm[:, :, :], ps[h][:, 0:NB * H].rearrange("p (b h) -> p b h", h=H), h)
                for g in range(2):
                    act.wait_ge(S["forget_spread"], l * 2 + g + 1)
                    h = jobs.half[f"bfb{g}"]
                    evac(fb[:, 4 * g:4 * g + 4, :], banks(h), h)

                def stage(br, src, i, p, scale=HD ** -0.5):
                    act.activation(qz[HD * p:HD * p + HD, p, :], src[HD * p:HD * p + HD, ds(i, 1), :]
                                   .rearrange("p a b -> p (a b)"), ACT.Copy, scale=scale).then_inc(S["heads_staged"], 1)

                def attend(br, blocks, src, sinks=False):
                    def exps(i, p):
                        h = i * 2 + p
                        act.wait_ge(S["heads_scores_read"], PRIMED + nth_head(br, l) + h + 1)
                        if sinks:
                            act.activation(stat[:, 88 + 4 * p:92 + 4 * p], stat[:, 64 + 4 * p:68 + 4 * p], ACT.Exp,
                                           bias=sink[:, ds(h, 1)])
                        for b, _, n, _, at in blocks:
                            ins = act.activation(logit[:, p, at:at + n], logit[:, p, at:at + n], ACT.Exp,
                                                 bias=stat[:, 64 + 4 * p + b:65 + 4 * p + b],
                                                 accum_out=stat[:, 72 + 4 * p + b:73 + 4 * p + b])
                        ins.then_inc(S["heads_probs"], 1)

                    n = len(turned_blocks(blocks)) * P

                    def head(i, p, last):
                        h = i * 2 + p
                        if not last:
                            act.wait_ge(S["heads_scores"], nth_head(br, l) + h + 1)
                            stage(br, src, i + 1, p)
                        act.wait_ge(S["heads_turned"], nth_soft(br, l) + h + 1)
                        act.activation(probT[:, 0:n], ps[1][:, 0:n], ACT.Copy).then_inc(S["heads_turned_read"], 1)
                        if p == 0:
                            exps(i, 1)
                        elif not last:
                            exps(i + 1, 0)

                    stage(br, src, 0, 0)
                    stage(br, src, 0, 1)
                    exps(0, 0)
                    with act.Fori(0, 3) as i:
                        head(i, 0, False)
                        head(i, 1, False)
                    head(3, 0, True)
                    head(3, 1, True)

                def turn_out(name, k, high):
                    act.wait_ge(S["y_turned"], l * 4 + k)
                    act.activation(high, banks(jobs.half[name]), ACT.Copy).then_inc(S["y_high"], 1)

                read_out(act, "bqA", l)
                attend("fox", causal, Q)
                turn_out("btA", 1, yAH)
                act.wait_ge(S["roped"], PRIMED + l * 5 + 2)
                attend("dsa", causal, qB)
                turn_out("btB", 2, yBH)
                others("bqC", l)
                ahead("bkC", l)
                rope_read("bqC", Q, 2)
                others("bkC", l)
                ahead("bvC", l)
                rope_read("bkC", K, 3)
                others("bvC", l)
                ahead("bgC", l)
                done(act, "bvC", l)
                evac(V, banks(jobs.half["bvC"]), jobs.half["bvC"])

                def ret_stage(i, p):
                    h = i * 2 + p
                    stage("ret", K, i, p)
                    act.activation(decay[:, p, :], C["dist"], ACT.Exp, scale=C["logdecay"][:, ds(h, 1)])\
                        .then_inc(S["ret_decay"], 1)

                def ret_head(i, p, last):
                    h = i * 2 + p
                    if not last:
                        act.wait_ge(S["heads_scores"], nth_head("ret", l) + h + 1)
                        act.wait_ge(S["heads_scores_read"], PRIMED + nth_head("ret", l) + h + 1)
                        ret_stage(i + 1, p)
                    act.wait_ge(S["heads_out"], nth_head("ret", l) + h + 1)
                    act.activation(otm[:, :, ds(i * P + p * HD, HD)], ps[1][:, 3 * T:3 * T + NB * HD]
                                   .rearrange("p (b d) -> p b d", d=HD), ACT.Copy).then_inc(S["heads_out_read"], 1)

                act.wait_ge(S["roped"], PRIMED + l * 5 + 4)
                ret_stage(0, 0)
                ret_stage(0, 1)
                with act.Fori(0, 3) as i:
                    ret_head(i, 0, False)
                    ret_head(i, 1, False)
                ret_head(3, 0, True)
                ret_head(3, 1, True)
                act.wait_ge(S["group_centred"], l + 1)
                act.activation(gsq, otm, ACT.Square).then_inc(S["group_squared"], 1)
                act.wait_ge(S["group_var"], l + 1)
                act.activation(stat[:, 0:32], stat[:, 32:64], ACT.Sqrt, bias=eps, scale=1.0 / HD).then_inc(S["group_std"], 1)
                others("bgC", l)
                ahead("bqD", l)
                done(act, "bgC", l)
                evac(gC, banks(jobs.half["bgC"]), jobs.half["bgC"], ACT.Silu)
                others("bqD", l)
                read_out(act, "btC", l)
                act.activation(yCH, gC, ACT.Copy).then_inc(S["y_high"], 1)
                ahead("bgt0", l)
                rope_read("bqD", qD, 4)
                for g in range(2):
                    for r in (0, HD):
                        ins = act.activation(kDD[r:r + HD, g, :], mix1[HD * g:HD * g + HD, 3, :], ACT.Copy)
                ins.then_inc(S["kk_copied"], 1)
                act.wait_ge(S["roped"], PRIMED + l * 5 + 5)
                attend("swa", window, qD, sinks=True)
                turn_out("btD", 4, yDH)

                with act.Fori(0, 2) as c:
                    for n in range(4):
                        others(f"bgt{n}", l, c)
                        ahead(f"bbr{n}", l, c)
                        done(act, f"bgt{n}", l, c)
                        act.wait_ge(drained[jobs.half["bbr0"]], jobs.nth("bbr0", l, c) + (n - 1))
                        h = jobs.half[f"bgt{n}"]
                        evac(gate_b[n % 2], banks(h), h, ACT.Sigmoid)
                        if n < 3:
                            ahead(f"bgt{n + 1}", l, c)
                    ahead("bgt0", l, c + 1)
                for c in range(2):
                    act.wait_ge(S["merged_b"], PRIMED + l * 6 + 3 * c + 3)
                    act.activation(merged_bH[c], merged_b[:, 4 * c:4 * c + 4, :], ACT.Copy).then_inc(S["merged_b_high"], 1)
                others("bwo0", l)
                ahead("bwo1", l)
                others("bwo1", l)
                ahead("bupa", l)
                read_out(act, "bwo0", l)
                read_out(act, "bwo1", l)
                square("bss_ff")
                root("bss_ff", l)
                round_norm("bss_ff", l)

                def conv_group(name, g, p, i=0):
                    done(act, name, l, i)
                    act.wait_ge(S["ff_split"], NG + l * NG + g - 1)
                    h = jobs.half[name]
                    for j in range(4):
                        ch = g * 2 + (j if j < 2 else NF + j - 2)
                        ins = act.activation(conv[:, p, j, :], ps[h][:, j * T:j * T + T], ACT.Identity,
                                             scale=vec[:, ds(ch + W_C2, 1)], bias=vec[:, ds(ch + W_CB, 1)])
                    ins.then_inc(S["conv_begun"], 1)
                    read_out(act, name, l, i)
                    act.activation(conv[:, p, 0:2, :], conv[:, p, 0:2, :], ACT.Silu).then_inc(S["silu_b"], 1)

                def round_ff_b(g, p):
                    act.wait_ge(S["ff_ready"], l * NG + g + 1)
                    round_ff(conv[:, p, 0:2, :], g)

                with act.Fori(0, 5) as i:
                    others("bupa", l, i)
                    ahead("bupb", l, i)
                    conv_group("bupa", i * 2, 0, i)
                    others("bupb", l, i)
                    round_ff_b(i * 2, 0)
                    ahead("bupa", l, i + 1)
                    conv_group("bupb", i * 2 + 1, 1, i)
                    round_ff_b(i * 2 + 1, 1)
                others("bupc", l)
                ahead("bdn0", l)
                conv_group("bupc", NG - 1, 0)
                round_ff_b(NG - 1, 0)
                others("bdn0", l)
                ahead("bdn1", l)
                others("bdn1", l)
            read_out(act, "bdn0", LAYERS - 1)
            read_out(act, "bdn1", LAYERS - 1)
            square("css_fin")
            root("css_fin")
            for g in range(2):
                act.wait_ge(S["out_turned"], g + 1)
                h = jobs.half[f"cout{g}"]
                evac(o_out[:, :, 512 * g:512 * g + 512], banks(h), h)

        @block.vector
        def _(dve):
            link = Chain(dve, S["dve_step"])
            for name in ("heads_scores_read", "heads_out_read", "s5_y_read", "roped", "index_scored", "merged_b"):
                dve.sem_inc(S[name], PRIMED)
            dve.memset(eps, EPS).then_inc(S["constants_set"], 1)
            dve.memset(half_pi, float(np.pi / 2)).then_inc(S["constants_set"], 1)

            def inverse_root(name, l=0, n=T):
                read_out(dve, name, l)
                dve.reciprocal(rms[:, 0:n], rms[:, 0:n]).then_inc(S["rstd"], 1)
                dve.wait_ge(S["rstd"], nth_norm(name, l))

            def norm(name, buf, gains, n=T):
                inverse_root(name, 0, n)
                for k in range(KD):
                    ins = dve.scalar_tensor_tensor(out=buf[:, k, :], in0=buf[:, k, :], scalar=gains[:, k:k + 1],
                                                   in1=rms[:, 0:n], op0=ALU.mult, op1=ALU.mult)
                ins.then_inc(S["normed"], 1)

            def split_norm(name, gains, l=0):
                inverse_root(name, l)
                first = split_chunks(name, l)

                def whole_chunk(k):
                    dve.scalar_tensor_tensor(out=sq[:, k, :], in0=hT[:, k, :], scalar=gains[:, k:k + 1], in1=rms[:, :],
                                             op0=ALU.mult, op1=ALU.mult).then_inc(S["normed_chunk"], 1)

                whole_chunk(0)
                whole_chunk(1)
                for k in range(KD):
                    dve.wait_ge(S["normed_high"], first + k + 1)
                    dve.tensor_tensor(nL[:, k, :], sq[:, k, :], plainly(nH[:, k, :]), ALU.subtract).then_inc(S["normed_split"], 1)
                    if k + 2 < KD:
                        whole_chunk(k + 2)

            def rest(part, whole_value, high):
                return dve.tensor_tensor(part, whole_value, plainly(high), ALU.subtract)

            def add_back(name, g, l=0):
                done(dve, name, l)
                h = jobs.half[name]
                dve.tensor_tensor(hT[:, 4 * g:4 * g + 4, :], hT[:, 4 * g:4 * g + 4, :], banks(h), ALU.add)\
                   .then_inc(drained[h], 1)

            def wide(v, n):
                return v.unsqueeze(2).to_broadcast([v.shape[0], v.shape[1], n])

            read_out(dve, "avecs")
            norm("ass_mem", mT, vec0[:, V_MEM:V_MEM + KD], n=M)
            split_norm("ass_mix", vec0[:, V_MIX:V_MIX + KD])

            R = [row[0:32, n, :] for n in range(24)]
            lre, lim, lr, theta, k, r, sin, cos, nr, li, den, t1, t2 = (R[n] for n in (4, 5, 10, 8, 9, 1, 12, 13, 14, 15, 16, 17, 18))
            step = row[0:32, 7, 0:2].unsqueeze(2).to_broadcast([32, 2, STATE])

            def halves(v):
                return v.rearrange("p (g s) -> p g s", s=STATE)

            dve.wait_ge(S["s5_loaded"], 48)
            dve.wait_ge(S["s5_step"], 1)
            dve.tensor_tensor(halves(lr), halves(lre), step, ALU.mult).then_inc(S["s5_exponent"], 1)
            link(dve.tensor_tensor(halves(theta), halves(lim), step, ALU.mult))
            link(dve.tensor_scalar(k, theta, INV_2PI, ROUND, ALU.mult, ALU.add))
            link(dve.tensor_scalar(k, k, ROUND, None, ALU.subtract))
            link(dve.scalar_tensor_tensor(out=t1, in0=k, scalar=-C1, in1=theta, op0=ALU.mult, op1=ALU.add))
            link(dve.scalar_tensor_tensor(out=t2, in0=k, scalar=-C2, in1=t1, op0=ALU.mult, op1=ALU.add))
            dve.tensor_scalar(r, t2, INV_2PI, None, ALU.mult).then_inc(S["s5_phase"], 1)
            link(dve.tensor_tensor(t1, lre, lre, ALU.mult))
            link(dve.tensor_tensor(t2, lim, lim, ALU.mult))
            link(dve.tensor_tensor(den, t1, t2, ALU.add))
            link(dve.reciprocal(den, den))
            dve.wait_ge(S["s5_magnitude"], 1)
            dve.wait_ge(S["s5_circle"], 2)
            link(dve.tensor_tensor(nr, R[0], cos, ALU.mult))
            link(dve.tensor_scalar(nr, nr, 1.0, None, ALU.subtract))
            link(dve.tensor_tensor(li, R[0], sin, ALU.mult))
            link(dve.tensor_tensor(t1, nr, lre, ALU.mult))
            link(dve.tensor_tensor(t2, li, lim, ALU.mult))
            link(dve.tensor_tensor(t1, t1, t2, ALU.add))
            link(dve.tensor_tensor(R[2], t1, den, ALU.mult))
            link(dve.tensor_tensor(t1, li, lre, ALU.mult))
            link(dve.tensor_tensor(t2, nr, lim, ALU.mult))
            link(dve.tensor_tensor(t1, t1, t2, ALU.subtract))
            dve.tensor_tensor(R[3], t1, den, ALU.mult).then_inc(S["s5_params"], 1)
            read_out(dve, "as5col")
            dve.wait_ge(S["s5b_loaded"], 32)
            f_re, f_im = (wide(s5col[:, n, :], CHAN) for n in (2, 3))
            for n, (b, f) in enumerate(((0, f_re), (1, f_im), (1, f_re), (0, f_im))):
                link(dve.tensor_tensor(bprod[n], bnat[b], f, ALU.mult))
            dve.wait_ge(S["zeros_set"], 5)
            for g in range(2):
                at, ch = slice(STATE * g, STATE * g + STATE), slice(CHAN * g, CHAN * g + CHAN)
                dve.tensor_tensor(zb[0][at, :, ch], bprod[0][at], bprod[1][at], ALU.subtract)
                ins = dve.tensor_tensor(zb[1][at, :, ch], bprod[2][at], bprod[3][at], ALU.add)
            ins.then_inc(S["s5_bbar"], 1)

            read_out(dve, "as5C")
            read_out(dve, "axa")
            with dve.Fori(0, 4) as c:
                def nearest(t):
                    dve.wait_ge(S["s5_turns"], c * 8 + t + 1)
                    dve.tensor_scalar(whole[:, t % 2, :], turn[:, t % 2, :], ROUND, ROUND, ALU.add, ALU.subtract)\
                       .then_inc(S["s5_whole"], 1)

                def rotate(t):
                    p = t % 2
                    dve.wait_ge(S["s5_driven"], c * 8 + t + 1)
                    dve.wait_ge(S["s5_trig"], c * 8 + t + 1)
                    dve.wait_ge(S["s5_out"], PRIMED + c * 8 + (t - 1 if t >= 2 else 0))
                    for n, (b, f) in enumerate(((0, 0), (1, 1), (1, 0), (0, 1))):
                        ins = dve.tensor_tensor(prod[:, p, n, :], ps[0][:, (2 * p + b) * T:(2 * p + b + 1) * T],
                                                trig[:, t % 4, f, :], ALU.mult)
                    ins.then_inc(S["s5_rotated"], 1)

                def scan(t):
                    p, d = t % 2, t // 4
                    dve.wait_ge(S["s5_z"], c * 8 + t + 1)
                    dve.wait_ge(S["s5_back_pool"], PRIMED + c * 8 + (t - 1 if t >= 2 else 0))
                    decay_rate = s5col[:, 0, ds(c * 4 + (d * 16 + t % 4), 1)].to_broadcast([P, T])
                    for n in range(2):
                        o, z = st[:, p, n, :], zt[:, p, n, :]
                        if d:
                            o, z = o[:, ::-1], z[:, ::-1]
                        ins = dve.tensor_tensor_scan(o, decay_rate, z, 0.0, ALU.mult, ALU.add).then_inc(S["s5_scanned"], 1)
                    dve.wait_ge(S["s5_scanned"], c * 16 + 2 * t + 2)
                    for n in range(2):
                        ins = dve.tensor_tensor(prod[:, p, n, :], st[:, p, n, :], trig[:, t % 4, n, :], ALU.mult)
                    ins.then_inc(S["s5_back_dve"], 1)

                nearest(0)
                nearest(1)
                for t in range(8):
                    rotate(t)
                    if t < 6:
                        nearest(t + 2)
                    if t:
                        scan(t - 1)
                scan(7)
                dve.wait_ge(S["s5_out"], PRIMED + c * 8 + 8)
                dve.scalar_tensor_tensor(out=uT[:, ds(c, 1), :].rearrange("p a b -> p (a b)"),
                                         in0=uT[:, ds(c, 1), :].rearrange("p a b -> p (a b)"),
                                         scalar=vec0[:, ds(c + V_D, 1)], in1=ps[1][:, 0:T], op0=ALU.mult, op1=ALU.add)\
                   .then_inc(S["s5_y_read"], 1)
            dve.wait_ge(S["ya_high"], 1)
            rest(yL, uT, yH).then_inc(S["ya_split"], 1)
            read_out(dve, "aglu")
            dve.tensor_tensor(uT, uT, svt, ALU.mult).then_inc(S["ya_ready"], 1)
            dve.wait_ge(S["ya_ready"], 1)
            dve.wait_ge(S["ya_high"], 2)
            rest(yL, uT, yH).then_inc(S["ya_split"], 1)
            dve.wait_ge(S["mem_high"], 1)
            rest(mL, mT, mH).then_inc(S["mem_split"], 1)

            read_out(dve, "azv0")
            read_out(dve, "azv1")
            for b in range(NB):
                for g in range(2):
                    link(dve.bn_stats(stat[:, (2 * b + g) * 6:(2 * b + g) * 6 + 6], zv[:, b, 512 * g:512 * g + 512]))
            for b in range(NB):
                ins = dve.bn_aggr(stat[:, 48 + 2 * b:50 + 2 * b], stat[:, 12 * b:12 * b + 12])
            ins.then_inc(S["zv_stats"], 1)
            dve.wait_ge(S["zv_std"], 1)
            link(dve.reciprocal(stat[:, 56:60], stat[:, 56:60]))
            for b in range(NB):
                link(dve.tensor_scalar(zv[:, b, :], zv[:, b, :], stat[:, 48 + 2 * b:49 + 2 * b], stat[:, 56 + b:57 + b],
                                       ALU.subtract, ALU.mult))
            dve.wait_ge(S["sgu_loaded"], 64)
            link(dve.tensor_tensor(zv, zv, lng.unsqueeze(1).to_broadcast([P, NB, D]), ALU.mult))
            dve.tensor_tensor(zv, zv, lnb.unsqueeze(1).to_broadcast([P, NB, D]), ALU.add).then_inc(S["zv_normed"], 1)
            read_out(dve, "azu0")
            read_out(dve, "azu1")
            for g in range(2):
                dve.wait_ge(S["sv_done"], g + 1)
                half = jobs.half[f"asv{g}"]
                for h in range(4):
                    ins = dve.tensor_tensor(svt[:, h, :].rearrange("p (b t) -> p b t", t=P),
                                            ps[half][:, h * T:h * T + T].rearrange("p (b t) -> p b t", t=P),
                                            sgub[:, 4 * g + h, :].unsqueeze(1).to_broadcast([P, NB, P]), ALU.add)
                ins.then_inc(drained[half], 1)
                read_out(dve, f"asv{g}")
                dve.tensor_tensor(zu[:, 4 * g:4 * g + 4, :], zu[:, 4 * g:4 * g + 4, :], svt, ALU.mult).then_inc(S["yb_ready"], 1)
                dve.wait_ge(S["yb_ready"], g + 1)
            for g in range(2):
                dve.wait_ge(S["yb_high"], g + 1)
                half = slice(4 * g, 4 * g + 4)
                rest(zuL[:, half, :], zu[:, half, :], zuH[:, half, :]).then_inc(S["yb_split"], 1)

            dve.wait_ge(S["yb_split"], 2)
            with dve.Fori(0, 2) as c:
                read_out(dve, "aga", 0, c)
                done(dve, "apa", 0, c)
                h = jobs.half["apa"]
                dve.tensor_tensor(merged_a[:, ds(c * 4, 4), :], banks(h), gate_a[0], ALU.mult).then_inc(drained[h], 1)
                read_out(dve, "agb", 0, c)
                done(dve, "apb", 0, c)
                h = jobs.half["apb"]
                dve.tensor_tensor(gate_a[1], banks(h), gate_a[1], ALU.mult).then_inc(S["gated_a"], 1)
                dve.wait_ge(S["gated_a"], c + 1)
                dve.tensor_tensor(merged_a[:, ds(c * 4, 4), :], merged_a[:, ds(c * 4, 4), :], gate_a[1], ALU.add)\
                   .then_inc(S["merged_a"], 1)
                dve.wait_ge(S["merged_a"], c + 1)
                dve.sem_inc(drained[h], 1)
            for c in range(2):
                dve.wait_ge(S["merged_a_high"], c + 1)
                rest(merged_aL[:, 4 * c:4 * c + 4, :], merged_a[:, 4 * c:4 * c + 4, :], merged_aH[c]).then_inc(S["merged_a_split"], 1)
            for g in range(2):
                add_back(f"awo{g}", g)
            split_norm("ass_xa", vec0[:, V_XA:V_XA + KD])

            def x_max(h):
                half, p = jobs.half[f"axs{h}"], h % 2
                dve.wait_ge(S["x_scores"], h + 1)
                mx = stat[:, 64 + 4 * p:68 + 4 * p]
                link(dve.tensor_reduce(mx, ps[half][:, 0:NB * M].rearrange("p (b m) -> p b m", m=M), AXX, ALU.max))
                dve.tensor_scalar(mx, mx, -float((D // 4) ** -0.5), None, ALU.mult).then_inc(S["x_max"], 1)

            def x_norm(h):
                p = h % 2
                read_out(dve, f"axs{h}")
                link(dve.reciprocal(stat[:, 80 + 4 * p:84 + 4 * p], stat[:, 72 + 4 * p:76 + 4 * p]))
                dve.tensor_tensor(xp[:, p, :, :], xp[:, p, :, :], wide(stat[:, 80 + 4 * p:84 + 4 * p], M), ALU.mult)\
                   .then_inc(S["x_probs"], 1)

            x_max(0)
            x_max(1)

            def x_rest(h):
                dve.wait_ge(S["xo_high"], h + 1)
                half, two = jobs.half[f"axv{h}"], slice(2 * h, 2 * h + 2)
                rest(xoL[:, two, :], banks(half, n=2), xoH[:, two, :]).then_inc(drained[half], 1)

            x_norm(0)
            x_max(2)
            x_norm(1)
            x_rest(0)
            x_max(3)
            x_norm(2)
            x_rest(1)
            x_norm(3)
            x_rest(2)
            x_rest(3)
            for g in range(2):
                add_back(f"axo{g}", g)
            split_norm("ass_ff", vec0[:, V_FF:V_FF + KD])

            def ff_rest(raw, g, n):
                dve.wait_ge(S["ff_high"], n + 1)
                rest(ffL[:, ds(g * 2, 2), :], raw, ffH[:, ds(g * 2, 2), :]).then_inc(S["ff_split"], 1)

            def gate_up(name, g, p, i=0):
                dve.wait_ge(S["silu_a"], g + 1)
                h = jobs.half[name]
                dve.tensor_tensor(ff_raw[:, p, :, :], sg_a[:, p, :, :], banks(h)[:, 2:4, :], ALU.mult).then_inc(drained[h], 1)
                ff_rest(ff_raw[:, p, :, :], g, g)

            with dve.Fori(0, 5) as i:
                gate_up("aupa", i * 2, 0, i)
                gate_up("aupb", i * 2 + 1, 1, i)
            gate_up("aupc", NG - 1, 0)
            for g in range(2):
                add_back(f"adn{g}", g)
            norm("ass_fin", hT[:, :, :], vec0[:, V_FIN:V_FIN + KD])
            dve.wait_ge(S["normed"], WHOLE_NORMS["ass_fin"])

            with dve.Fori(0, LAYERS) as l:
                read_out(dve, "bvecs", l)
                split_norm("bss_at", vec[:, W_AT:W_AT + KD], l)

                def rope(name, buf, n):
                    read_out(dve, name, l)
                    turned = Chain(dve, S["rope_step"], l * 10 + n * 2)
                    cos, sin = (C[x].unsqueeze(1).to_broadcast([P, NB, T]) for x in ("cos", "sin"))
                    turned(dve.tensor_tensor(buf, buf, cos, ALU.mult))
                    turned(dve.tensor_tensor(part, part, sin, ALU.mult))
                    dve.tensor_tensor(buf, buf, part, ALU.add).then_inc(S["roped"], 1)
                    dve.wait_ge(S["roped"], PRIMED + l * 5 + n + 1)

                rope("bmix1", mix1, 0)
                read_out(dve, "bmix2", l)
                wi = stat[:, 96:112].rearrange("p (b h) -> p b h", h=4)
                dve.tensor_scalar(wi, mix2[:, :, MW:MW + 4], float(4 ** -0.5 * 64 ** -0.5), None, ALU.mult)\
                   .then_inc(S["index_weights"], 1)
                dve.wait_ge(S["index_weights"], l + 1)
                steps = Chain(dve, S["index_step"], l * 12)
                for b in range(1, NB):
                    n = (b + 1) * P
                    read_out(dve, f"bix{b}", l)
                    steps(dve.tensor_scalar(score[b], relu[:, 0, 0:n], wi[:, b, 0:1], None, ALU.mult))
                    for h in range(1, 4):
                        steps(dve.scalar_tensor_tensor(out=score[b], in0=relu[:, h, 0:n], scalar=wi[:, b, h:h + 1],
                                                       in1=score[b], op0=ALU.mult, op1=ALU.add))
                    dve.tensor_tensor(score[b], score[b], C["cmask"][:, T - n:T], ALU.add).then_inc(S["index_scored"], 1)
                assert steps.n == 12
                dve.wait_ge(S["index_scored"], PRIMED + l * 3 + 3)
                plain(dve)
                with dve.Fori(0, TOPK // 8) as r:
                    taken = Chain(dve, S["topk_step"], l * (6 * TOPK // 8) + r * 6)
                    best = [None] + [stat[:, 112 + 8 * (b - 1):120 + 8 * (b - 1)] for b in range(1, NB)]
                    for b in range(1, NB):
                        plain(dve)
                        taken(dve.max(best[b], score[b]))
                    for b in range(1, NB):
                        plain(dve)
                        taken(dve.match_replace(score[b], best[b], score[b], GONE))
                dve.tensor_copy(selb[:, 0:P], C["cmask"][:, T - P:T])
                for b in range(1, NB):
                    at = causal[b][4]
                    ins = dve.tensor_scalar(selb[:, at:at + (b + 1) * P], score[b], GONE, NEG, ALU.not_equal, ALU.mult)
                ins.then_inc(S["selected"], 1)
                dve.wait_ge(S["selected"], l + 1)
                rope("bqB", qB, 1)

                dve.wait_ge(S["forget_log"], l + 1)
                dve.tensor_copy(onehot[0:H, :, :], ident[0:H, 0:H].unsqueeze(2).to_broadcast([H, H, P]))
                steps = Chain(dve, S["forget_sum_step"], l * 2)
                steps(dve.tensor_scalar(fx[0:H, :], fx[0:H, :], 0.0, None, ALU.min))
                steps(dve.tensor_tensor(fx[0:H, :], fx[0:H, :], fe[0:H, :], ALU.subtract))
                dve.tensor_tensor_scan(fF[0:H, :], ones[0:H, 0:1].to_broadcast([H, T]), fx[0:H, :], 0.0, ALU.mult, ALU.add)\
                   .then_inc(S["forget_sum"], 1)

                def attend(br, blocks, bias, sinks=False):
                    def scores(i, p):
                        h = i * 2 + p
                        mx = stat[:, 64 + 4 * p:68 + 4 * p]
                        dve.wait_ge(S["heads_scores"], nth_head(br, l) + h + 1)
                        biases = {}
                        for b, k0, n, at, to in blocks:
                            biases[b] = bias(b, k0, n, to, h)
                            if br == "fox":
                                ins = dve.scalar_tensor_tensor(out=logit[:, p, to:to + n], in0=biases[b], scalar=ftm[:, b, ds(h, 1)],
                                                               in1=fb[:, ds(h, 1), k0:k0 + n].rearrange("p a b -> p (a b)"),
                                                               op0=ALU.add, op1=ALU.subtract)
                                biases[b] = logit[:, p, to:to + n]
                        if br == "fox":
                            ins.then_inc(S["fox_biased"], 1)
                            dve.wait_ge(S["fox_biased"], l * H + h + 1)
                        plain(dve)
                        for b, k0, n, at, to in blocks:
                            ins = dve.tensor_tensor_reduce(logit[:, p, to:to + n], ps[0][:, at:at + n], biases[b], 1.0, -3e38,
                                                           ALU.add, ALU.max, mx[:, b:b + 1])
                        ins.then_inc(S["heads_max"], 1)
                        dve.wait_ge(S["heads_max"], nth_soft(br, l) + h + 1)
                        if sinks:
                            dve.tensor_scalar(mx, mx, sink[:, ds(h, 1)], None, ALU.max).then_inc(S["sink_max"], 1)
                            dve.wait_ge(S["sink_max"], l * H + h + 1)
                        dve.tensor_scalar(mx, mx, -1.0, None, ALU.mult).then_inc(S["heads_scores_read"], 1)

                    def head(i, p, last):
                        h = i * 2 + p
                        if not last:
                            scores(i + 1, p)
                        dve.wait_ge(S["heads_out"], nth_head(br, l) + h + 1)
                        total = stat[:, 72 + 4 * p:76 + 4 * p]
                        if sinks:
                            dve.tensor_tensor(total, total, stat[:, 88 + 4 * p:92 + 4 * p], ALU.add).then_inc(S["sink_sum"], 1)
                            dve.wait_ge(S["sink_sum"], l * H + h + 1)
                        dve.reciprocal(stat[:, 80 + 4 * p:84 + 4 * p], total).then_inc(S["heads_inverse"], 1)
                        dve.wait_ge(S["heads_inverse"], nth_soft(br, l) + h + 1)
                        dve.tensor_tensor(otm[:, :, ds(i * P + p * HD, HD)],
                                          ps[1][:, 3 * T:3 * T + NB * HD].rearrange("p (b d) -> p b d", d=HD),
                                          wide(stat[:, 80 + 4 * p:84 + 4 * p], HD), ALU.mult).then_inc(S["heads_out_read"], 1)

                    scores(0, 0)
                    scores(0, 1)
                    with dve.Fori(0, 3) as i:
                        head(i, 0, False)
                        head(i, 1, False)
                    head(3, 0, True)
                    head(3, 1, True)

                def y_rest(name, k, part, high):
                    dve.wait_ge(S["y_high"], l * 4 + k)
                    h = jobs.half[name]
                    rest(part, banks(h), high).then_inc(drained[h], 1)

                read_out(dve, "bft", l)
                read_out(dve, "bfb0", l)
                read_out(dve, "bfb1", l)
                attend("fox", causal, lambda b, k0, n, to, h: C["cmask"][:, T - n:T])
                y_rest("btA", 1, yAL, yAH)
                attend("dsa", causal, lambda b, k0, n, to, h: selb[:, to:to + n])
                y_rest("btB", 2, yBL, yBH)
                rope("bqC", Q, 2)
                rope("bkC", K, 3)

                def ret_decayed(i, p):
                    h = i * 2 + p
                    dve.wait_ge(S["ret_decay"], l * H + h + 1)
                    dve.wait_ge(S["heads_scores"], nth_head("ret", l) + h + 1)
                    for j, n, at, to in forward:
                        ins = dve.tensor_tensor(logit[:, p, to:to + n], ps[0][:, at:at + n], decay[:, p, 0:n], ALU.mult)
                    ins.then_inc(S["heads_scores_read"], 1)

                plain(dve)
                with dve.Fori(0, 4) as i:
                    ret_decayed(i, 0)
                    ret_decayed(i, 1)
                dve.wait_ge(S["heads_out_read"], PRIMED + nth_head("ret", l) + H)
                grouped = otm.rearrange("p b (h d) -> p (b h) d", d=HD)
                mean, var = stat[:, 0:32], stat[:, 32:64]
                steps = Chain(dve, S["group_step"], l * 3)
                steps(dve.tensor_reduce(mean, grouped, AXX, ALU.add))
                steps(dve.tensor_scalar(mean, mean, 1.0 / HD, None, ALU.mult))
                dve.tensor_tensor(grouped, grouped, wide(mean, HD), ALU.subtract).then_inc(S["group_centred"], 1)
                dve.wait_ge(S["group_squared"], l + 1)
                dve.tensor_reduce(var, gsq.rearrange("p b (h d) -> p (b h) d", d=HD), AXX, ALU.add).then_inc(S["group_var"], 1)
                dve.wait_ge(S["group_std"], l + 1)
                steps(dve.reciprocal(mean, mean))
                dve.tensor_tensor(grouped, grouped, wide(mean, HD), ALU.mult).then_inc(S["group_normed"], 1)
                read_out(dve, "bgC", l)
                dve.wait_ge(S["y_turned"], l * 4 + 3)
                h = jobs.half["btC"]
                for c in range(NB):
                    ins = dve.scalar_tensor_tensor(out=gC[:, c, :], in0=ps[h][:, c * T:c * T + T], scalar=vec[:, W_RET + c:W_RET + c + 1],
                                                   in1=gC[:, c, :], op0=ALU.mult, op1=ALU.mult)
                ins.then_inc(drained[h], 1)
                read_out(dve, "btC", l)
                dve.wait_ge(S["y_high"], l * 4 + 3)
                rest(yCL, gC, yCH).then_inc(S["yc_split"], 1)
                rope("bqD", qD, 4)
                attend("swa", window, lambda b, k0, n, to, h: C["band"][:, 2 * P - n:2 * P], sinks=True)

                y_rest("btD", 4, yDL, yDH)

                with dve.Fori(0, 2) as c:
                    for n in range(4):
                        read_out(dve, f"bgt{n}", l, c)
                        done(dve, f"bbr{n}", l, c)
                        h = jobs.half[f"bbr{n}"]
                        sums = merged_b[:, ds(c * 4, 4), :]
                        gate = gate_b[n % 2]
                        dve.tensor_tensor(gate if n else sums, banks(h), gate, ALU.mult).then_inc(S["gated_b"], 1)
                        dve.wait_ge(S["gated_b"], l * 8 + c * 4 + n + 1)
                        if n:
                            dve.tensor_tensor(sums, sums, gate, ALU.add).then_inc(S["merged_b"], 1)
                            dve.wait_ge(S["merged_b"], PRIMED + l * 6 + c * 3 + n)
                        dve.sem_inc(drained[h], 1)
                for c in range(2):
                    dve.wait_ge(S["merged_b_high"], l * 2 + c + 1)
                    rest(merged_bL[:, 4 * c:4 * c + 4, :], merged_b[:, 4 * c:4 * c + 4, :], merged_bH[c]).then_inc(S["merged_b_split"], 1)
                for g in range(2):
                    add_back(f"bwo{g}", g, l)
                split_norm("bss_ff", vec[:, W_FF:W_FF + KD], l)

                def conv_group(name, g, p, i=0):
                    dve.wait_ge(S["conv_begun"], l * NG + g + 1)
                    h = jobs.half[name]
                    for shift, at in ((1, W_C1), (2, W_C0)):
                        for j in range(4):
                            ch = g * 2 + (j if j < 2 else NF + j - 2)
                            ins = dve.scalar_tensor_tensor(out=conv[:, p, j, shift:T], in0=ps[h][:, j * T:j * T + T - shift],
                                                           scalar=vec[:, ds(ch + at, 1)], in1=conv[:, p, j, shift:T],
                                                           op0=ALU.mult, op1=ALU.add)
                        if shift == 1:
                            ins.then_inc(S["conv_step"], 1)
                            dve.wait_ge(S["conv_step"], l * NG + g + 1)
                    ins.then_inc(drained[h], 1)
                    dve.wait_ge(S["silu_b"], l * NG + g + 1)
                    dve.tensor_tensor(conv[:, p, 0:2, :], conv[:, p, 0:2, :], conv[:, p, 2:4, :], ALU.mult).then_inc(S["ff_ready"], 1)
                    ff_rest(conv[:, p, 0:2, :], g, NG + l * NG + g)

                with dve.Fori(0, 5) as i:
                    conv_group("bupa", i * 2, 0, i)
                    conv_group("bupb", i * 2 + 1, 1, i)
                conv_group("bupc", NG - 1, 0)
                for g in range(2):
                    add_back(f"bdn{g}", g, l)
            norm("css_fin", hT[:, :, :], vec0[:, V_FIN2:V_FIN2 + KD])

        @block.gpsimd
        def _(pool):
            def rests(name, l=0, i=0, cols=512):
                for u in range(ring.units[name]):
                    s, p = ring.slot[(name, u)], ring.split[(name, u)]
                    pool.wait_ge(weights_high, ring.at(ring.before, name, u, l, i) + 1)
                    pool.tensor_tensor(wL[:, p, 0:cols], slot[:, s, 0:cols], plainly(wH[:, p, 0:cols]), ALU.subtract)\
                        .then_inc(weights_split, 1)

            pool.sem_inc(S["s5_back_pool"], PRIMED)
            pool.memset(qz[:, :, :], 0.0).then_inc(S["zeros_set"], 1)
            pool.dma_start(bnat[0], I["s5_b_re"].rearrange("(t q) c -> q t c", q=P)).then_inc(S["s5b_loaded"], 16)
            pool.dma_start(bnat[1], I["s5_b_im"].rearrange("(t q) c -> q t c", q=P)).then_inc(S["s5b_loaded"], 16)
            pool.wait_ge(S["x_turned"], 2)
            for buf in zb + cnat:
                pool.memset(buf, 0.0).then_inc(S["zeros_set"], 1)
            pool.wait_ge(S["zeros_set"], 5)
            for n, key in enumerate(("s5_c_re", "s5_c_im")):
                rows = I[key].rearrange("(q r) s -> r q s", r=P)
                for j in range(4):
                    for g in range(2):
                        at = 32 * j + CHAN * g
                        pool.dma_start(cnat[n][at:at + CHAN, :, STATE * g:STATE * g + STATE], rows[at:at + CHAN, :, :])\
                            .then_inc(S["s5c_loaded"], 16)
            rests("axa")
            pool.wait_ge(S["normed_split"], KD)
            pool.dma_start(rms[:, :], I["consts"][:, N_CONSTS:N_CONSTS + T]).then_inc(S["iota_loaded"], 16)
            rests("aglu")
            with pool.Fori(0, 4) as c:
                def fraction(t):
                    pool.wait_ge(S["s5_whole"], c * 8 + t + 1)
                    pool.tensor_tensor(turn[:, t % 2, :], turn[:, t % 2, :], whole[:, t % 2, :], ALU.subtract)\
                        .then_inc(S["s5_fraction"], 1)

                def turned(t):
                    p = t % 2
                    pool.wait_ge(S["s5_rotated"], c * 8 + t + 1)
                    pool.tensor_tensor(zt[:, p, 0, :], prod[:, p, 0, :], prod[:, p, 1, :], ALU.add)
                    pool.tensor_tensor(zt[:, p, 1, :], prod[:, p, 2, :], prod[:, p, 3, :], ALU.subtract).then_inc(S["s5_z"], 1)

                def back(t):
                    p = t % 2
                    pool.wait_ge(S["s5_scanned"], c * 16 + 2 * t + 2)
                    for n in range(2):
                        ins = pool.tensor_tensor(prod[:, p, 2 + n, :], st[:, p, n, :], trig[:, t % 4, 1 - n, :], ALU.mult)
                    ins.then_inc(S["s5_back_pool"], 1)

                fraction(0)
                fraction(1)
                for t in range(8):
                    turned(t)
                    if t < 6:
                        fraction(t + 2)
                    if t:
                        back(t - 1)
                back(7)
            pool.wait_ge(S["s5_y_read"], PRIMED + 4)
            pool.dma_start(wsn, I["sgu_w"].rearrange("h t s -> t h s")).then_inc(S["sgu_loaded"], 16)
            pool.dma_start(sgub, I["sgu_bias"].unsqueeze(0).to_broadcast([P, H, P])).then_inc(S["sgu_loaded"], 16)
            pool.dma_start(lng, I["sgu_ln_g"].unsqueeze(0).to_broadcast([P, D])).then_inc(S["sgu_loaded"], 16)
            pool.dma_start(lnb, I["sgu_ln_b"].unsqueeze(0).to_broadcast([P, D])).then_inc(S["sgu_loaded"], 16)
            for name in ("azu0", "azu1", "azv0", "azv1"):
                rests(name)
            with pool.Fori(0, 2) as c:
                for name in ("aga", "apa", "agb", "apb"):
                    rests(name, 0, c)
            for name in ("wo", "wk", "wv", "wq", "xo"):
                for g in range(2):
                    rests(f"a{name}{g}")
            with pool.Fori(0, 5) as i:
                rests("aupa", 0, i)
                rests("aupb", 0, i)
            for name in ("aupc", "adn0", "adn1"):
                rests(name)
            with pool.Fori(0, LAYERS) as l:
                rests("bmix1", l)
                rests("bmix2", l, cols=MIX2)
                for name in ("qB", "qA", "kA", "vA", "qC", "kC", "vC", "gC", "qD"):
                    rests("b" + name, l)
                with pool.Fori(0, 2) as c:
                    for n in range(4):
                        rests(f"bgt{n}", l, c)
                        rests(f"bbr{n}", l, c)
                rests("bwo0", l)
                rests("bwo1", l)
                with pool.Fori(0, 5) as i:
                    rests("bupa", l, i)
                    rests("bupb", l, i)
                for name in ("bupc", "bdn0", "bdn1"):
                    rests(name, l)


_SHAPES = {
    "x": (512, 1024), "mem": (256, 1024), "mix_norm_g": (1024,), "w_in": (1024, 4608), "s5_lam_re": (32, 128),
    "s5_lam_im": (32, 128), "s5_log_step": (32, 2), "s5_b_re": (4096, 16), "s5_b_im": (4096, 16),
    "s5_c_re": (1024, 64), "s5_c_im": (1024, 64), "s5_d": (512,), "s5_w_glu": (512, 512), "sgu_ln_g": (1024,),
    "sgu_ln_b": (1024,), "sgu_w": (8, 128, 128), "sgu_bias": (8, 128), "w_proj_a": (512, 1024),
    "w_proj_b": (1024, 1024), "w_out": (1024, 1024), "xattn_norm_g": (1024,), "mem_norm_g": (1024,),
    "w_q": (1024, 1024), "w_k": (1024, 1024), "w_v": (1024, 1024), "w_xo": (1024, 1024), "ffn_norm_g": (1024,),
    "w_gate": (1024, 2816), "w_up": (1024, 2816), "w_down": (2816, 1024), "final_norm_g": (1024,),
    "attn_norm_2": (2, 1024), "w_in_2": (2048, 9420), "forget_bias_2": (2, 8), "ret_norm_2": (2, 512),
    "attn_sinks_2": (2, 8), "w_branch_2": (4096, 1024), "w_out_2": (2048, 1024), "ffn_norm_2": (2, 1024),
    "w_up_2": (2048, 5632), "conv_w_2": (6, 5632), "conv_b_2": (2, 5632), "w_down_2": (5632, 1024),
    "final_norm_2": (1024,),
}


def kernel(**inputs):
    import numpy as _np
    import concourse.bacc as _bacc
    from concourse import mybir as _mybir
    from concourse.bass_utils import run_bass_kernel_spmd as _run

    nc = _bacc.Bacc("TRN2", target_bir_lowering=False, num_devices=1)
    arrays = {name: _np.ascontiguousarray(inputs[name]).reshape(shape) for name, shape in _SHAPES.items()}
    arrays["consts"] = constants()
    handles = {name: nc.dram_tensor(f"in_{name}", a.shape, _mybir.dt.from_np(a.dtype), kind="ExternalInput").ap()
               for name, a in arrays.items()}
    out = nc.dram_tensor("out", (512, 1024), _mybir.dt.float32, kind="ExternalOutput").ap()
    two_blocks(nc, handles, out)
    r = _run(nc, [{f"in_{name}": a for name, a in arrays.items()}], core_ids=[0])
    return r.results[0]["out"].reshape(1, 512, 1024)
```

```python
from contextlib import ExitStack

import numpy as np
import concourse.bass as bass
from concourse import mybir

ALU = mybir.AluOpType
ACT = mybir.ActivationFunctionType
F32 = mybir.dt.float32
F32R = mybir.dt.float32r
AXX = mybir.AxisListType.X

P = 128
T = 512
NB = T // P
D = 1024
KD = D // P
M = 256
EPS = 1e-6
FF = 2816
NF = FF // P
NG = NF // 2
H = 8
HD = 64
TOPK = 128
LAYERS = 2
NEG = -1e30
GONE = -3e38
GROUPS, STATE, CHAN = 32, 64, 16
QUADS = 8
TWO_PI = 6.283185
INV_2PI = float(np.float32(1.0 / (2.0 * np.pi)))
C1 = 6.28125
C2 = float(2.0 * np.pi - 6.28125)
ROUND = 12582912.0

FOX_Q, FOX_K, FOX_V, FOX_F = 0, 512, 1024, 1536
DSA_Q, DSA_K, DSA_V, IDX_Q, IDX_K, IDX_W = 1544, 2056, 2120, 2184, 2440, 2504
RET_Q, RET_K, RET_V, RET_G = 2508, 3020, 3532, 4044
SWA_Q, SWA_K, SWA_V = 4556, 5068, 5196
GATES = 5324
MF, MW, MVB, MVD, MIX2 = 0, 8, 12, 76, 204

SLOTS = 8
ARENA = 27776
SPLITS = 4

FIRST = [[("xa", 8, 1)], [("glu", 4, 1)], [("zv0", 8, 1), ("zv1", 8, 1), ("zu0", 8, 1), ("zu1", 8, 1)],
         ("loop", 2, [("ga", 8, 1), ("pa", 4, 1), ("gb", 8, 1), ("pb", 8, 1), (None, 4, 0)]),
         [("wo0", 8, 1), ("wo1", 8, 1), ("wk0", 8, 1), ("wk1", 8, 1), ("wv0", 8, 1), ("wv1", 8, 1),
          ("wq0", 8, 1), ("wq1", 8, 1), ("xo0", 8, 1), ("xo1", 8, 1)],
         ("loop", 5, [("upa", 8, 2), ("upb", 8, 2)]), [("upc", 8, 2), ("dn0", 22, 1), ("dn1", 22, 1)]]
LAYER = [[("mix1", 8, 4), ("mix2", 8, 4), ("qB", 8, 1), ("qA", 8, 1), ("kA", 8, 1), ("vA", 8, 1),
          ("qC", 8, 1), ("kC", 8, 1), ("vC", 8, 1), ("qD", 8, 1), ("gC", 8, 1)],
         ("loop", 2, [(f"{s}{n}", u, 1) for n in range(4) for s, u in (("gt", 8), ("br", 4))]),
         [("wo0", 8, 1), ("wo1", 8, 1)],
         ("loop", 5, [("upa", 8, 2), ("upb", 8, 2)]), [("upc", 8, 2), ("dn0", 22, 1), ("dn1", 22, 1)]]


def pad_units(parts):
    n = sum((p[1] if p[0] == "loop" else 1) * sum(u for _, u, _ in (p[2] if p[0] == "loop" else p))
            for p in parts)
    return parts + [[(None, -n % SLOTS, 0)]]


PRIMED = 1


class Ring:

    def __init__(self):
        self.slot, self.split, self.before, self.landed, self.units = {}, {}, {}, {}, {}
        self.room, self.split_room = {}, {}
        at = before = 0
        pieces, owner, split_owner = [0] * SLOTS, [0] * SLOTS, [0] * SPLITS
        stages = [("a", 0, pad_units(FIRST))] + [("b", l, pad_units(LAYER)) for l in range(LAYERS)]
        for stage, l, parts in stages:
            for part in parts:
                reps, body = (part[1], part[2]) if part[0] == "loop" else (1, part)
                for i in range(reps):
                    for name, units, dmas in body:
                        for u in range(units):
                            s, p = at % SLOTS, at % SPLITS
                            at += 1
                            if name is None:
                                continue
                            key = (stage + name, u)
                            pieces[s] += 16 * dmas
                            assert self.slot.setdefault(key, s) == s
                            self.split[key] = p
                            self.units[stage + name] = units
                            self.before[key + (l, i)] = before
                            self.landed[key + (l, i)] = pieces[s]
                            self.room[key] = max(self.room.get(key, -SLOTS), owner[s] - before)
                            self.split_room[key] = max(self.split_room.get(key, -SLOTS), split_owner[p] - before)
                            before += 1
                            owner[s] = split_owner[p] = before

    def at(self, table, name, u, l, i):
        v = table[(name, u, 0, 0)]
        for reg, other in ((l, (1, 0)), (i, (0, 1))):
            if (name, u) + other in table:
                v = v + reg * (table[(name, u) + other] - table[(name, u, 0, 0)])
        return v


JOBS_FIRST = ["vecs", "x0", "x1", "memT", "ss_mem", "ss_mix", "xa", "s5col", "s5B", "s5C", "glu",
              "zv0", "zv1", "zu0", "zu1", "wsT", "sv0", "sv1", (2, ["ga", "pa", "gb", "pb"]),
              "wo0", "wo1", "wk0", "wk1", "wv0", "wv1", "ss_xa", "wq0", "wq1",
              "xs0", "xs1", "xt0", "xs2", "xv0", "xt1", "xs3", "xv1", "xt2", "xv2", "xt3", "xv3",
              "xo0", "xo1", "ss_ff", (5, ["upa", "upb"]), "upc", "dn0", "dn1", "ss_fin"]
JOBS_LAYER = ["vecs", "ss_at", "mix1", "mix2", "ix1", "ix2", "ix3", "qB", "qA", "kA", "lf", "vA",
              "ft", "fb0", "fb1", "tA", "tB", "qC", "kC", "vC", "qD", "gC", "tC", "tD",
              (2, [f"{s}{n}" for n in range(4) for s in ("gt", "br")]), "wo0", "wo1", "ss_ff",
              (5, ["upa", "upb"]), "upc", "dn0", "dn1"]
JOBS_LAST = ["ss_fin", "out0", "out1"]
AFTER = {"fox": ("btA", "btB"), "dsa": ("btA", "btB"), "swa": ("btC", "btD")}


class Jobs:

    def __init__(self):
        self.half, self.before = {}, {}
        seq, count = 0, [0, 0]
        for stage, l, jobs in [("a", 0, JOBS_FIRST)] + [("b", l, JOBS_LAYER) for l in range(LAYERS)] + [
                ("c", 0, JOBS_LAST)]:
            for job in jobs:
                reps, body = job if isinstance(job, tuple) else (1, [job])
                for i in range(reps):
                    for name in body:
                        h = seq % 2
                        assert self.half.setdefault(stage + name, h) == h, (stage, name)
                        self.before[(stage + name, l, i)] = count[h]
                        count[h] += 1
                        seq += 1

    def nth(self, name, l=0, i=0):
        v = self.before[(name, 0, 0)]
        for reg, other in ((l, (1, 0)), (i, (0, 1))):
            if (name,) + other in self.before:
                v = v + reg * (self.before[(name,) + other] - self.before[(name, 0, 0)])
        return v


NORMS = {"ass_mem": 0, "ass_mix": 1, "ass_xa": 2, "ass_ff": 3, "ass_fin": 4, "bss_at": 5, "bss_ff": 6, "css_fin": 9}
WHOLE_NORMS = {"ass_mem": 1, "css_fin": 2}
SPLIT_NORMS = {"ass_mix": 0, "ass_xa": 1, "ass_ff": 2, "bss_at": 3, "bss_ff": 4}


def nth_norm(name, l=0):
    return NORMS[name] + (l * 2 if name[0] == "b" else 0) + 1


STATES = {"ass_xa": 0, "ass_ff": 1, "ass_fin": 2, "bss_at": 3, "bss_ff": 4, "css_fin": 3 + 2 * LAYERS}
SQUARES_AT = {"ass_xa": 18432, "ass_ff": 10240}


def state(name, l=0):
    return STATES[name] + (l * 2 if name[0] == "b" else 0)


def state_parts(name, l=0):
    return STATES[name] * 5 + (l * 10 if name[0] == "b" else 0)


def split_chunks(name, l=0):
    return SPLIT_NORMS[name] * KD + (l * (2 * KD) if name[0] == "b" else 0)


class Chain:

    def __init__(self, eng, sem, base=0):
        self.eng, self.sem, self.base, self.n = eng, sem, base, 0

    def __call__(self, ins):
        self.n += 1
        ins.then_inc(self.sem, 1)
        self.eng.wait_ge(self.sem, self.base + self.n)


CONSTS = (("ident", P), ("ones", P), ("cmask", T), ("band", 2 * P), ("cos", T), ("sin", T),
          ("dist", T), ("logdecay", H))
N_CONSTS = sum(n for _, n in CONSTS)


def constants():
    f32, row, col = np.float32, np.arange(P)[:, None], np.arange(T)[None, :]
    inv = (1.0 / np.power(f32(10000.0), np.arange(HD // 2, dtype=f32) * f32(2.0) / f32(HD))).astype(f32)
    angle = (np.arange(T, dtype=f32)[None, :] * inv[np.arange(P) % 32][:, None]).astype(f32).astype(np.float64)
    sign = np.where(np.arange(P) % HD < 32, -1.0, 1.0)[:, None]
    j = np.arange(2 * P)[None, :]
    tables = {
        "ident": np.eye(P), "ones": np.ones((P, P)), "iota": np.broadcast_to(col, (P, T)),
        "cmask": np.where(col - (T - P) > row, NEG, 0.0),
        "band": np.where((j > row) & (j <= row + P), 0.0, NEG),
        "cos": np.cos(angle), "sin": np.sin(angle) * sign,
        "dist": np.where(col >= row, col - row, -NEG),
        "logdecay": np.broadcast_to(np.log(1.0 - 2.0 ** (-5.0 - np.arange(H)))[None, :], (P, H)),
    }
    return np.ascontiguousarray(np.concatenate([np.asarray(tables[n], f32) for n in [n for n, _ in CONSTS] + ["iota"]], axis=1))


V_MIX, V_MEM, V_XA, V_FF, V_FIN, V_FIN2, V_D, V_ROWS = 0, 8, 16, 24, 32, 40, 48, 52
W_AT, W_FF, W_RET, W_CB, W_C2, W_C0, W_C1 = 0, 8, 16, 20, 64, 108, 152
W_ROWS1, W_ROWS2 = 108, 88


def two_blocks(nc, I, out):
    ring, jobs = Ring(), Jobs()
    ds = bass.ds
    with ExitStack() as ctx:
        def sb(name, *shape):
            return ctx.enter_context(nc.sbuf_tensor(name, [P, *shape], F32))

        class Signals(dict):
            def __missing__(self, name):
                self[name] = ctx.enter_context(nc.semaphore(name))
                return self[name]

        S = Signals()
        landed = [S[f"weights_landed{s}"] for s in range(SLOTS)]
        weights_high, weights_split = S["weights_high"], S["weights_split"]
        weights_used = S["weights_used"]
        drained = [S["half0_drained"], S["half1_drained"]]

        ps = [ctx.enter_context(nc.psum_tensor(f"half{h}", [P, 4 * T], F32)) for h in range(2)]
        hT = sb("hT", KD, T)
        nH = ctx.enter_context(nc.sbuf_tensor("nH", [P, KD, T], F32R))
        nL = ctx.enter_context(nc.sbuf_tensor("nL", [P, KD, T], F32R))
        slot = sb("slot", SLOTS, 512)
        wH = ctx.enter_context(nc.sbuf_tensor("wH", [P, SPLITS, 512], F32R))
        wL = ctx.enter_context(nc.sbuf_tensor("wL", [P, SPLITS, 512], F32R))
        consts = sb("consts", N_CONSTS)
        C, at = {}, 0
        for name, n in CONSTS:
            C[name] = consts[:, at:at + n]
            at += n
        ident, ones = C["ident"], C["ones"]
        vrow = sb("vrow", 2, P)
        vec = sb("vec", W_ROWS1 + W_ROWS2)
        vec0 = sb("vec0", V_ROWS)
        rms = sb("rms", T)
        qz = sb("qz", 2, T)
        small = sb("small", 160)
        eps, half_pi, rounder = small[:, 0:1], small[:, 1:2], small[:, 154:155]
        stat = small[:, 2:154]
        with nc.sbuf_tensor("arena", [P, ARENA], F32) as arena:
            pass
        arena_split = ctx.enter_context(nc.sbuf_tensor("arena_split", [P, ARENA], F32R))

        def A(at, *shape, of=arena):
            n = int(np.prod(shape))
            v = of[:, at:at + n]
            if len(shape) == 2:
                v = v.rearrange("p (a b) -> p a b", b=shape[1])
            elif len(shape) == 3:
                v = v.rearrange("p (a b c) -> p a b c", b=shape[1], c=shape[2])
            return v

        def banks(h, n=4, w=T):
            return ps[h][:, 0:n * T].rearrange("p (a b) -> p a b", b=T)[:, :, 0:w]

        def R(at, *shape):
            return A(at, *shape, of=arena_split)

        def plainly(v):
            return v.bitcast(F32)

        x_in, mem_in, mT = A(0, NB, D), A(4096, 2, D), A(6144, KD, M)
        uT = A(8192, NB, T)
        s5w = A(10240, QUADS, 5, P)
        cnat = [A(0, QUADS, P), A(1024, QUADS, P)]
        zb = [A(2048, 32, 32), A(3072, 32, 32)]
        ust = qz
        stg = [A(3072, 2, 5 * P), A(4352, 2, 5 * P)]
        trig = A(0, 3, 2, T)
        turn, whole = A(15360, 2, T), A(16384, 2, T)
        prod, zt, st = A(17408, 3, 4, T), A(23552, 2, 2, T), A(25600, 2, 2, T)
        row = A(17408, 24, P)
        bnat = [A(20480, 32, CHAN), A(20992, 32, CHAN)]
        bprod = [A(15360 + 512 * n, 32, CHAN) for n in range(4)]
        s5col = sb("s5col", 4, 32)
        yH, yL = R(0, NB, T), R(2048, NB, T)
        zv, zu = A(10240, NB, D), A(14336, KD, T)
        wsn, wsT, sgub = A(18432, H, P), A(19456, H, P), A(20480, H, P)
        lng, lnb, svt = A(21504, D), A(22528, D), A(23552, 4, T)
        zuH, zuL = R(18432, KD, T), R(10240, KD, T)
        gate_a, merged_a = [A(4096, 4, T), A(25600, 4, T)], A(14336, KD, T)
        merged_aH, merged_aL = [R(23552, 4, T), R(0, 4, T)], R(14336, KD, T)
        mH, mL = R(8192, KD, M), R(6144, KD, M)
        xq, xk, xv = A(10240, KD, T), A(2048, KD, M), A(4096, 2, D)
        xp, xpT, xoH, xoL = A(14336, 2, NB, M), A(16384, 2, 2, T), R(18432, KD, T), R(22528, KD, T)

        def squares(name):
            return A(8192, KD, M) if name == "ass_mem" else A(SQUARES_AT.get(name, 22528), KD, T)

        ffH, ffL = R(0, NF, T), R(11264, NF, T)
        sg_a, ff_raw = A(22528, 2, 2, T), A(24576, 2, 2, T)

        Q, K, V = A(0, NB, T), A(2048, NB, T), A(4096, NB, T)
        qB, gC, qD = A(6144, NB, T), K, Q
        mix1, mix2 = A(8192, NB, T), A(10240, NB, MIX2)
        kBB, kII, kDD = A(11056, T), A(11568, T), A(4096, 2, T)
        selb = A(12080, 1280)
        logit = A(13360, 2, 1280)
        probT = A(15920, 1280)
        fb, part = A(17200, H, T), A(17200, NB, T)
        otm, otm2 = A(21296, NB, T), A(19248, NB, T)
        yAH, yAL, yBH, yBL = R(23344, NB, T), R(25392, NB, T), R(6144, NB, T), R(11056, NB, T)
        yCH, yCL, yDH, yDL = R(17200, NB, T), R(2048, NB, T), R(0, NB, T), R(4096, NB, T)
        fx, fe, fF, onehot = A(13360, T), A(13872, T), A(14384, T), R(14896, H, P)
        fFH, fFL = R(13360, T), R(13872, T)
        relu, score = A(23344, NB, T), [None, A(15920, 256), A(16176, 384), A(16560, 512)]
        decay, gsq = A(19248, 2, T), A(17200, NB, T)
        gate_b, merged_b = [A(8192, 4, T), A(21296, 4, T)], A(13104, KD, T)
        merged_bH, merged_bL = [R(17200, 4, T), R(0, 4, T)], R(13104, KD, T)
        conv = A(22528, 2, 4, T)
        o_out = A(0, NB, D)
        ftm = sb("ftm", NB, H)
        sink = sb("sink", H)
        fbias = sb("fbias", 1)

        causal = [(0, 0, 128, 896, 0), (1, 0, 256, 1024, 128), (2, 0, 384, 512, 384), (3, 0, 512, 0, 768)]
        window = [(0, 0, 128, 896, 0), (1, 0, 256, 1024, 128), (2, 128, 256, 512, 384), (3, 256, 256, 0, 640)]
        forward = [(0, 512, 0, 0), (1, 384, 512, 512), (2, 256, 1024, 896), (3, 128, 896, 1152)]

        def turned_blocks(blocks):
            return [(j, b, k0, at) for j in range(NB) for b, k0, n, _, at in blocks if k0 <= j * P < k0 + n]

        def nth_head(br, l):
            return l * (4 * H) + ("fox", "dsa", "ret", "swa").index(br) * H

        def nth_soft(br, l):
            return l * (3 * H) + ("fox", "dsa", "swa").index(br) * H

        def done(eng, name, l=0, i=0):
            eng.wait_ge(weights_used, ring.at(ring.before, name, ring.units[name] - 1, l, i) + 1)

        def plain(eng):
            eng.nop(nofuse=True)

        def read_out(eng, name, l=0, i=0):
            eng.wait_ge(drained[jobs.half[name]], jobs.nth(name, l, i) + 1)

        for name, reps, after in (("aupa", 5, "aupc"), ("bupa", 5, "bupc")):
            for u in range(ring.units[name]):
                assert ring.slot[(name, u)] == ring.slot[(after, u)] and ring.split_room[(name, u)] == ring.split_room[(after, u)]
                for table in (ring.before, ring.landed):
                    assert ring.at(table, name, u, 0, reps) == ring.at(table, after, u, 0, 0)

        def lin(w, r0, c0):
            return lambda u: [(slice(0, 512), w[ds(r0 + u * P, P), ds(c0, 512)])]

        block = ctx.enter_context(nc.Block())

        @block.sync
        def _(sp):
            sp.dma_start(x_in, I["x"].rearrange("(b p) d -> p b d", p=P)).then_inc(S["x_loaded"], 16)

            def load(name, pieces, l=0, i=0):
                for u in range(ring.units[name]):
                    s = ring.slot[(name, u)]
                    free = ring.at(ring.before, name, u, l, i) + ring.room[(name, u)]
                    if not isinstance(free, int) or free > 0:
                        sp.wait_ge(weights_split, free)
                        plain(sp)
                    for cols, src in pieces(u):
                        sp.dma_start(slot[:, s, cols], src).then_inc(landed[s], 16)

            w = I["w_in"]
            load("axa", lin(w, 0, 0))
            load("aglu", lin(I["s5_w_glu"], 0, 0))
            for g in range(2):
                load(f"azv{g}", lin(w, 0, 1536 + 512 * g))
            for g in range(2):
                load(f"azu{g}", lin(w, 0, 512 + 512 * g))
            with sp.Fori(0, 2) as c:
                load("aga", lin(w, 0, c * 512 + 2560), 0, c)
                load("apa", lin(I["w_proj_a"], 0, c * 512), 0, c)
                load("agb", lin(w, 0, c * 512 + 3584), 0, c)
                load("apb", lin(I["w_proj_b"], 0, c * 512), 0, c)
            for name, key in (("wo", "w_out"), ("wk", "w_k"), ("wv", "w_v"), ("wq", "w_q"), ("xo", "w_xo")):
                for g in range(2):
                    load(f"a{name}{g}", lin(I[key], 0, 512 * g))

            def up(first, second, r0, g):
                return lambda u: [(slice(0, 256), first[ds(r0 + u * P, P), ds(g * 256, 256)]),
                                  (slice(256, 512), second(u, g))]

            def up_a(g):
                return up(I["w_gate"], lambda u, g: I["w_up"][ds(u * P, P), ds(g * 256, 256)], 0, g)

            with sp.Fori(0, 5) as i:
                load("aupa", up_a(i * 2), 0, i)
                load("aupb", up_a(i * 2 + 1), 0, i)
            load("aupc", up_a(NG - 1))
            for g in range(2):
                load(f"adn{g}", lin(I["w_down"], 0, 512 * g))

            w = I["w_in_2"]
            with sp.Fori(0, LAYERS) as l:
                r = l * D
                sp.wait_ge(S["vecs_turned"], 1)
                sp.wait_ge(S["merged_b"], PRIMED + l * 6)
                seen = S["layer_vecs_loaded"]
                for at, n, key in ((W_AT, 8, "attn_norm_2"), (W_FF, 8, "ffn_norm_2"), (W_RET, 4, "ret_norm_2"), (W_CB, 44, "conv_b_2")):
                    sp.dma_start(vrow[at:at + n, 0, :], I[key][ds(l, 1), :].rearrange("o (r p) -> (o r) p", p=P)).then_inc(seen, 16)
                taps = I["conv_w_2"]
                sp.dma_start(vrow[W_C2:W_C2 + 44, 0, :], taps[ds(l * 3 + 2, 1), :].rearrange("o (r p) -> (o r) p", p=P)).then_inc(seen, 16)
                sp.dma_start(vrow[0:88, 1, :], taps[ds(l * 3, 2), :].rearrange("o (r p) -> (o r) p", p=P)).then_inc(seen, 16)
                sp.dma_start(sink[:, :], I["attn_sinks_2"][ds(l, 1), :].to_broadcast([P, H])).then_inc(seen, 16)
                sp.dma_start(fbias[0:H, :], I["forget_bias_2"][ds(l, 1), :].rearrange("o h -> h o")).then_inc(seen, 16)

                def cols(*pieces):
                    def unit(u):
                        at, got = 0, []
                        for c0, n in pieces:
                            got.append((slice(at, at + n), w[ds(r + u * P, P), c0:c0 + n]))
                            at += n
                        return got
                    return unit

                load("bmix1", cols((IDX_Q, 256), (DSA_K, 64), (IDX_K, 64), (SWA_K, 128)), l)
                load("bmix2", cols((FOX_F, 8), (IDX_W, 4), (DSA_V, 64), (SWA_V, 128)), l)
                for name, c0 in (("qB", DSA_Q), ("qA", FOX_Q), ("kA", FOX_K), ("vA", FOX_V), ("qC", RET_Q),
                                 ("kC", RET_K), ("vC", RET_V), ("qD", SWA_Q), ("gC", RET_G)):
                    load("b" + name, lin(w, r, c0), l)
                with sp.Fori(0, 2) as c:
                    for n in range(4):
                        load(f"bgt{n}", lin(w, r, c * 512 + GATES + n * D), l, c)
                        load(f"bbr{n}", lin(I["w_branch_2"], l * 2048 + n * 512, c * 512), l, c)
                for g in range(2):
                    load(f"bwo{g}", lin(I["w_out_2"], r, 512 * g), l)

                def up_b(g):
                    w2 = I["w_up_2"]
                    return up(w2, lambda u, g: w2[ds(r + u * P, P), ds(g * 256 + FF, 256)], r, g)

                with sp.Fori(0, 5) as i:
                    load("bupa", up_b(i * 2), l, i)
                    load("bupb", up_b(i * 2 + 1), l, i)
                load("bupc", up_b(NG - 1), l)
                for g in range(2):
                    load(f"bdn{g}", lin(I["w_down_2"], l * FF, 512 * g), l)

            rows = out.rearrange("(b p) d -> p b d", p=P)
            for g in range(2):
                read_out(sp, f"cout{g}")
                sp.dma_start(rows[:, :, 512 * g:512 * g + 512], o_out[:, :, 512 * g:512 * g + 512])\
                  .then_inc(S["stored"], 16)
            sp.wait_ge(S["stored"], 32)

        @block.tensor
        def _(pe):
            def fill(name, l=0, i=0):
                h, n = jobs.half[name], jobs.nth(name, l, i)
                if not isinstance(n, int) or n > 0:
                    pe.wait_ge(drained[h], n)
                return ps[h]

            def linear(name, act, l=0, i=0, n=T, tokens=None, cols=512, ready=None):
                o = fill(name, l, i)
                last = ring.units[name] - 1
                for k in range(last + 1):
                    p = ring.split[(name, k)]
                    pe.wait_ge(weights_split, ring.at(ring.before, name, k, l, i) + 1)
                    if ready:
                        pe.wait_ge(*ready(k))
                    high, rest = act(k)
                    for j in range(tokens or 4):
                        block = slice(j * P, j * P + P)
                        if tokens:
                            dst = o[:, j * T:j * T + cols]
                            passes = [(high[:, block], wH[:, p, 0:cols]), (high[:, block], wL[:, p, 0:cols]),
                                      (rest[:, block], wH[:, p, 0:cols])]
                        else:
                            dst = o[:, j * T:j * T + n]
                            passes = [(wH[:, p, block], high), (wH[:, p, block], rest), (wL[:, p, block], high)]
                        for m, (lhsT, rhs) in enumerate(passes):
                            mm = pe.matmul(dst, lhsT, rhs, start=(k == 0 and m == 0), stop=(k == last and m == 2))
                    mm.then_inc(weights_used, 1)

            def split(high, rest):
                return lambda k: (high[:, k, :], rest[:, k, :])

            stream = split(nH, nL)

            def normed(name, l=0):
                return lambda k: (S["normed_split"], split_chunks(name, l) + k + 1)

            def multiplied(before):
                return lambda k: (S["ff_split"], before + k // 2 + 1)

            def halves(high, rest):
                return lambda k: (high[k // 4][:, k % 4, :], rest[:, k, :])

            def square_sum(name, l=0, n=T):
                o = fill(name, l)
                first = name in ("ass_mem", "ass_mix")
                if first:
                    pe.wait_ge(S["squared_first"], nth_norm(name))
                for k in range(KD) if first else (0, 4, 5, 6, 7):
                    if not first and k == 0:
                        pe.wait_ge(S["half_summed"], state(name, l) + 1)
                    elif not first:
                        pe.wait_ge(S["squared"], state_parts(name, l) + k - 2)
                    mm = pe.matmul(o[:, 0:n], ones, squares(name)[:, k, :], start=(k == 0), stop=(k == KD - 1))
                mm.then_inc(S["summed"], 1)

            pe.sem_inc(S["s5_out"], PRIMED)
            pe.wait_ge(S["consts_loaded"], 16)
            pe.wait_ge(S["vecs_loaded"], 16 * 7)
            o = fill("avecs")
            pe.transpose(o[:, 0:V_ROWS], vrow[0:V_ROWS, 0, :], ident[0:V_ROWS, 0:V_ROWS]).then_inc(S["vecs_turned"], 1)
            pe.wait_ge(S["x_loaded"], 16)
            for g in range(2):
                o = fill(f"ax{g}")
                for c in range(4):
                    for b in range(NB):
                        mm = pe.transpose(o[:, c * T + b * P:c * T + b * P + P],
                                          x_in[:, b, (4 * g + c) * P:(4 * g + c + 1) * P], ident)
                mm.then_inc(S["x_turned"], 1)
            pe.wait_ge(S["mem_loaded"], 16)
            o = fill("amemT")
            for c in range(KD):
                for b in range(2):
                    mm = pe.transpose(o[:, c * M + b * P:c * M + b * P + P], mem_in[:, b, c * P:c * P + P], ident)
            mm.then_inc(S["mem_turned"], 1)
            square_sum("ass_mem", n=M)
            square_sum("ass_mix")
            linear("axa", stream, ready=normed("ass_mix"))

            o = fill("as5col")
            pe.wait_ge(S["s5_params"], 1)
            for n in range(4):
                mm = pe.transpose(o[:, 32 * n:32 * n + 32], row[0:32, n, :], ident[0:32, 0:32])
            mm.then_inc(S["s5_turned"], 1)
            o = fill("as5B")
            pe.wait_ge(S["s5_bbar"], 1)
            for q in range(QUADS):
                for n in range(2):
                    mm = pe.transpose(o[:, (2 * q + n) * P:(2 * q + n + 1) * P], zb[n][:, 4 * q:4 * q + 4, :], ident)
            mm.then_inc(S["s5_turned"], 1)
            o = fill("as5C")
            pe.wait_ge(S["s5c_loaded"], 16 * 16)
            for q in range(QUADS):
                for n in range(2):
                    mm = pe.transpose(o[:, (2 * q + n) * P:(2 * q + n + 1) * P], cnat[n][:, q, :], ident)
            mm.then_inc(S["s5_turned"], 1)
            read_out(pe, "as5B")
            read_out(pe, "as5C")
            with pe.Fori(0, 2) as c:
                def drive(t):
                    e, d, j, p = t // 8, t % 8 // 4, t % 4, t % 2
                    if t % 8 == 0:
                        pe.wait_ge(S["s5_staged"], c * 2 + e + 1)
                    if t >= 2:
                        pe.wait_ge(S["s5_rotated"], c * 16 + t - 1)
                    for n in range(2):
                        mm = pe.matmul(ps[0][:, (2 * p + n) * T:(2 * p + n + 1) * T],
                                       stg[e][32 * j:32 * j + 32, d, n * P:n * P + P], ust[32 * j:32 * j + 32, e, :],
                                       start=True, stop=True)
                    mm.then_inc(S["s5_driven"], 1)

                def out_of_states(t):
                    e, d, j = t // 8, t % 8 // 4, t % 4
                    pe.wait_ge(S["s5_back_dve"], c * 16 + t + 1)
                    pe.wait_ge(S["s5_back_pool"], PRIMED + c * 16 + t + 1)
                    if t % 8 == 0:
                        pe.wait_ge(S["s5_y_read"], PRIMED + c * 2)
                    for n, kind in enumerate((2, 3, 4, 4)):
                        mm = pe.matmul(ps[1][32 * j:32 * j + 32, e * T:e * T + T],
                                       stg[e][:, d, kind * P + 32 * j:kind * P + 32 * j + 32], prod[:, t % 3, n, :],
                                       start=(d == 0 and n == 0), stop=(d == 1 and n == 3), skip_group_check=True)
                    mm.then_inc(S["s5_out"], 1)

                drive(0)
                drive(1)
                for t in range(16):
                    if t < 14:
                        drive(t + 2)
                    if t:
                        out_of_states(t - 1)
                out_of_states(15)
            pe.wait_ge(S["s5_y_read"], PRIMED + 4)
            pe.wait_ge(S["ya_split"], 1)
            linear("aglu", split(yH, yL))

            for g in range(2):
                linear(f"azv{g}", stream, tokens=NB)
            for g in range(2):
                linear(f"azu{g}", stream)
            o = fill("awsT")
            pe.wait_ge(S["sgu_loaded"], 16 * 4)
            for h in range(H):
                mm = pe.transpose(o[:, h * P:h * P + P], wsn[:, h, :], ident)
            mm.then_inc(S["ws_turned"], 1)
            pe.wait_ge(S["zv_normed"], 1)
            read_out(pe, "awsT")
            for g in range(2):
                o = fill(f"asv{g}")
                for h in range(4):
                    for b in range(NB):
                        mm = pe.matmul(o[:, h * T + b * P:h * T + b * P + P], zv[:, b, (4 * g + h) * P:(4 * g + h + 1) * P],
                                       wsT[:, 4 * g + h, :], start=True, stop=True)
                mm.then_inc(S["sv_done"], 1)
            with pe.Fori(0, 2) as c:
                linear("aga", stream, 0, c)
                pe.wait_ge(S["ya_split"], 2)
                linear("apa", split(yH, yL), 0, c)
                linear("agb", stream, 0, c)
                pe.wait_ge(S["yb_split"], 2)
                linear("apb", split(zuH, zuL), 0, c)
            linear("awo0", halves(merged_aH, merged_aL), ready=lambda k: (S[f"merged_a_split{k // 4}"], 1))
            linear("awo1", halves(merged_aH, merged_aL))

            pe.wait_ge(S["mem_split"], 1)
            for g in range(2):
                linear(f"awk{g}", split(mH, mL), n=M)
            for g in range(2):
                linear(f"awv{g}", split(mH, mL), tokens=2)
            square_sum("ass_xa")
            for g in range(2):
                linear(f"awq{g}", stream, ready=normed("ass_xa"))
            read_out(pe, "awq0")
            read_out(pe, "awq1")

            def x_scores(h):
                o = fill(f"axs{h}")
                for b in range(NB):
                    for c in range(2):
                        mm = pe.matmul(o[:, b * M:b * M + M], xq[:, 2 * h + c, b * P:b * P + P], xk[:, 2 * h + c, :],
                                       start=(c == 0), stop=(c == 1))
                mm.then_inc(S["x_scores"], 1)

            def x_turn(h):
                pe.wait_ge(S["x_probs"], h + 1)
                o = fill(f"axt{h}")
                for m in range(2):
                    for b in range(NB):
                        mm = pe.transpose(o[:, m * T + b * P:m * T + b * P + P], xp[:, h % 2, b, m * P:m * P + P], ident)
                mm.then_inc(S["x_probs_turned"], 1)

            def x_out(h):
                read_out(pe, f"axt{h}")
                o = fill(f"axv{h}")
                for c in range(2):
                    for m in range(2):
                        mm = pe.matmul(o[:, c * T:c * T + T], xv[:, m, (2 * h + c) * P:(2 * h + c + 1) * P],
                                       xpT[:, h % 2, m, :], start=(m == 0), stop=(m == 1))
                mm.then_inc(S["x_out"], 1)

            x_scores(0)
            x_scores(1)
            x_turn(0)
            x_scores(2)
            x_out(0)
            x_turn(1)
            x_scores(3)
            x_out(1)
            for h in (2, 3):
                x_turn(h)
                x_out(h)
            read_out(pe, "axv3")
            for g in range(2):
                linear(f"axo{g}", split(xoH, xoL))
            square_sum("ass_ff")
            with pe.Fori(0, 5) as i:
                linear("aupa", stream, 0, i, ready=normed("ass_ff"))
                linear("aupb", stream, 0, i)
            linear("aupc", stream)
            linear("adn0", split(ffH, ffL), ready=multiplied(0))
            linear("adn1", split(ffH, ffL))
            square_sum("ass_fin")

            with pe.Fori(0, LAYERS) as l:
                o = fill("bvecs", l)
                pe.wait_ge(S["layer_vecs_loaded"], l * (16 * 8) + 16 * 8)
                pe.transpose(o[:, 0:W_ROWS1], vrow[0:W_ROWS1, 0, :], ident[0:W_ROWS1, 0:W_ROWS1])
                pe.transpose(o[:, W_ROWS1:W_ROWS1 + W_ROWS2], vrow[0:W_ROWS2, 1, :], ident[0:W_ROWS2, 0:W_ROWS2])\
                  .then_inc(S["layer_vecs_turned"], 1)
                square_sum("bss_at", l)
                linear("bmix1", stream, l, ready=normed("bss_at", l))
                linear("bmix2", stream, l, tokens=NB, cols=MIX2)
                pe.wait_ge(S["roped"], PRIMED + l * 5 + 1)
                pe.wait_ge(S["kk_copied"], l * 2 + 1)
                for b in range(1, NB):
                    o = fill(f"bix{b}", l)
                    n = (b + 1) * P
                    for h in range(4):
                        r0 = HD * (h % 2)
                        mm = pe.matmul(o[:, h * T:h * T + n], mix1[r0:r0 + HD, h // 2, b * P:b * P + P],
                                       kII[r0:r0 + HD, 0:n], start=True, stop=True)
                    mm.then_inc(S["index_dots"], 1)
                for name in ("bqB", "bqA", "bkA"):
                    linear(name, stream, l)
                o = fill("blf", l)
                read_out(pe, "bmix2", l)
                for b in range(NB):
                    mm = pe.transpose(o[0:H, b * P:b * P + P], mix2[:, b, MF:MF + H], ident)
                mm.then_inc(S["forget_turned"], 1)
                linear("bvA", stream, l, tokens=NB)
                o = fill("bft", l)
                pe.wait_ge(S["forget_sum"], l + 1)
                for b in range(NB):
                    if b == 0:
                        plain(pe)
                    mm = pe.transpose(o[:, b * H:b * H + H], fF[0:H, b * P:b * P + P], ident[0:H, 0:H])
                mm.then_inc(S["forget_turned"], 1)
                pe.wait_ge(S["forget_split"], l + 1)
                for g in range(2):
                    o = fill(f"bfb{g}", l)
                    for h in range(4):
                        for n, part_of_sum in enumerate((fFH, fFL)):
                            mm = pe.matmul(o[:, h * T:h * T + T], onehot[0:H, 4 * g + h, :], part_of_sum[0:H, :],
                                           start=(n == 0), stop=(n == 1))
                    mm.then_inc(S["forget_spread"], 1)

                def attend(br, blocks, keys, values, after):
                    scored, turned_half = (ps[jobs.half[name]] for name in after)

                    def half_free(name):
                        pe.wait_ge(drained[jobs.half[name]], jobs.nth(name, l))

                    def scores(i, p):
                        h = i * 2 + p
                        pe.wait_ge(S["heads_staged"], nth_head(br, l) + h + 1)
                        pe.wait_ge(S["heads_scores_read"], PRIMED + nth_head(br, l) + h)
                        for b, k0, n, at, _ in blocks:
                            mm = pe.matmul(scored[:, at:at + n], qz[:, p, b * P:b * P + P], keys(i, k0, n),
                                           start=True, stop=True)
                        mm.then_inc(S["heads_scores"], 1)

                    turned = turned_blocks(blocks)

                    def head(i, p, last):
                        h = i * 2 + p
                        pe.wait_ge(S["heads_probs"], nth_soft(br, l) + h + 1)
                        for n, (j, b, k0, at) in enumerate(turned):
                            mm = pe.transpose(turned_half[:, n * P:n * P + P],
                                              logit[:, p, at + j * P - k0:at + j * P - k0 + P], ident)
                        mm.then_inc(S["heads_turned"], 1)
                        if not last:
                            scores(i + 1, p)
                        pe.wait_ge(S["heads_turned_read"], nth_soft(br, l) + h + 1)
                        pe.wait_ge(S["heads_out_read"], PRIMED + nth_head(br, l) + h)
                        for b in range(NB):
                            mine = [(n, j) for n, (j, bb, _, _) in enumerate(turned) if bb == b]
                            for n, j in mine:
                                mm = pe.matmul(turned_half[:, 3 * T + b * HD:3 * T + b * HD + HD], probT[:, n * P:n * P + P],
                                               values(j, i, p), start=(n == mine[0][0]), stop=(n == mine[-1][0]))
                        mm.then_inc(S["heads_out"], 1)

                    half_free(after[0])
                    scores(0, 0)
                    scores(0, 1)
                    half_free(after[1])
                    plain(pe)
                    with pe.Fori(0, 3) as i:
                        head(i, 0, False)
                        head(i, 1, False)
                    head(3, 0, True)
                    head(3, 1, True)
                    pe.wait_ge(S["heads_out_read"], PRIMED + nth_head(br, l) + H)

                def turn_out(name, mixed=otm):
                    o = fill(name, l)
                    for c in range(NB):
                        for b in range(NB):
                            mm = pe.transpose(o[:, c * T + b * P:c * T + b * P + P], mixed[:, b, c * P:c * P + P], ident)
                    mm.then_inc(S["y_turned"], 1)

                attend("fox", causal, lambda i, k0, n: K[:, ds(i, 1), k0:k0 + n].rearrange("p a b -> p (a b)"),
                       lambda j, i, p: V[:, j, ds(i * P + p * HD, HD)], AFTER["fox"])
                attend("dsa", causal, lambda i, k0, n: kBB[:, k0:k0 + n],
                       lambda j, i, p: mix2[:, j, MVB:MVB + HD], AFTER["dsa"])
                turn_out("btA")
                turn_out("btB", otm2)
                for name in ("bqC", "bkC"):
                    linear(name, stream, l)
                linear("bvC", stream, l, tokens=NB)

                for name in ("bqD", "bgC"):
                    pe.wait_ge(drained[jobs.half[name]], jobs.nth(name, l))
                pe.wait_ge(S["roped"], PRIMED + l * 5 + 4)
                read_out(pe, "bvC", l)

                def ret_scores(i, p):
                    h = i * 2 + p
                    pe.wait_ge(S["heads_staged"], nth_head("ret", l) + h + 1)
                    pe.wait_ge(S["heads_scores_read"], PRIMED + nth_head("ret", l) + h)
                    for j, n, at, _ in forward:
                        mm = pe.matmul(ps[0][:, at:at + n], qz[:, p, j * P:j * P + P],
                                       Q[:, ds(i, 1), j * P:T].rearrange("p a b -> p (a b)"), start=True, stop=True)
                    mm.then_inc(S["heads_scores"], 1)

                def ret_out(i, p):
                    h = i * 2 + p
                    pe.wait_ge(S["heads_scores_read"], PRIMED + nth_head("ret", l) + h + 1)
                    pe.wait_ge(S["heads_out_read"], PRIMED + nth_head("ret", l) + h)
                    for b in range(NB):
                        for j in range(b + 1):
                            at = forward[j][3] + (b - j) * P
                            mm = pe.matmul(ps[1][:, 3 * T + b * HD:3 * T + b * HD + HD], logit[:, p, at:at + P],
                                           V[:, j, ds(i * P + p * HD, HD)], start=(j == 0), stop=(j == b))
                    mm.then_inc(S["heads_out"], 1)

                ret_scores(0, 0)
                with pe.Fori(0, 3) as i:
                    ret_scores(i, 1)
                    ret_out(i, 0)
                    ret_scores(i + 1, 0)
                    ret_out(i, 1)
                ret_scores(3, 1)
                ret_out(3, 0)
                ret_out(3, 1)
                pe.wait_ge(S["heads_out_read"], PRIMED + nth_head("ret", l) + H)
                linear("bqD", stream, l)
                linear("bgC", stream, l)
                pe.wait_ge(S["kk_copied"], l * 2 + 2)
                attend("swa", window, lambda i, k0, n: kDD[:, ds(i // 2, 1), k0:k0 + n].rearrange("p a b -> p (a b)"),
                       lambda j, i, p: mix2[:, j, ds(i // 2 * HD + MVD, HD)], AFTER["swa"])
                pe.wait_ge(S["group_normed"], l + 1)
                turn_out("btC")
                turn_out("btD", otm2)
                with pe.Fori(0, 2) as c:
                    for n, (high, rest) in enumerate(((yAH, yAL), (yBH, yBL), (yCH, yCL), (yDH, yDL))):
                        linear(f"bgt{n}", stream, l, c)
                        if n == 2:
                            pe.wait_ge(S["yc_split"], l + 1)
                        linear(f"bbr{n}", split(high, rest), l, c)
                linear("bwo0", halves(merged_bH, merged_bL), l, ready=lambda k: (S[f"merged_b_split{k // 4}"], l + 1))
                linear("bwo1", halves(merged_bH, merged_bL), l)
                square_sum("bss_ff", l)
                with pe.Fori(0, 5) as i:
                    linear("bupa", stream, l, i, ready=normed("bss_ff", l))
                    linear("bupb", stream, l, i)
                linear("bupc", stream, l)
                linear("bdn0", split(ffH, ffL), l, ready=multiplied(NG + l * NG))
                linear("bdn1", split(ffH, ffL), l)
            square_sum("css_fin")
            pe.wait_ge(S["normed"], WHOLE_NORMS["css_fin"])
            for g in range(2):
                o = fill(f"cout{g}")
                for b in range(NB):
                    for c in range(4):
                        mm = pe.transpose(o[:, b * T + c * P:b * T + c * P + P], hT[:, 4 * g + c, b * P:b * P + P], ident)
                mm.then_inc(S["out_turned"], 1)

        @block.scalar
        def _(act):
            link = Chain(act, S["act_step"])
            act.dma_start(consts[:, 0:2 * P], I["consts"][:, 0:2 * P]).then_inc(S["consts_loaded"], 16)
            for at, key in ((V_MIX, "mix_norm_g"), (V_MEM, "mem_norm_g"), (V_XA, "xattn_norm_g"), (V_FF, "ffn_norm_g"),
                            (V_FIN, "final_norm_g"), (V_FIN2, "final_norm_2"), (V_D, "s5_d")):
                n = I[key].shape[-1] // P
                act.dma_start(vrow[at:at + n, 0, :], I[key].rearrange("(r p) -> r p", p=P)).then_inc(S["vecs_loaded"], 16)
            act.dma_start(row[0:32, 4, :], I["s5_lam_re"]).then_inc(S["s5_loaded"], 16)
            act.dma_start(row[0:32, 5, :], I["s5_lam_im"]).then_inc(S["s5_loaded"], 16)
            act.dma_start(row[0:32, 6, 0:2], I["s5_log_step"]).then_inc(S["s5_loaded"], 16)
            act.dma_start(mem_in, I["mem"].rearrange("(b p) d -> p b d", p=P)).then_inc(S["mem_loaded"], 16)
            act.dma_start(consts[:, 2 * P:], I["consts"][:, 2 * P:N_CONSTS]).then_inc(S["tables_loaded"], 16)

            def evac(dst, src, h, func=ACT.Copy, **kw):
                act.activation(dst, src, func, **kw).then_inc(drained[h], 1)

            def round_units(name, l, i, units, cols):
                for u in units:
                    s, p = ring.slot[(name, u)], ring.split[(name, u)]
                    act.wait_ge(landed[s], ring.at(ring.landed, name, u, l, i))
                    free = ring.at(ring.before, name, u, l, i) + ring.split_room[(name, u)]
                    if not isinstance(free, int) or free > 0:
                        act.wait_ge(weights_used, free)
                    act.activation(wH[:, p, 0:cols], slot[:, s, 0:cols], ACT.Copy).then_inc(weights_high, 1)

            def ahead(name, l=0, i=0, cols=512):
                round_units(name, l, i, range(SPLITS), cols)

            def others(name, l=0, i=0, cols=512):
                round_units(name, l, i, range(SPLITS, ring.units[name]), cols)

            def square_first(name, src):
                act.activation(squares(name), src, ACT.Square).then_inc(S["squared_first"], 1)

            def square_half(name, l=0):
                act.wait_ge(S["residual"], state_parts(name, l) + 1)
                act.activation(squares(name)[:, 0:4, :], hT[:, 0:4, :], ACT.Square).then_inc(S["squared"], 1)

            def square_rest(name, l=0):
                for k in range(4, KD):
                    act.wait_ge(S["residual"], state_parts(name, l) + k - 2)
                    act.activation(squares(name)[:, k, :], hT[:, k, :], ACT.Square).then_inc(S["squared"], 1)

            def root(name, l=0, n=T):
                act.wait_ge(S["summed"], nth_norm(name, l))
                evac(rms[:, 0:n], ps[jobs.half[name]][:, 0:n], jobs.half[name], ACT.Sqrt, bias=eps, scale=1.0 / D)

            def round_norm(name, l=0):
                for k in range(KD):
                    act.wait_ge(S["normed_chunk"], split_chunks(name, l) + k + 1)
                    act.activation(nH[:, k, :], squares(name)[:, k, :], ACT.Copy).then_inc(S["normed_high"], 1)

            act.wait_ge(S["vecs_turned"], 1)
            evac(vec0[:, :], ps[jobs.half["avecs"]][:, 0:V_ROWS], jobs.half["avecs"])
            for g in range(2):
                act.wait_ge(S["x_turned"], g + 1)
                evac(hT[:, 4 * g:4 * g + 4, :], banks(jobs.half[f"ax{g}"]), jobs.half[f"ax{g}"])
            act.wait_ge(S["mem_turned"], 1)
            h = jobs.half["amemT"]
            evac(mT, ps[h][:, :].rearrange("p (c m) -> p c m", m=M), h)
            read_out(act, "amemT")
            square_first("ass_mem", mT)
            read_out(act, "ax0")
            read_out(act, "ax1")
            square_first("ass_mix", hT[:, :, :])
            act.wait_ge(S["constants_set"], 3)
            root("ass_mem", n=M)
            ahead("axa")
            act.wait_ge(S["normed"], WHOLE_NORMS["ass_mem"])
            root("ass_mix")
            round_norm("ass_mix")
            others("axa")

            R = [row[0:32, n, :] for n in range(24)]
            act.wait_ge(S["s5_loaded"], 48)
            act.activation(row[0:32, 7, 0:2], row[0:32, 6, 0:2], ACT.Exp).then_inc(S["s5_step"], 1)
            act.wait_ge(S["s5_exponent"], 1)
            act.activation(R[0], R[10], ACT.Exp).then_inc(S["s5_magnitude"], 1)
            act.wait_ge(S["s5_phase"], 1)
            link(act.activation(R[11], R[1], ACT.Abs))
            act.activation(R[12], R[1], ACT.Sin, scale=TWO_PI).then_inc(S["s5_circle"], 1)
            act.activation(R[13], R[11], ACT.Sin, bias=half_pi[0:32, :], scale=-TWO_PI).then_inc(S["s5_circle"], 1)
            done(act, "axa")
            evac(uT, banks(jobs.half["axa"]), jobs.half["axa"])
            act.wait_ge(S["s5_turned"], 1)
            h = jobs.half["as5col"]
            link(act.activation(s5col[:, :, :], ps[h][:, 0:4 * 32].rearrange("p (a b) -> p a b", b=32), ACT.Copy))
            evac(s5col[:, 1, 16:32], ps[h][:, 32 + 16:64], h, scale=-1.0)
            act.wait_ge(S["s5_turned"], 2)
            h = jobs.half["as5B"]
            evac(s5w[:, :, 0:2, :], ps[h][:, :].rearrange("p (q k s) -> p q k s", q=QUADS, k=2), h)
            act.wait_ge(S["s5_turned"], 3)
            h = jobs.half["as5C"]
            c_re, c_im = (ps[h][:, :].rearrange("p (q k s) -> p q k s", q=QUADS, k=2)[:, :, k, :] for k in range(2))
            act.activation(s5w[:, :, 2, :], c_re, ACT.Copy)
            act.activation(s5w[:, :, 3, :], c_re, ACT.Copy, scale=-1.0)
            evac(s5w[:, :, 4, :], c_im, h, scale=-1.0)
            read_out(act, "axa")
            read_out(act, "as5B")
            read_out(act, "as5C")
            read_out(act, "as5col")
            act.wait_ge(S["s5_bbar"], 1)
            act.wait_ge(S["iota_loaded"], 16)
            ahead("aglu")
            with act.Fori(0, 2) as c:
                act.wait_ge(S["s5_out"], PRIMED + c * 16)
                for e in range(2):
                    act.activation(ust[:, e, :], uT[:, ds(c * 2 + e, 1), :].rearrange("p a b -> p (a b)"), ACT.Copy)
                    for d in range(2):
                        ins = act.activation(stg[e][:, d, :], s5w[:, ds(c * 2 + (e + 4 * d), 1), :, :]
                                             .rearrange("p q a b -> p (q a b)"), ACT.Copy)
                    ins.then_inc(S["s5_staged"], 1)

                def turns(t):
                    col = t // 8 * 4 + t % 8 // 4 * 16 + t % 4
                    rate = s5col[:, 1, ds(c * 8 + col, 1)]
                    act.activation(turn[:, t % 2, :], rms[:, :], ACT.Copy, scale=rate)
                    act.activation(whole[:, t % 2, :], rms[:, :], ACT.Identity, scale=rate, bias=rounder).then_inc(S["s5_turns"], 1)

                turns(0)
                turns(1)
                for t in range(16):
                    p = t % 2
                    act.wait_ge(S["s5_fraction"], c * 16 + t + 1)
                    act.activation(whole[:, p, :], turn[:, p, :], ACT.Abs).then_inc(S["s5_abs"], 1)
                    if t >= 3:
                        act.wait_ge(S["s5_back_dve"], c * 16 + t - 2)
                        act.wait_ge(S["s5_back_pool"], PRIMED + c * 16 + t - 2)
                    act.activation(trig[:, t % 3, 1, :], turn[:, p, :], ACT.Sin, scale=-TWO_PI)
                    act.wait_ge(S["s5_abs"], c * 16 + t + 1)
                    act.activation(trig[:, t % 3, 0, :], whole[:, p, :], ACT.Sin, bias=half_pi, scale=-TWO_PI)\
                        .then_inc(S["s5_trig"], 1)
                    if t < 14:
                        act.wait_ge(S["s5_trig"], c * 16 + t + 1)
                        turns(t + 2)
            act.wait_ge(S["s5_y_read"], PRIMED + 4)
            act.activation(uT, uT, ACT.Gelu_apprx_tanh).then_inc(S["s5_gelu"], 1)
            act.wait_ge(S["s5_gelu"], 1)
            act.activation(yH, uT, ACT.Copy).then_inc(S["ya_high"], 1)
            ahead("azv0")
            done(act, "aglu")
            evac(svt, banks(jobs.half["aglu"]), jobs.half["aglu"], ACT.Sigmoid)
            others("azv0")
            act.wait_ge(S["ya_ready"], 1)
            act.activation(yH, uT, ACT.Copy).then_inc(S["ya_high"], 1)

            ahead("azv1")
            done(act, "azv0")
            evac(zv[:, :, 0:512], banks(jobs.half["azv0"]), jobs.half["azv0"], ACT.Gelu_apprx_tanh)
            others("azv1")
            ahead("azu0")
            done(act, "azv1")
            evac(zv[:, :, 512:1024], banks(jobs.half["azv1"]), jobs.half["azv1"], ACT.Gelu_apprx_tanh)
            others("azu0")
            ahead("azu1")
            act.wait_ge(S["zv_stats"], 1)
            act.activation(stat[:, 56:60], stat[:, 48:56].rearrange("p (a b) -> p a b", b=2)[:, :, 1], ACT.Sqrt, bias=eps)\
               .then_inc(S["zv_std"], 1)
            done(act, "azu0")
            evac(zu[:, 0:4, :], banks(jobs.half["azu0"]), jobs.half["azu0"], ACT.Gelu_apprx_tanh)
            others("azu1")
            act.wait_ge(S["ya_split"], 2)
            act.activation(mH, mT, ACT.Copy).then_inc(S["mem_high"], 1)
            done(act, "azu1")
            evac(zu[:, 4:8, :], banks(jobs.half["azu1"]), jobs.half["azu1"], ACT.Gelu_apprx_tanh)
            act.wait_ge(S["ws_turned"], 1)
            h = jobs.half["awsT"]
            evac(wsT, ps[h][:, 0:H * P].rearrange("p (a b) -> p a b", b=P), h)
            with act.Fori(0, 2) as c:
                ahead("aga", 0, c)
                others("aga", 0, c)
                ahead("apa", 0, c)
                for n, (key, then) in enumerate((("ga", "gb"), ("gb", None))):
                    done(act, "a" + key, 0, c)
                    act.wait_ge(drained[jobs.half["apa"]], jobs.nth("apa", 0, c) + (n - 1))
                    h = jobs.half["a" + key]
                    evac(gate_a[n], banks(h), h, ACT.Sigmoid)
                    if n == 0:
                        ahead("agb", 0, c)
                        others("agb", 0, c)
                        ahead("apb", 0, c)
                others("apb", 0, c)

            def round_merged(c, ready, merged, high, signal):
                act.wait_ge(*ready)
                act.activation(high[c], merged[:, 4 * c:4 * c + 4, :], ACT.Copy).then_inc(signal, 1)

            round_merged(0, (S["merged_a"], 1), merged_a, merged_aH, S["merged_a_high"])
            ahead("awo0")
            round_merged(1, (S["merged_a"], 2), merged_a, merged_aH, S["merged_a_high"])
            others("awo0")
            ahead("awo1")
            square_half("ass_xa")
            others("awo1")

            ahead("awk0")
            others("awk0")
            square_rest("ass_xa")
            ahead("awk1")
            done(act, "awk0")
            evac(xk[:, 0:4, :], banks(jobs.half["awk0"], w=M), jobs.half["awk0"])
            others("awk1")
            ahead("awv0")
            done(act, "awk1")
            evac(xk[:, 4:8, :], banks(jobs.half["awk1"], w=M), jobs.half["awk1"])
            others("awv0")
            ahead("awv1")
            done(act, "awv0")
            evac(xv[:, :, 0:512], banks(jobs.half["awv0"], n=2), jobs.half["awv0"])
            others("awv1")
            ahead("awq0")
            done(act, "awv1")
            evac(xv[:, :, 512:1024], banks(jobs.half["awv1"], n=2), jobs.half["awv1"])
            root("ass_xa")
            round_norm("ass_xa")
            others("awq0")
            ahead("awq1")
            done(act, "awq0")
            evac(xq[:, 0:4, :], banks(jobs.half["awq0"]), jobs.half["awq0"])
            others("awq1")
            ahead("axo0")
            done(act, "awq1")
            evac(xq[:, 4:8, :], banks(jobs.half["awq1"]), jobs.half["awq1"])

            def x_exp(h):
                act.wait_ge(S["x_max"], h + 1)
                p, half = h % 2, jobs.half[f"axs{h}"]
                for b in range(NB):
                    ins = act.activation(xp[:, p, b, :], ps[half][:, b * M:b * M + M], ACT.Exp, scale=float((D // 4) ** -0.5),
                                         bias=stat[:, 64 + 4 * p + b:65 + 4 * p + b], accum_out=stat[:, 72 + 4 * p + b:73 + 4 * p + b])
                ins.then_inc(drained[half], 1)

            def x_turned(h):
                act.wait_ge(S["x_probs_turned"], h + 1)
                evac(xpT[:, h % 2, :, :], banks(jobs.half[f"axt{h}"], n=2), jobs.half[f"axt{h}"])

            def x_outs(h):
                act.wait_ge(S["x_out"], h + 1)
                act.activation(xoH[:, 2 * h:2 * h + 2, :], banks(jobs.half[f"axv{h}"], n=2), ACT.Copy).then_inc(S["xo_high"], 1)

            x_exp(0)
            x_exp(1)
            x_turned(0)
            x_exp(2)
            x_outs(0)
            x_turned(1)
            x_exp(3)
            x_outs(1)
            for h in (2, 3):
                x_turned(h)
                x_outs(h)
            others("axo0")
            ahead("axo1")
            square_half("ass_ff")
            others("axo1")
            ahead("aupa")
            square_rest("ass_ff")
            root("ass_ff")
            round_norm("ass_ff")

            def round_ff(raw, g):
                act.activation(ffH[:, ds(g * 2, 2), :], raw, ACT.Copy).then_inc(S["ff_high"], 1)

            def round_ff_a(name, g, p, i=0):
                read_out(act, name, 0, i)
                round_ff(ff_raw[:, p, :, :], g)

            def silu_a(name, p, i=0):
                done(act, name, 0, i)
                act.activation(sg_a[:, p, :, :], banks(jobs.half[name], n=2), ACT.Silu).then_inc(S["silu_a"], 1)

            with act.Fori(0, 5) as i:
                others("aupa", 0, i)
                ahead("aupb", 0, i)
                silu_a("aupa", 0, i)
                others("aupb", 0, i)
                round_ff_a("aupa", i * 2, 0, i)
                ahead("aupa", 0, i + 1)
                silu_a("aupb", 1, i)
                round_ff_a("aupb", i * 2 + 1, 1, i)
            others("aupc")
            ahead("adn0")
            silu_a("aupc", 0)
            round_ff_a("aupc", NG - 1, 0)
            others("adn0")
            ahead("adn1")
            square_half("ass_fin")
            others("adn1")
            square_rest("ass_fin")
            root("ass_fin")
            square_half("bss_at")

            act.wait_ge(S["tables_loaded"], 16)
            act.wait_ge(S["zeros_set"], 5)
            with act.Fori(0, LAYERS) as l:
                act.wait_ge(S["layer_vecs_turned"], l + 1)
                h = jobs.half["bvecs"]
                evac(vec[:, :], ps[h][:, 0:W_ROWS1 + W_ROWS2], h)
                square_rest("bss_at", l)
                ahead("bmix1", l)
                root("bss_at", l)
                round_norm("bss_at", l)

                def rope_read(name, dst, turn_no):
                    done(act, name, l)
                    act.wait_ge(S["roped"], PRIMED + l * 5 + turn_no)
                    h = jobs.half[name]
                    act.activation(dst, banks(h), ACT.Copy)
                    for r in range(0, P, 32):
                        ins = act.activation(part[r:r + 32, :, :], banks(h)[r ^ 32:(r ^ 32) + 32, :, :], ACT.Copy)
                    ins.then_inc(drained[h], 1)

                others("bmix1", l)
                ahead("bmix2", l, cols=MIX2)
                done(act, "bmix1", l)
                act.wait_ge(S["roped"], PRIMED + l * 5)
                h = jobs.half["bmix1"]
                act.activation(mix1[:, 0:2, :], banks(h, n=2), ACT.Copy)
                for r in range(0, P, 32):
                    if r == HD:
                        round_units("bmix2", l, 0, range(SPLITS, SPLITS + 2), MIX2)
                    ins = act.activation(part[r:r + 32, 0:2, :], banks(h, n=2)[r ^ 32:(r ^ 32) + 32, :, :], ACT.Copy)
                ins.then_inc(S["mix1_copied"], 1)
                round_units("bmix2", l, 0, range(SPLITS + 2, KD), MIX2)
                ahead("bqB", l)
                done(act, "bmix2", l)
                h = jobs.half["bmix2"]
                evac(mix2, banks(h, w=MIX2), h)
                act.wait_ge(S["roped"], PRIMED + l * 5 + 1)
                for r in (0, HD):
                    ins = act.activation(kII[r:r + HD, :], mix1[HD:P, 2, :], ACT.Copy)
                ins.then_inc(S["kk_copied"], 1)
                for r in (0, HD):
                    act.activation(kBB[r:r + HD, :], mix1[0:HD, 2, :], ACT.Copy)
                for b in range(1, NB):
                    act.wait_ge(S["index_dots"], l * 3 + b)
                    act.wait_ge(S["index_scored"], PRIMED + l * 3 + b - 1)
                    h = jobs.half[f"bix{b}"]
                    evac(relu[:, :, 0:(b + 1) * P], banks(h, w=(b + 1) * P), h, ACT.Relu)
                others("bqB", l)
                ahead("bqA", l)
                rope_read("bqB", qB, 1)
                others("bqA", l)
                ahead("bkA", l)
                done(act, "bqA", l)
                evac(Q, banks(jobs.half["bqA"]), jobs.half["bqA"])
                others("bkA", l)
                ahead("bvA", l)
                done(act, "bkA", l)
                evac(K, banks(jobs.half["bkA"]), jobs.half["bkA"])
                act.wait_ge(S["forget_turned"], l * 2 + 1)
                h = jobs.half["blf"]
                evac(fx[0:H, :], ps[h][0:H, 0:T], h, ACT.Identity, bias=fbias[0:H, :])
                read_out(act, "blf", l)
                steps = Chain(act, S["forget_step"], l * 2)
                steps(act.activation(fe[0:H, :], fx[0:H, :], ACT.Abs))
                steps(act.activation(fe[0:H, :], fe[0:H, :], ACT.Exp, scale=-1.0))
                act.activation(fe[0:H, :], fe[0:H, :], ACT.Ln, bias=ones[0:H, 0:1]).then_inc(S["forget_log"], 1)
                others("bvA", l)
                ahead("bqC", l)
                done(act, "bvA", l)
                evac(V, banks(jobs.half["bvA"]), jobs.half["bvA"])
                act.wait_ge(S["forget_turned"], l * 2 + 2)
                h = jobs.half["bft"]
                evac(ftm[:, :, :], ps[h][:, 0:NB * H].rearrange("p (b h) -> p b h", h=H), h)
                act.wait_ge(S["roped"], PRIMED + l * 5 + 2)
                plain(act)
                for g in range(2):
                    act.wait_ge(S["forget_spread"], l * 2 + g + 1)
                    h = jobs.half[f"bfb{g}"]
                    evac(fb[:, 4 * g:4 * g + 4, :], banks(h), h)

                def stage(br, src, i, p, scale=HD ** -0.5):
                    act.activation(qz[HD * p:HD * p + HD, p, :], src[HD * p:HD * p + HD, ds(i, 1), :]
                                   .rearrange("p a b -> p (a b)"), ACT.Copy, scale=scale).then_inc(S["heads_staged"], 1)

                def attend(br, blocks, src, sinks=False):
                    turned_half = ps[jobs.half[AFTER[br][1]]]

                    def exps(i, p, first=False):
                        h = i * 2 + p
                        if not first:
                            act.wait_ge(S["heads_inverse"], PRIMED + nth_soft(br, l) + h - 1)
                        act.wait_ge(S["heads_scores_read"], PRIMED + nth_head(br, l) + h + 1)
                        if sinks:
                            act.activation(stat[:, 88 + 4 * p:92 + 4 * p], stat[:, 64 + 4 * p:68 + 4 * p], ACT.Exp,
                                           bias=sink[:, ds(h, 1)])
                        for b, _, n, _, at in blocks:
                            ins = act.activation(logit[:, p, at:at + n], logit[:, p, at:at + n], ACT.Exp,
                                                 bias=stat[:, 64 + 4 * p + b:65 + 4 * p + b],
                                                 accum_out=stat[:, 72 + 4 * p + b:73 + 4 * p + b])
                        ins.then_inc(S["heads_probs"], 1)

                    n = len(turned_blocks(blocks)) * P

                    def head(i, p, last):
                        h = i * 2 + p
                        if not last:
                            act.wait_ge(S["heads_scores"], nth_head(br, l) + h + 1)
                            stage(br, src, i + 1, p)
                        act.wait_ge(S["heads_turned"], nth_soft(br, l) + h + 1)
                        act.activation(probT[:, 0:n], turned_half[:, 0:n], ACT.Copy).then_inc(S["heads_turned_read"], 1)
                        if p == 0:
                            exps(i, 1)
                        elif not last:
                            exps(i + 1, 0)

                    stage(br, src, 0, 0)
                    stage(br, src, 0, 1)
                    exps(0, 0, True)
                    with act.Fori(0, 3) as i:
                        head(i, 0, False)
                        head(i, 1, False)
                    head(3, 0, True)
                    head(3, 1, True)

                def turn_out(name, k, high):
                    act.wait_ge(S["y_turned"], l * 4 + k)
                    act.activation(high, banks(jobs.half[name]), ACT.Copy).then_inc(S["y_high"], 1)

                read_out(act, "bqA", l)
                attend("fox", causal, Q)
                attend("dsa", causal, qB)
                turn_out("btA", 1, yAH)
                turn_out("btB", 2, yBH)
                others("bqC", l)
                ahead("bkC", l)
                rope_read("bqC", Q, 2)
                others("bkC", l)
                ahead("bvC", l)
                rope_read("bkC", K, 3)
                others("bvC", l)
                ahead("bqD", l)
                done(act, "bvC", l)
                evac(V, banks(jobs.half["bvC"]), jobs.half["bvC"])

                def ret_stage(i, p):
                    h = i * 2 + p
                    stage("ret", K, i, p)
                    act.activation(decay[:, p, :], C["dist"], ACT.Exp, scale=C["logdecay"][:, ds(h, 1)])\
                        .then_inc(S["ret_decay"], 1)

                def ret_head(i, p, last):
                    h = i * 2 + p
                    if not last:
                        act.wait_ge(S["heads_scores"], nth_head("ret", l) + h + 1)
                        act.wait_ge(S["heads_scores_read"], PRIMED + nth_head("ret", l) + h + 1)
                        ret_stage(i + 1, p)
                    act.wait_ge(S["heads_out"], nth_head("ret", l) + h + 1)
                    act.activation(otm[:, :, ds(i * P + p * HD, HD)], ps[1][:, 3 * T:3 * T + NB * HD]
                                   .rearrange("p (b d) -> p b d", d=HD), ACT.Copy).then_inc(S["heads_out_read"], 1)

                act.wait_ge(S["roped"], PRIMED + l * 5 + 4)
                ret_stage(0, 0)
                ret_stage(0, 1)
                with act.Fori(0, 3) as i:
                    ret_head(i, 0, False)
                    ret_head(i, 1, False)
                ret_head(3, 0, True)
                ret_head(3, 1, True)
                act.wait_ge(S["group_centred"], l + 1)
                act.activation(gsq, otm, ACT.Square).then_inc(S["group_squared"], 1)
                act.wait_ge(S["group_var"], l + 1)
                act.activation(stat[:, 0:32], stat[:, 32:64], ACT.Sqrt, bias=eps, scale=1.0 / HD).then_inc(S["group_std"], 1)
                others("bqD", l)
                ahead("bgC", l)
                rope_read("bqD", qD, 4)
                for g in range(2):
                    for r in (0, HD):
                        ins = act.activation(kDD[r:r + HD, g, :], mix1[HD * g:HD * g + HD, 3, :], ACT.Copy)
                ins.then_inc(S["kk_copied"], 1)
                others("bgC", l)
                done(act, "bgC", l)
                evac(gC, banks(jobs.half["bgC"]), jobs.half["bgC"], ACT.Silu)
                act.wait_ge(S["roped"], PRIMED + l * 5 + 5)
                attend("swa", window, qD, sinks=True)
                ahead("bgt0", l)
                read_out(act, "btC", l)
                act.activation(yCH, gC, ACT.Copy).then_inc(S["y_high"], 1)
                turn_out("btD", 4, yDH)

                def gates(c):
                    for n in range(4):
                        others(f"bgt{n}", l, c)
                        ahead(f"bbr{n}", l, c)
                        done(act, f"bgt{n}", l, c)
                        act.wait_ge(drained[jobs.half["bbr0"]], jobs.nth("bbr0", l, c) + (n - 1))
                        h = jobs.half[f"bgt{n}"]
                        evac(gate_b[n % 2], banks(h), h, ACT.Sigmoid)
                        if n < 3:
                            ahead(f"bgt{n + 1}", l, c)
                        elif c == 0:
                            ahead("bgt0", l, 1)

                gates(0)
                gates(1)
                round_merged(0, (S["merged_b"], PRIMED + l * 6 + 3), merged_b, merged_bH, S["merged_b_high"])
                ahead("bwo0", l)
                round_merged(1, (S["merged_b"], PRIMED + l * 6 + 6), merged_b, merged_bH, S["merged_b_high"])
                others("bwo0", l)
                ahead("bwo1", l)
                square_half("bss_ff", l)
                others("bwo1", l)
                ahead("bupa", l)
                square_rest("bss_ff", l)
                root("bss_ff", l)
                round_norm("bss_ff", l)

                def conv_last(name, g, p, i=0):
                    done(act, name, l, i)
                    act.wait_ge(S["ff_split"], NG + l * NG + g - 1)
                    h = jobs.half[name]
                    for j in range(4):
                        ch = g * 2 + (j if j < 2 else NF + j - 2)
                        ins = act.activation(conv[:, p, j, :], ps[h][:, j * T:j * T + T], ACT.Identity,
                                             scale=vec[:, ds(ch + W_C2, 1)], bias=vec[:, ds(ch + W_CB, 1)])
                    ins.then_inc(S["conv_begun"], 1)

                def silu_b(name, g, p, i=0):
                    read_out(act, name, l, i)
                    act.activation(conv[:, p, 0:2, :], conv[:, p, 0:2, :], ACT.Silu).then_inc(S["silu_b"], 1)

                def round_ff_b(g, p):
                    act.wait_ge(S["ff_ready"], l * NG + g + 1)
                    round_ff(conv[:, p, 0:2, :], g)

                others("bupa", l)
                with act.Fori(0, 5) as i:
                    ahead("bupb", l, i)
                    conv_last("bupa", i * 2, 0, i)
                    others("bupb", l, i)
                    silu_b("bupa", i * 2, 0, i)
                    ahead("bupa", l, i + 1)
                    conv_last("bupb", i * 2 + 1, 1, i)
                    round_ff_b(i * 2, 0)
                    others("bupa", l, i + 1)
                    silu_b("bupb", i * 2 + 1, 1, i)
                    round_ff_b(i * 2 + 1, 1)
                ahead("bdn0", l)
                conv_last("bupc", NG - 1, 0)
                round_units("bdn0", l, 0, range(SPLITS, 7), 512)
                silu_b("bupc", NG - 1, 0)
                round_ff_b(NG - 1, 0)
                round_units("bdn0", l, 0, range(7, NF), 512)
                ahead("bdn1", l)
                square_half("bss_at", l + 1)
                others("bdn1", l)
            square_rest("css_fin")
            root("css_fin")
            for g in range(2):
                act.wait_ge(S["out_turned"], g + 1)
                h = jobs.half[f"cout{g}"]
                evac(o_out[:, :, 512 * g:512 * g + 512], banks(h), h)

        @block.vector
        def _(dve):
            link = Chain(dve, S["dve_step"])
            for name in ("heads_scores_read", "heads_out_read", "heads_inverse", "s5_y_read", "roped", "index_scored", "merged_b"):
                dve.sem_inc(S[name], PRIMED)
            dve.memset(eps, EPS).then_inc(S["constants_set"], 1)
            dve.memset(half_pi, float(np.pi / 2)).then_inc(S["constants_set"], 1)
            dve.memset(rounder, ROUND).then_inc(S["constants_set"], 1)

            def inverse_root(name, l=0, n=T):
                read_out(dve, name, l)
                dve.reciprocal(rms[:, 0:n], rms[:, 0:n]).then_inc(S["rstd"], 1)
                dve.wait_ge(S["rstd"], nth_norm(name, l))

            def norm(name, buf, gains, n=T, new_state=False):
                inverse_root(name, 0, n)
                for k in range(KD):
                    ins = dve.scalar_tensor_tensor(out=buf[:, k, :], in0=buf[:, k, :], scalar=gains[:, k:k + 1],
                                                   in1=rms[:, 0:n], op0=ALU.mult, op1=ALU.mult)
                    if new_state and k >= 3:
                        ins.then_inc(S["residual"], 1)
                if not new_state:
                    ins.then_inc(S["normed"], 1)

            def split_norm(name, gains, l=0):
                inverse_root(name, l)
                first = split_chunks(name, l)

                def whole_chunk(k):
                    dve.scalar_tensor_tensor(out=squares(name)[:, k, :], in0=hT[:, k, :], scalar=gains[:, k:k + 1], in1=rms[:, :],
                                             op0=ALU.mult, op1=ALU.mult).then_inc(S["normed_chunk"], 1)

                whole_chunk(0)
                whole_chunk(1)
                for k in range(KD):
                    dve.wait_ge(S["normed_high"], first + k + 1)
                    dve.tensor_tensor(nL[:, k, :], squares(name)[:, k, :], plainly(nH[:, k, :]), ALU.subtract).then_inc(S["normed_split"], 1)
                    if k + 2 < KD:
                        whole_chunk(k + 2)

            def rest(part, whole_value, high):
                return dve.tensor_tensor(part, whole_value, plainly(high), ALU.subtract)

            def half_sum(name, l=0):
                sq = squares(name)
                dve.wait_ge(S["squared"], state_parts(name, l) + 1)
                dve.tensor_tensor(sq[:, 0:2, :], sq[:, 0:2, :], sq[:, 2:4, :], ALU.add).then_inc(S["quarters_summed"], 1)
                dve.wait_ge(S["quarters_summed"], state(name, l) + 1)
                dve.tensor_tensor(sq[:, 0, :], sq[:, 0, :], sq[:, 1, :], ALU.add).then_inc(S["half_summed"], 1)

            def add_back(jobs_of, name, l=0, next_l=0):
                parts = state_parts(name, next_l)
                done(dve, jobs_of + "0", l)
                h = jobs.half[jobs_of + "0"]
                dve.tensor_tensor(hT[:, 0:4, :], hT[:, 0:4, :], banks(h), ALU.add).then_inc(S["residual"], 1)
                dve.wait_ge(S["residual"], parts + 1)
                dve.sem_inc(drained[h], 1)
                half_sum(name, next_l)
                done(dve, jobs_of + "1", l)
                h = jobs.half[jobs_of + "1"]
                for k in range(4):
                    dve.tensor_tensor(hT[:, 4 + k, :], hT[:, 4 + k, :], banks(h)[:, k, :], ALU.add).then_inc(S["residual"], 1)
                dve.wait_ge(S["residual"], parts + 5)
                dve.sem_inc(drained[h], 1)

            def wide(v, n):
                return v.unsqueeze(2).to_broadcast([v.shape[0], v.shape[1], n])

            read_out(dve, "avecs")
            norm("ass_mem", mT, vec0[:, V_MEM:V_MEM + KD], n=M)
            split_norm("ass_mix", vec0[:, V_MIX:V_MIX + KD])

            R = [row[0:32, n, :] for n in range(24)]
            lre, lim, lr, theta, k, r, sin, cos, nr, li, den, t1, t2 = (R[n] for n in (4, 5, 10, 8, 9, 1, 12, 13, 14, 15, 16, 17, 18))
            step = row[0:32, 7, 0:2].unsqueeze(2).to_broadcast([32, 2, STATE])

            def halves(v):
                return v.rearrange("p (g s) -> p g s", s=STATE)

            dve.wait_ge(S["s5_loaded"], 48)
            dve.wait_ge(S["s5_step"], 1)
            dve.tensor_tensor(halves(lr), halves(lre), step, ALU.mult).then_inc(S["s5_exponent"], 1)
            link(dve.tensor_tensor(halves(theta), halves(lim), step, ALU.mult))
            link(dve.tensor_scalar(k, theta, INV_2PI, ROUND, ALU.mult, ALU.add))
            link(dve.tensor_scalar(k, k, ROUND, None, ALU.subtract))
            link(dve.scalar_tensor_tensor(out=t1, in0=k, scalar=-C1, in1=theta, op0=ALU.mult, op1=ALU.add))
            link(dve.scalar_tensor_tensor(out=t2, in0=k, scalar=-C2, in1=t1, op0=ALU.mult, op1=ALU.add))
            dve.tensor_scalar(r, t2, INV_2PI, None, ALU.mult).then_inc(S["s5_phase"], 1)
            link(dve.tensor_tensor(t1, lre, lre, ALU.mult))
            link(dve.tensor_tensor(t2, lim, lim, ALU.mult))
            link(dve.tensor_tensor(den, t1, t2, ALU.add))
            link(dve.reciprocal(den, den))
            dve.wait_ge(S["s5_magnitude"], 1)
            dve.wait_ge(S["s5_circle"], 2)
            link(dve.tensor_tensor(nr, R[0], cos, ALU.mult))
            link(dve.tensor_scalar(nr, nr, 1.0, None, ALU.subtract))
            link(dve.tensor_tensor(li, R[0], sin, ALU.mult))
            link(dve.tensor_tensor(t1, nr, lre, ALU.mult))
            link(dve.tensor_tensor(t2, li, lim, ALU.mult))
            link(dve.tensor_tensor(t1, t1, t2, ALU.add))
            link(dve.tensor_tensor(R[2], t1, den, ALU.mult))
            link(dve.tensor_tensor(t1, li, lre, ALU.mult))
            link(dve.tensor_tensor(t2, nr, lim, ALU.mult))
            link(dve.tensor_tensor(t1, t1, t2, ALU.subtract))
            dve.tensor_tensor(R[3], t1, den, ALU.mult).then_inc(S["s5_params"], 1)
            read_out(dve, "as5col")
            dve.wait_ge(S["s5b_loaded"], 32)
            f_re, f_im = (wide(s5col[:, n, :], CHAN) for n in (2, 3))
            for n, (b, f) in enumerate(((0, f_re), (1, f_im), (1, f_re), (0, f_im))):
                link(dve.tensor_tensor(bprod[n], bnat[b], f, ALU.mult))
            dve.wait_ge(S["zeros_set"], 4)
            for g in range(2):
                at, ch = slice(STATE * g, STATE * g + STATE), slice(CHAN * g, CHAN * g + CHAN)
                dve.tensor_tensor(zb[0][at, :, ch], bprod[0][at], bprod[1][at], ALU.subtract)
                ins = dve.tensor_tensor(zb[1][at, :, ch], bprod[2][at], bprod[3][at], ALU.add)
            ins.then_inc(S["s5_bbar"], 1)

            read_out(dve, "as5C")
            read_out(dve, "axa")
            with dve.Fori(0, 2) as c:
                def fraction(t):
                    p = t % 2
                    dve.wait_ge(S["s5_turns"], c * 16 + t + 1)
                    dve.scalar_tensor_tensor(out=turn[:, p, :], in0=whole[:, p, :], scalar=ROUND, in1=turn[:, p, :],
                                             op0=ALU.subtract, op1=ALU.subtract).then_inc(S["s5_fraction"], 1)

                def rotate(t):
                    dve.wait_ge(S["s5_driven"], c * 16 + t + 1)
                    dve.wait_ge(S["s5_trig"], c * 16 + t + 1)
                    dve.wait_ge(S["s5_out"], PRIMED + c * 16 + (t - 2 if t >= 3 else 0))
                    for n, (b, f) in enumerate(((0, 0), (1, 1), (1, 0), (0, 1))):
                        bank = 2 * (t % 2) + b
                        ins = dve.tensor_tensor(prod[:, t % 3, n, :], ps[0][:, bank * T:bank * T + T], trig[:, t % 3, f, :], ALU.mult)
                    ins.then_inc(S["s5_rotated"], 1)

                def scan(t):
                    p, d = t % 2, t % 8 // 4
                    dve.wait_ge(S["s5_z"], c * 16 + t + 1)
                    dve.wait_ge(S["s5_back_pool"], PRIMED + c * 16 + (t - 1 if t >= 2 else 0))
                    col = t // 8 * 4 + d * 16 + t % 4
                    decay_rate = s5col[:, 0, ds(c * 8 + col, 1)].to_broadcast([P, T])
                    for n in range(2):
                        o, z = st[:, p, n, :], zt[:, p, n, :]
                        if d:
                            o, z = o[:, ::-1], z[:, ::-1]
                        dve.tensor_tensor_scan(o, decay_rate, z, 0.0, ALU.mult, ALU.add).then_inc(S["s5_scanned"], 1)
                    dve.wait_ge(S["s5_scanned"], c * 32 + 2 * t + 2)
                    for n in range(2):
                        ins = dve.tensor_tensor(prod[:, t % 3, n, :], st[:, p, n, :], trig[:, t % 3, n, :], ALU.mult)
                    ins.then_inc(S["s5_back_dve"], 1)

                def output(e):
                    dve.wait_ge(S["s5_out"], PRIMED + c * 16 + 8 * e + 8)
                    u = uT[:, ds(c * 2 + e, 1), :].rearrange("p a b -> p (a b)")
                    dve.scalar_tensor_tensor(out=u, in0=u, scalar=vec0[:, ds(c * 2 + (e + V_D), 1)], in1=ps[1][:, e * T:e * T + T],
                                             op0=ALU.mult, op1=ALU.add).then_inc(S["s5_y_read"], 1)

                fraction(0)
                fraction(1)
                for t in range(16):
                    rotate(t)
                    if t < 14:
                        fraction(t + 2)
                    if t:
                        scan(t - 1)
                    if t == 11:
                        output(0)
                scan(15)
                output(1)
            dve.wait_ge(S["ya_high"], 1)
            rest(yL, uT, yH).then_inc(S["ya_split"], 1)
            read_out(dve, "aglu")
            dve.tensor_tensor(uT, uT, svt, ALU.mult).then_inc(S["ya_ready"], 1)
            dve.wait_ge(S["ya_ready"], 1)
            dve.wait_ge(S["ya_high"], 2)
            rest(yL, uT, yH).then_inc(S["ya_split"], 1)

            read_out(dve, "azv0")
            read_out(dve, "azv1")
            for b in range(NB):
                for g in range(2):
                    link(dve.bn_stats(stat[:, (2 * b + g) * 6:(2 * b + g) * 6 + 6], zv[:, b, 512 * g:512 * g + 512]))
            for b in range(NB):
                ins = dve.bn_aggr(stat[:, 48 + 2 * b:50 + 2 * b], stat[:, 12 * b:12 * b + 12])
            ins.then_inc(S["zv_stats"], 1)
            dve.wait_ge(S["zv_std"], 1)
            link(dve.reciprocal(stat[:, 56:60], stat[:, 56:60]))
            for b in range(NB):
                link(dve.tensor_scalar(zv[:, b, :], zv[:, b, :], stat[:, 48 + 2 * b:49 + 2 * b], stat[:, 56 + b:57 + b],
                                       ALU.subtract, ALU.mult))
            dve.wait_ge(S["sgu_loaded"], 64)
            link(dve.tensor_tensor(zv, zv, lng.unsqueeze(1).to_broadcast([P, NB, D]), ALU.mult))
            dve.tensor_tensor(zv, zv, lnb.unsqueeze(1).to_broadcast([P, NB, D]), ALU.add).then_inc(S["zv_normed"], 1)
            dve.wait_ge(S["mem_high"], 1)
            rest(mL, mT, mH).then_inc(S["mem_split"], 1)
            read_out(dve, "azu0")
            read_out(dve, "azu1")
            for g in range(2):
                dve.wait_ge(S["sv_done"], g + 1)
                half = jobs.half[f"asv{g}"]
                for h in range(4):
                    ins = dve.tensor_tensor(svt[:, h, :].rearrange("p (b t) -> p b t", t=P),
                                            ps[half][:, h * T:h * T + T].rearrange("p (b t) -> p b t", t=P),
                                            sgub[:, 4 * g + h, :].unsqueeze(1).to_broadcast([P, NB, P]), ALU.add)
                ins.then_inc(drained[half], 1)
                read_out(dve, f"asv{g}")
                dve.tensor_tensor(zu[:, 4 * g:4 * g + 4, :], zu[:, 4 * g:4 * g + 4, :], svt, ALU.mult).then_inc(S["yb_ready"], 1)
                dve.wait_ge(S["yb_ready"], g + 1)
            for g in range(2):
                half = slice(4 * g, 4 * g + 4)
                dve.tensor_copy(zuH[:, half, :], zu[:, half, :]).then_inc(S["yb_high"], 1)
                dve.wait_ge(S["yb_high"], g + 1)
                rest(zuL[:, half, :], zu[:, half, :], zuH[:, half, :]).then_inc(S["yb_split"], 1)

            dve.wait_ge(S["yb_split"], 2)
            with dve.Fori(0, 2) as c:
                read_out(dve, "aga", 0, c)
                done(dve, "apa", 0, c)
                h = jobs.half["apa"]
                dve.tensor_tensor(merged_a[:, ds(c * 4, 4), :], banks(h), gate_a[0], ALU.mult).then_inc(drained[h], 1)
                read_out(dve, "agb", 0, c)
                done(dve, "apb", 0, c)
                h = jobs.half["apb"]
                dve.tensor_tensor(gate_a[1], banks(h), gate_a[1], ALU.mult).then_inc(S["gated_a"], 1)
                dve.wait_ge(S["gated_a"], c + 1)
                dve.tensor_tensor(merged_a[:, ds(c * 4, 4), :], merged_a[:, ds(c * 4, 4), :], gate_a[1], ALU.add)\
                   .then_inc(S["merged_a"], 1)
                dve.wait_ge(S["merged_a"], c + 1)
                dve.sem_inc(drained[h], 1)
            dve.wait_ge(S["merged_a_high"], 2)
            rest(merged_aL[:, 4:8, :], merged_a[:, 4:8, :], merged_aH[1]).then_inc(S["merged_a_split1"], 1)
            add_back("awo", "ass_xa")
            split_norm("ass_xa", vec0[:, V_XA:V_XA + KD])

            def x_max(h):
                half, p = jobs.half[f"axs{h}"], h % 2
                dve.wait_ge(S["x_scores"], h + 1)
                mx = stat[:, 64 + 4 * p:68 + 4 * p]
                link(dve.tensor_reduce(mx, ps[half][:, 0:NB * M].rearrange("p (b m) -> p b m", m=M), AXX, ALU.max))
                dve.tensor_scalar(mx, mx, -float((D // 4) ** -0.5), None, ALU.mult).then_inc(S["x_max"], 1)

            def x_norm(h):
                p = h % 2
                read_out(dve, f"axs{h}")
                link(dve.reciprocal(stat[:, 80 + 4 * p:84 + 4 * p], stat[:, 72 + 4 * p:76 + 4 * p]))
                dve.tensor_tensor(xp[:, p, :, :], xp[:, p, :, :], wide(stat[:, 80 + 4 * p:84 + 4 * p], M), ALU.mult)\
                   .then_inc(S["x_probs"], 1)

            x_max(0)
            x_max(1)

            def x_rest(h):
                dve.wait_ge(S["xo_high"], h + 1)
                half, two = jobs.half[f"axv{h}"], slice(2 * h, 2 * h + 2)
                rest(xoL[:, two, :], banks(half, n=2), xoH[:, two, :]).then_inc(drained[half], 1)

            x_norm(0)
            x_max(2)
            x_norm(1)
            x_rest(0)
            x_max(3)
            x_norm(2)
            x_rest(1)
            x_norm(3)
            x_rest(2)
            x_rest(3)
            add_back("axo", "ass_ff")
            split_norm("ass_ff", vec0[:, V_FF:V_FF + KD])

            def ff_rest(raw, g, n):
                dve.wait_ge(S["ff_high"], n + 1)
                rest(ffL[:, ds(g * 2, 2), :], raw, ffH[:, ds(g * 2, 2), :]).then_inc(S["ff_split"], 1)

            def gate_up(name, g, p, i=0):
                dve.wait_ge(S["silu_a"], g + 1)
                h = jobs.half[name]
                dve.tensor_tensor(ff_raw[:, p, :, :], sg_a[:, p, :, :], banks(h)[:, 2:4, :], ALU.mult).then_inc(drained[h], 1)
                ff_rest(ff_raw[:, p, :, :], g, g)

            with dve.Fori(0, 5) as i:
                gate_up("aupa", i * 2, 0, i)
                gate_up("aupb", i * 2 + 1, 1, i)
            gate_up("aupc", NG - 1, 0)
            add_back("adn", "ass_fin")
            norm("ass_fin", hT[:, :, :], vec0[:, V_FIN:V_FIN + KD], new_state=True)
            dve.wait_ge(S["residual"], state_parts("bss_at") + 5)
            half_sum("bss_at")

            dve.wait_ge(S["tables_loaded"], 16)
            with dve.Fori(0, LAYERS) as l:
                read_out(dve, "bvecs", l)
                split_norm("bss_at", vec[:, W_AT:W_AT + KD], l)

                def rope(name, buf, n):
                    read_out(dve, name, l)
                    turned = Chain(dve, S["rope_step"], l * 10 + n * 2)
                    cos, sin = (C[x].unsqueeze(1).to_broadcast([P, NB, T]) for x in ("cos", "sin"))
                    turned(dve.tensor_tensor(buf, buf, cos, ALU.mult))
                    turned(dve.tensor_tensor(part, part, sin, ALU.mult))
                    dve.tensor_tensor(buf, buf, part, ALU.add).then_inc(S["roped"], 1)
                    dve.wait_ge(S["roped"], PRIMED + l * 5 + n + 1)

                done(dve, "bmix1", l)
                dve.wait_ge(S["roped"], PRIMED + l * 5)
                h = jobs.half["bmix1"]
                dve.tensor_copy(mix1[:, 2:4, :], banks(h)[:, 2:4, :])
                for r in range(0, P, 32):
                    ins = dve.tensor_copy(part[r:r + 32, 2:4, :], banks(h)[r ^ 32:(r ^ 32) + 32, 2:4, :])
                ins.then_inc(S["mix1_swapped"], 1)
                dve.wait_ge(S["mix1_swapped"], l + 1)
                dve.wait_ge(S["mix1_copied"], l + 1)
                dve.sem_inc(drained[h], 1)
                rope("bmix1", mix1, 0)
                read_out(dve, "bmix2", l)
                wi = stat[:, 96:112].rearrange("p (b h) -> p b h", h=4)
                dve.tensor_scalar(wi, mix2[:, :, MW:MW + 4], float(4 ** -0.5 * 64 ** -0.5), None, ALU.mult)\
                   .then_inc(S["index_weights"], 1)
                dve.wait_ge(S["index_weights"], l + 1)
                steps = Chain(dve, S["index_step"], l * 12)
                for b in range(1, NB):
                    n = (b + 1) * P
                    read_out(dve, f"bix{b}", l)
                    steps(dve.tensor_scalar(score[b], relu[:, 0, 0:n], wi[:, b, 0:1], None, ALU.mult))
                    for h in range(1, 4):
                        steps(dve.scalar_tensor_tensor(out=score[b], in0=relu[:, h, 0:n], scalar=wi[:, b, h:h + 1],
                                                       in1=score[b], op0=ALU.mult, op1=ALU.add))
                    dve.tensor_tensor(score[b], score[b], C["cmask"][:, T - n:T], ALU.add).then_inc(S["index_scored"], 1)
                assert steps.n == 12
                dve.wait_ge(S["index_scored"], PRIMED + l * 3 + 3)
                plain(dve)
                with dve.Fori(0, TOPK // 8) as r:
                    taken = Chain(dve, S["topk_step"], l * (6 * TOPK // 8) + r * 6)
                    best = [None] + [stat[:, 112 + 8 * (b - 1):120 + 8 * (b - 1)] for b in range(1, NB)]
                    for b in range(1, NB):
                        plain(dve)
                        taken(dve.max(best[b], score[b]))
                    for b in range(1, NB):
                        plain(dve)
                        taken(dve.match_replace(score[b], best[b], score[b], GONE))
                dve.tensor_copy(selb[:, 0:P], C["cmask"][:, T - P:T])
                for b in range(1, NB):
                    at = causal[b][4]
                    ins = dve.tensor_scalar(selb[:, at:at + (b + 1) * P], score[b], GONE, NEG, ALU.not_equal, ALU.mult)
                ins.then_inc(S["selected"], 1)
                dve.wait_ge(S["selected"], l + 1)

                dve.wait_ge(S["forget_log"], l + 1)
                dve.tensor_copy(onehot[0:H, :, :], ident[0:H, 0:H].unsqueeze(2).to_broadcast([H, H, P]))
                steps = Chain(dve, S["forget_sum_step"], l * 2)
                steps(dve.tensor_scalar(fx[0:H, :], fx[0:H, :], 0.0, None, ALU.min))
                steps(dve.tensor_tensor(fx[0:H, :], fx[0:H, :], fe[0:H, :], ALU.subtract))
                dve.tensor_tensor_scan(fF[0:H, :], ones[0:H, 0:1].to_broadcast([H, T]), fx[0:H, :], 0.0, ALU.mult, ALU.add)\
                   .then_inc(S["forget_sum"], 1)
                dve.wait_ge(S["forget_sum"], l + 1)
                dve.tensor_copy(fFH[0:H, :], fF[0:H, :]).then_inc(S["forget_high"], 1)
                dve.wait_ge(S["forget_high"], l + 1)
                rest(fFL[0:H, :], fF[0:H, :], fFH[0:H, :]).then_inc(S["forget_split"], 1)
                rope("bqB", qB, 1)

                def attend(br, blocks, bias, sinks=False, mixed=otm):
                    scored, turned_half = (ps[jobs.half[name]] for name in AFTER[br])

                    def scores(i, p, first=False):
                        h = i * 2 + p
                        mx = stat[:, 64 + 4 * p:68 + 4 * p]
                        biases = {b: bias(b, k0, n, to, h) for b, k0, n, _, to in blocks}
                        if br == "fox":
                            if not first:
                                dve.wait_ge(S["heads_turned"], nth_soft(br, l) + h - 1)
                            for b, k0, n, at, to in blocks:
                                ins = dve.scalar_tensor_tensor(out=logit[:, p, to:to + n], in0=biases[b], scalar=ftm[:, b, ds(h, 1)],
                                                               in1=fb[:, ds(h, 1), k0:k0 + n].rearrange("p a b -> p (a b)"),
                                                               op0=ALU.add, op1=ALU.subtract)
                                biases[b] = logit[:, p, to:to + n]
                            ins.then_inc(S["fox_biased"], 1)
                            dve.wait_ge(S["fox_biased"], l * H + h + 1)
                        dve.wait_ge(S["heads_scores"], nth_head(br, l) + h + 1)
                        plain(dve)
                        for b, k0, n, at, to in blocks:
                            ins = dve.tensor_tensor_reduce(logit[:, p, to:to + n], scored[:, at:at + n], biases[b], 1.0, -3e38,
                                                           ALU.add, ALU.max, mx[:, b:b + 1])
                        ins.then_inc(S["heads_max"], 1)
                        dve.wait_ge(S["heads_max"], nth_soft(br, l) + h + 1)
                        if sinks:
                            dve.tensor_scalar(mx, mx, sink[:, ds(h, 1)], None, ALU.max).then_inc(S["sink_max"], 1)
                            dve.wait_ge(S["sink_max"], l * H + h + 1)
                        dve.tensor_scalar(mx, mx, -1.0, None, ALU.mult).then_inc(S["heads_scores_read"], 1)

                    def head(i, p, last):
                        h = i * 2 + p
                        if not last:
                            scores(i + 1, p)
                        dve.wait_ge(S["heads_out"], nth_head(br, l) + h + 1)
                        total = stat[:, 72 + 4 * p:76 + 4 * p]
                        if sinks:
                            dve.tensor_tensor(total, total, stat[:, 88 + 4 * p:92 + 4 * p], ALU.add).then_inc(S["sink_sum"], 1)
                            dve.wait_ge(S["sink_sum"], l * H + h + 1)
                        dve.reciprocal(stat[:, 80 + 4 * p:84 + 4 * p], total).then_inc(S["heads_inverse"], 1)
                        dve.wait_ge(S["heads_inverse"], PRIMED + nth_soft(br, l) + h + 1)
                        dve.tensor_tensor(mixed[:, :, ds(i * P + p * HD, HD)],
                                          turned_half[:, 3 * T:3 * T + NB * HD].rearrange("p (b d) -> p b d", d=HD),
                                          wide(stat[:, 80 + 4 * p:84 + 4 * p], HD), ALU.mult).then_inc(S["heads_out_read"], 1)

                    scores(0, 0, True)
                    scores(0, 1, True)
                    with dve.Fori(0, 3) as i:
                        head(i, 0, False)
                        head(i, 1, False)
                    head(3, 0, True)
                    head(3, 1, True)

                def y_rest(name, k, part, high):
                    dve.wait_ge(S["y_high"], l * 4 + k)
                    h = jobs.half[name]
                    rest(part, banks(h), high).then_inc(drained[h], 1)

                read_out(dve, "bft", l)
                read_out(dve, "bfb0", l)
                read_out(dve, "bfb1", l)
                attend("fox", causal, lambda b, k0, n, to, h: C["cmask"][:, T - n:T])
                attend("dsa", causal, lambda b, k0, n, to, h: selb[:, to:to + n],
                       mixed=otm2)
                y_rest("btA", 1, yAL, yAH)
                y_rest("btB", 2, yBL, yBH)
                rope("bqC", Q, 2)
                rope("bkC", K, 3)

                def ret_decayed(i, p):
                    h = i * 2 + p
                    dve.wait_ge(S["ret_decay"], l * H + h + 1)
                    dve.wait_ge(S["heads_scores"], nth_head("ret", l) + h + 1)
                    for j, n, at, to in forward:
                        ins = dve.tensor_tensor(logit[:, p, to:to + n], ps[0][:, at:at + n], decay[:, p, 0:n], ALU.mult)
                    ins.then_inc(S["heads_scores_read"], 1)

                plain(dve)
                with dve.Fori(0, 4) as i:
                    ret_decayed(i, 0)
                    ret_decayed(i, 1)
                dve.wait_ge(S["heads_out_read"], PRIMED + nth_head("ret", l) + H)
                grouped = otm.rearrange("p b (h d) -> p (b h) d", d=HD)
                mean, var = stat[:, 0:32], stat[:, 32:64]
                steps = Chain(dve, S["group_step"], l * 3)
                steps(dve.tensor_reduce(mean, grouped, AXX, ALU.add))
                steps(dve.tensor_scalar(mean, mean, 1.0 / HD, None, ALU.mult))
                dve.tensor_tensor(grouped, grouped, wide(mean, HD), ALU.subtract).then_inc(S["group_centred"], 1)
                dve.wait_ge(S["group_squared"], l + 1)
                dve.tensor_reduce(var, gsq.rearrange("p b (h d) -> p (b h) d", d=HD), AXX, ALU.add).then_inc(S["group_var"], 1)
                dve.wait_ge(S["group_std"], l + 1)
                steps(dve.reciprocal(mean, mean))
                dve.tensor_tensor(grouped, grouped, wide(mean, HD), ALU.mult).then_inc(S["group_normed"], 1)
                rope("bqD", qD, 4)
                read_out(dve, "bgC", l)
                attend("swa", window, lambda b, k0, n, to, h: C["band"][:, 2 * P - n:2 * P], sinks=True, mixed=otm2)
                dve.wait_ge(S["y_turned"], l * 4 + 3)
                h = jobs.half["btC"]
                for c in range(NB):
                    ins = dve.scalar_tensor_tensor(out=gC[:, c, :], in0=ps[h][:, c * T:c * T + T], scalar=vec[:, W_RET + c:W_RET + c + 1],
                                                   in1=gC[:, c, :], op0=ALU.mult, op1=ALU.mult)
                ins.then_inc(drained[h], 1)
                dve.wait_ge(S["y_high"], l * 4 + 3)
                rest(yCL, gC, yCH).then_inc(S["yc_split"], 1)
                y_rest("btD", 4, yDL, yDH)

                with dve.Fori(0, 2) as c:
                    for n in range(4):
                        read_out(dve, f"bgt{n}", l, c)
                        done(dve, f"bbr{n}", l, c)
                        h = jobs.half[f"bbr{n}"]
                        sums = merged_b[:, ds(c * 4, 4), :]
                        gate = gate_b[n % 2]
                        dve.tensor_tensor(gate if n else sums, banks(h), gate, ALU.mult).then_inc(S["gated_b"], 1)
                        dve.wait_ge(S["gated_b"], l * 8 + c * 4 + n + 1)
                        if n:
                            dve.tensor_tensor(sums, sums, gate, ALU.add).then_inc(S["merged_b"], 1)
                            dve.wait_ge(S["merged_b"], PRIMED + l * 6 + c * 3 + n)
                        dve.sem_inc(drained[h], 1)
                dve.wait_ge(S["merged_b_high"], l * 2 + 2)
                rest(merged_bL[:, 4:8, :], merged_b[:, 4:8, :], merged_bH[1]).then_inc(S["merged_b_split1"], 1)
                add_back("bwo", "bss_ff", l, l)
                split_norm("bss_ff", vec[:, W_FF:W_FF + KD], l)

                def conv_group(name, g, p, i=0):
                    dve.wait_ge(S["conv_begun"], l * NG + g + 1)
                    h = jobs.half[name]
                    for shift, at in ((1, W_C1), (2, W_C0)):
                        for j in range(4):
                            ch = g * 2 + (j if j < 2 else NF + j - 2)
                            ins = dve.scalar_tensor_tensor(out=conv[:, p, j, shift:T], in0=ps[h][:, j * T:j * T + T - shift],
                                                           scalar=vec[:, ds(ch + at, 1)], in1=conv[:, p, j, shift:T],
                                                           op0=ALU.mult, op1=ALU.add)
                        if shift == 1:
                            ins.then_inc(S["conv_step"], 1)
                            dve.wait_ge(S["conv_step"], l * NG + g + 1)
                    ins.then_inc(drained[h], 1)
                    dve.wait_ge(S["silu_b"], l * NG + g + 1)
                    dve.tensor_tensor(conv[:, p, 0:2, :], conv[:, p, 0:2, :], conv[:, p, 2:4, :], ALU.mult).then_inc(S["ff_ready"], 1)
                    ff_rest(conv[:, p, 0:2, :], g, NG + l * NG + g)

                with dve.Fori(0, 5) as i:
                    conv_group("bupa", i * 2, 0, i)
                    conv_group("bupb", i * 2 + 1, 1, i)
                conv_group("bupc", NG - 1, 0)
                add_back("bdn", "bss_at", l, l + 1)
            norm("css_fin", hT[:, :, :], vec0[:, V_FIN2:V_FIN2 + KD])

        @block.gpsimd
        def _(pool):
            def rests(name, l=0, i=0, cols=512):
                for u in range(ring.units[name]):
                    s, p = ring.slot[(name, u)], ring.split[(name, u)]
                    pool.wait_ge(weights_high, ring.at(ring.before, name, u, l, i) + 1)
                    pool.tensor_tensor(wL[:, p, 0:cols], slot[:, s, 0:cols], plainly(wH[:, p, 0:cols]), ALU.subtract)\
                        .then_inc(weights_split, 1)

            pool.sem_inc(S["s5_back_pool"], PRIMED)
            pool.dma_start(bnat[0], I["s5_b_re"].rearrange("(t q) c -> q t c", q=P)).then_inc(S["s5b_loaded"], 16)
            pool.dma_start(bnat[1], I["s5_b_im"].rearrange("(t q) c -> q t c", q=P)).then_inc(S["s5b_loaded"], 16)
            pool.wait_ge(S["x_turned"], 2)
            for buf in zb + cnat:
                pool.memset(buf, 0.0).then_inc(S["zeros_set"], 1)
            pool.wait_ge(S["zeros_set"], 4)
            for n, key in enumerate(("s5_c_re", "s5_c_im")):
                rows = I[key].rearrange("(q r) s -> r q s", r=P)
                for j in range(4):
                    for g in range(2):
                        at = 32 * j + CHAN * g
                        pool.dma_start(cnat[n][at:at + CHAN, :, STATE * g:STATE * g + STATE], rows[at:at + CHAN, :, :])\
                            .then_inc(S["s5c_loaded"], 16)
            rests("axa")
            pool.wait_ge(S["normed_split"], KD)
            pool.dma_start(rms[:, :], I["consts"][:, N_CONSTS:N_CONSTS + T]).then_inc(S["iota_loaded"], 16)
            rests("aglu")
            with pool.Fori(0, 2) as c:
                def turned(t):
                    p = t % 2
                    pool.wait_ge(S["s5_rotated"], c * 16 + t + 1)
                    pool.tensor_tensor(zt[:, p, 0, :], prod[:, t % 3, 0, :], prod[:, t % 3, 1, :], ALU.add)
                    pool.tensor_tensor(zt[:, p, 1, :], prod[:, t % 3, 2, :], prod[:, t % 3, 3, :], ALU.subtract).then_inc(S["s5_z"], 1)

                def back(t):
                    p = t % 2
                    pool.wait_ge(S["s5_scanned"], c * 32 + 2 * t + 2)
                    for n in range(2):
                        ins = pool.tensor_tensor(prod[:, t % 3, 2 + n, :], st[:, p, n, :], trig[:, t % 3, 1 - n, :], ALU.mult)
                    ins.then_inc(S["s5_back_pool"], 1)

                for t in range(16):
                    turned(t)
                    if t:
                        back(t - 1)
                back(15)
            pool.wait_ge(S["s5_y_read"], PRIMED + 4)
            pool.memset(qz[:, :, :], 0.0).then_inc(S["zeros_set"], 1)
            pool.dma_start(wsn, I["sgu_w"].rearrange("h t s -> t h s")).then_inc(S["sgu_loaded"], 16)
            pool.dma_start(sgub, I["sgu_bias"].unsqueeze(0).to_broadcast([P, H, P])).then_inc(S["sgu_loaded"], 16)
            pool.dma_start(lng, I["sgu_ln_g"].unsqueeze(0).to_broadcast([P, D])).then_inc(S["sgu_loaded"], 16)
            pool.dma_start(lnb, I["sgu_ln_b"].unsqueeze(0).to_broadcast([P, D])).then_inc(S["sgu_loaded"], 16)
            for name in ("azv0", "azv1", "azu0", "azu1"):
                rests(name)
            with pool.Fori(0, 2) as c:
                for name in ("aga", "apa", "agb", "apb"):
                    rests(name, 0, c)
            pool.wait_ge(S["merged_a_high"], 1)
            pool.tensor_tensor(merged_aL[:, 0:4, :], merged_a[:, 0:4, :], plainly(merged_aH[0]), ALU.subtract)\
                .then_inc(S["merged_a_split0"], 1)
            for name in ("wo", "wk", "wv", "wq", "xo"):
                for g in range(2):
                    rests(f"a{name}{g}")
            with pool.Fori(0, 5) as i:
                rests("aupa", 0, i)
                rests("aupb", 0, i)
            for name in ("aupc", "adn0", "adn1"):
                rests(name)
            with pool.Fori(0, LAYERS) as l:
                rests("bmix1", l)
                rests("bmix2", l, cols=MIX2)
                for name in ("qB", "qA", "kA", "vA", "qC", "kC", "vC", "qD", "gC"):
                    rests("b" + name, l)
                with pool.Fori(0, 2) as c:
                    for n in range(4):
                        rests(f"bgt{n}", l, c)
                        rests(f"bbr{n}", l, c)
                pool.wait_ge(S["merged_b_high"], l * 2 + 1)
                pool.tensor_tensor(merged_bL[:, 0:4, :], merged_b[:, 0:4, :], plainly(merged_bH[0]), ALU.subtract)\
                    .then_inc(S["merged_b_split0"], 1)
                rests("bwo0", l)
                rests("bwo1", l)
                with pool.Fori(0, 5) as i:
                    rests("bupa", l, i)
                    rests("bupb", l, i)
                for name in ("bupc", "bdn0", "bdn1"):
                    rests(name, l)


_SHAPES = {
    "x": (512, 1024), "mem": (256, 1024), "mix_norm_g": (1024,), "w_in": (1024, 4608), "s5_lam_re": (32, 128),
    "s5_lam_im": (32, 128), "s5_log_step": (32, 2), "s5_b_re": (4096, 16), "s5_b_im": (4096, 16),
    "s5_c_re": (1024, 64), "s5_c_im": (1024, 64), "s5_d": (512,), "s5_w_glu": (512, 512), "sgu_ln_g": (1024,),
    "sgu_ln_b": (1024,), "sgu_w": (8, 128, 128), "sgu_bias": (8, 128), "w_proj_a": (512, 1024),
    "w_proj_b": (1024, 1024), "w_out": (1024, 1024), "xattn_norm_g": (1024,), "mem_norm_g": (1024,),
    "w_q": (1024, 1024), "w_k": (1024, 1024), "w_v": (1024, 1024), "w_xo": (1024, 1024), "ffn_norm_g": (1024,),
    "w_gate": (1024, 2816), "w_up": (1024, 2816), "w_down": (2816, 1024), "final_norm_g": (1024,),
    "attn_norm_2": (2, 1024), "w_in_2": (2048, 9420), "forget_bias_2": (2, 8), "ret_norm_2": (2, 512),
    "attn_sinks_2": (2, 8), "w_branch_2": (4096, 1024), "w_out_2": (2048, 1024), "ffn_norm_2": (2, 1024),
    "w_up_2": (2048, 5632), "conv_w_2": (6, 5632), "conv_b_2": (2, 5632), "w_down_2": (5632, 1024),
    "final_norm_2": (1024,),
}


def kernel(**inputs):
    import numpy as _np
    import concourse.bacc as _bacc
    from concourse import mybir as _mybir
    from concourse.bass_utils import run_bass_kernel_spmd as _run

    nc = _bacc.Bacc("TRN2", target_bir_lowering=False, num_devices=1)
    arrays = {name: _np.ascontiguousarray(inputs[name]).reshape(shape) for name, shape in _SHAPES.items()}
    arrays["consts"] = constants()
    handles = {name: nc.dram_tensor(f"in_{name}", a.shape, _mybir.dt.from_np(a.dtype), kind="ExternalInput").ap()
               for name, a in arrays.items()}
    out = nc.dram_tensor("out", (512, 1024), _mybir.dt.float32, kind="ExternalOutput").ap()
    two_blocks(nc, handles, out)
    r = _run(nc, [{f"in_{name}": a for name, a in arrays.items()}], core_ids=[0])
    return r.results[0]["out"].reshape(1, 512, 1024)
```
